# Optimizing a Trainium2 kernel written in Bass

```python
import math
import jax, jax.numpy as jnp
from jax import lax
import numpy as np
import jax
import jax.numpy as jnp

D_MODEL = 1024
BATCH = 1
SEQ = 512
DEPTH = 2

GRID_W = 64
CTX_LEN = 256

MLA_HEADS = 8
QK_NOPE = 64
QK_ROPE = 32
V_HEAD = 64
Q_LORA = 384
KV_LORA = 256
AXIS_ROPE = QK_ROPE // 2
ROPE_BASE = 10000.0
Q_BLOCK = 128

FNET_GROUPS = 4
FNET_GROUP_W = 64
FNET_W = FNET_GROUPS * FNET_GROUP_W

HYENA_W = 256
HYENA_CONV = 3
FILTER_EMB = 33
FILTER_ORDER = 64
DECAY_TARGET = 1e-2
FAST_DECAY_PCT = 0.3
SLOW_DECAY_PCT = 1.5

MLA_W = MLA_HEADS * V_HEAD
MIX_W = MLA_W + FNET_W + HYENA_W
OFF_Q = 0
OFF_KV = OFF_Q + Q_LORA
OFF_KR = OFF_KV + KV_LORA
OFF_F = OFF_KR + QK_ROPE
OFF_H = OFF_F + FNET_W
IN_W = OFF_H + 3 * HYENA_W
D_FF = 4 * D_MODEL
N_MOD = 6
EPS = 1e-6


def rms_norm(x, g):
    xf = x.astype(jnp.float32)
    y = xf * lax.rsqrt(jnp.mean(xf * xf, axis=-1, keepdims=True) + EPS)
    return (y * g.astype(jnp.float32)).astype(x.dtype)

def modulation(cvec, w_mod, b_mod):
    m = (jax.nn.silu(cvec) @ w_mod + b_mod).reshape(-1, 1, N_MOD * D_MODEL)
    return jnp.split(m, N_MOD, axis=-1)

def modulate(h, shift, scale):
    return h * (1.0 + scale) + shift

def grid_rope_tables(n_tokens, dtype):
    rows = n_tokens // GRID_W
    row = jnp.repeat(jnp.arange(rows, dtype=jnp.float32), GRID_W)
    col = jnp.tile(jnp.arange(GRID_W, dtype=jnp.float32), rows)
    inv = ROPE_BASE ** (-jnp.arange(0, AXIS_ROPE, 2, dtype=jnp.float32) / AXIS_ROPE)
    ang = jnp.concatenate([row[:, None] * inv, col[:, None] * inv], axis=-1)
    return jnp.cos(ang).astype(dtype), jnp.sin(ang).astype(dtype)

def _rotate_half(v, cos, sin):
    half = v.shape[-1] // 2
    v1, v2 = v[..., :half], v[..., half:]
    return jnp.concatenate([v1 * cos - v2 * sin, v1 * sin + v2 * cos], axis=-1)

def apply_axial_rope(x, cos, sin):
    n = AXIS_ROPE // 2
    return jnp.concatenate([
        _rotate_half(x[..., :AXIS_ROPE], cos[..., :n], sin[..., :n]),
        _rotate_half(x[..., AXIS_ROPE:], cos[..., n:], sin[..., n:])], axis=-1)

def mla_queries(p, q_norm_g, w_uq, rope):
    B, L, _ = p.shape
    cq = rms_norm(p[..., OFF_Q:OFF_KV], q_norm_g)
    q = (cq @ w_uq).reshape(B, L, MLA_HEADS, QK_NOPE + QK_ROPE)
    q_nope, q_rope = q[..., :QK_NOPE], q[..., QK_NOPE:]
    if rope is not None:
        cos, sin = rope
        q_rope = apply_axial_rope(q_rope, cos[:, None, :], sin[:, None, :])
    return q_nope, q_rope

def mla_keys_values(p_kv, kv_norm_g, w_ukv, rope):
    B, L, _ = p_kv.shape
    ckv = rms_norm(p_kv[..., :KV_LORA], kv_norm_g)
    kv = (ckv @ w_ukv).reshape(B, L, MLA_HEADS, QK_NOPE + V_HEAD)
    k_rope = p_kv[..., KV_LORA:]
    if rope is not None:
        k_rope = apply_axial_rope(k_rope, *rope)
    return kv[..., :QK_NOPE], k_rope, kv[..., QK_NOPE:]

def mla_attention(q_nope, q_rope, k_nope, k_rope, v):
    B, L, H, _ = q_nope.shape
    nb = L // Q_BLOCK
    scale = 1.0 / math.sqrt(QK_NOPE + QK_ROPE)

    def to_blocks(t):
        return jnp.moveaxis(t.reshape(B, nb, Q_BLOCK, *t.shape[2:]), 1, 0)

    def block(qs):
        qn, qr = qs
        s = (jnp.einsum('bqhd,bkhd->bhqk', qn, k_nope)
             + jnp.einsum('bqhr,bkr->bhqk', qr, k_rope))
        prob = jax.nn.softmax(s.astype(jnp.float32) * scale, axis=-1).astype(v.dtype)
        return jnp.einsum('bhqk,bkhd->bqhd', prob, v)

    o = lax.map(block, (to_blocks(q_nope), to_blocks(q_rope)))
    return jnp.moveaxis(o, 0, 1).reshape(B, L, H * V_HEAD)

def fourier_mix(u):
    B, L, _ = u.shape
    g = u.reshape(B, L, FNET_GROUPS, FNET_GROUP_W).astype(jnp.float32)
    f = jnp.fft.fftn(g, axes=(1, 3), norm="ortho").real
    return f.reshape(B, L, FNET_W).astype(u.dtype)

def short_conv(u, w, b):
    L = u.shape[1]
    pad = (HYENA_CONV - 1) // 2
    up = jnp.pad(u, ((0, 0), (pad, HYENA_CONV - 1 - pad), (0, 0)))
    out = b
    for k in range(HYENA_CONV):
        out = out + up[:, k:k + L] * w[k]
    return out

def hyena_filters(L, w1, b1, freq, w2, b2, w3):
    f32 = jnp.float32
    t = jnp.linspace(0.0, 1.0, L, dtype=f32)[:, None]
    bands = (FILTER_EMB - 1) // 2
    fr = jnp.linspace(1e-4, bands - 1, bands, dtype=f32)
    ang = 2.0 * math.pi * jnp.arange(L, dtype=f32)[:, None] / L * fr
    z = jnp.concatenate([t, jnp.cos(ang), -jnp.sin(ang)], axis=-1)
    h = jnp.sin(freq * (z.astype(w1.dtype) @ w1 + b1))
    h = jnp.sin(freq * (h @ w2 + b2))
    h = (h @ w3).astype(f32)
    min_decay = math.log(DECAY_TARGET) / SLOW_DECAY_PCT
    max_decay = math.log(DECAY_TARGET) / FAST_DECAY_PCT
    deltas = jnp.abs(jnp.linspace(min_decay, max_decay, HYENA_W, dtype=f32))
    decay = jnp.exp(-t * deltas)
    h = h * jnp.tile(decay, (1, 2))
    h_fwd, h_bwd = h[:, :HYENA_W], h[:, HYENA_W:]
    k = jnp.concatenate([h_fwd, jnp.zeros((1, HYENA_W), f32), h_bwd[:0:-1]], axis=0)
    return k / jnp.sum(jnp.abs(k), axis=0, keepdims=True)

def hyena_mix(u, conv_w, conv_b, w1, b1, freq, w2, b2, w3, d_bias):
    B, L, _ = u.shape
    u = short_conv(u, conv_w, conv_b)
    x0, x1, v = jnp.split(u, 3, axis=-1)
    z = (x1 * v).astype(jnp.float32)
    k = hyena_filters(L, w1, b1, freq, w2, b2, w3)
    zf = jnp.fft.rfft(z, n=2 * L, axis=1)
    kf = jnp.fft.rfft(k, n=2 * L, axis=0)
    y = jnp.fft.irfft(zf * kf[None], n=2 * L, axis=1)[:, :L] + d_bias.astype(jnp.float32) * z
    return (x0.astype(jnp.float32) * y).astype(u.dtype)

def heads_out(att, p, hy, w_out):
    f = fourier_mix(p[..., OFF_F:OFF_H])
    hz = hyena_mix(p[..., OFF_H:], *hy)
    return jnp.concatenate([att, f, hz], axis=-1) @ w_out

def sq_relu_mlp(h, w1, w2):
    return jnp.square(jax.nn.relu(h @ w1)) @ w2

def first_inputs(seed: int = 0) -> dict:
    key = jax.random.key(seed)
    ks = jax.random.split(key, 26)

    def nrm(k, shape, scale):
        return jax.random.normal(k, shape, jnp.float32) * scale

    D = D_MODEL
    return {
        "x": nrm(ks[0], (BATCH, SEQ, D), 1.0),
        "c": nrm(ks[1], (BATCH, D), 1.0),
        "ctx": nrm(ks[2], (BATCH, CTX_LEN, D), 1.0),
        "c_ctx": nrm(ks[3], (D,), 1.0),
        "norm1_g": 1.0 + nrm(ks[4], (DEPTH, D), 0.05),
        "norm2_g": 1.0 + nrm(ks[5], (DEPTH, D), 0.05),
        "w_mod": nrm(ks[6], (DEPTH, D, N_MOD * D), 0.5 * D ** -0.5),
        "b_mod": nrm(ks[7], (DEPTH, N_MOD * D), 0.01),
        "w_in": nrm(ks[8], (DEPTH, D, IN_W), D ** -0.5),
        "q_norm_g": 1.0 + nrm(ks[9], (DEPTH, Q_LORA), 0.05),
        "kv_norm_g": 1.0 + nrm(ks[10], (DEPTH, KV_LORA), 0.05),
        "w_uq": nrm(ks[11], (DEPTH, Q_LORA, MLA_HEADS * (QK_NOPE + QK_ROPE)), Q_LORA ** -0.5),
        "w_ukv": nrm(ks[12], (DEPTH, KV_LORA, MLA_HEADS * (QK_NOPE + V_HEAD)), KV_LORA ** -0.5),
        "hy_conv_w": nrm(ks[13], (DEPTH, HYENA_CONV, 3 * HYENA_W), HYENA_CONV ** -0.5),
        "hy_conv_b": nrm(ks[14], (DEPTH, 3 * HYENA_W), 0.01),
        "hy_w1": nrm(ks[15], (DEPTH, FILTER_EMB, FILTER_ORDER), FILTER_EMB ** -0.5),
        "hy_b1": nrm(ks[16], (DEPTH, FILTER_ORDER), 0.1),
        "hy_freq": 1.0 + nrm(ks[17], (DEPTH, FILTER_ORDER), 0.05),
        "hy_w2": nrm(ks[18], (DEPTH, FILTER_ORDER, FILTER_ORDER), FILTER_ORDER ** -0.5),
        "hy_b2": nrm(ks[19], (DEPTH, FILTER_ORDER), 0.1),
        "hy_w3": nrm(ks[20], (DEPTH, FILTER_ORDER, 2 * HYENA_W), FILTER_ORDER ** -0.5),
        "hy_d": nrm(ks[21], (DEPTH, HYENA_W), 0.5),
        "w_out": nrm(ks[22], (DEPTH, MIX_W, D), MIX_W ** -0.5),
        "w_mlp1": nrm(ks[23], (DEPTH, D, D_FF), D ** -0.5),
        "w_mlp2": nrm(ks[24], (DEPTH, D_FF, D), D_FF ** -0.5),
        "final_norm_g": 1.0 + nrm(ks[25], (D,), 0.05),
    }

def first_block(x, c, ctx, c_ctx, norm1_g, norm2_g, w_mod, b_mod, w_in, q_norm_g, kv_norm_g,
              w_uq, w_ukv, hy_conv_w, hy_conv_b, hy_w1, hy_b1, hy_freq, hy_w2, hy_b2, hy_w3,
              hy_d, w_out, w_mlp1, w_mlp2, final_norm_g):
    L = x.shape[1]
    rope = grid_rope_tables(L, x.dtype)
    xc = ctx
    for l in range(DEPTH):
        last = l == DEPTH - 1
        hy = (hy_conv_w[l], hy_conv_b[l], hy_w1[l], hy_b1[l], hy_freq[l],
              hy_w2[l], hy_b2[l], hy_w3[l], hy_d[l])
        sh1, sc1, g1, sh2, sc2, g2 = modulation(c, w_mod[l], b_mod[l])
        csh1, csc1, cg1, csh2, csc2, cg2 = modulation(c_ctx, w_mod[l], b_mod[l])

        hx = modulate(rms_norm(x, norm1_g[l]), sh1, sc1)
        hc = modulate(rms_norm(xc, norm1_g[l]), csh1, csc1)
        px = hx @ w_in[l]
        if last:
            pc_kv = hc @ w_in[l][:, OFF_KV:OFF_F]
        else:
            pc = hc @ w_in[l]
            pc_kv = pc[..., OFF_KV:OFF_F]
        kn_c, kr_c, v_c = mla_keys_values(pc_kv, kv_norm_g[l], w_ukv[l], None)
        kn_x, kr_x, v_x = mla_keys_values(px[..., OFF_KV:OFF_F], kv_norm_g[l], w_ukv[l], rope)
        qn_x, qr_x = mla_queries(px, q_norm_g[l], w_uq[l], rope)
        att_x = mla_attention(qn_x, qr_x,
                              jnp.concatenate([kn_x, kn_c], axis=1),
                              jnp.concatenate([kr_x, kr_c], axis=1),
                              jnp.concatenate([v_x, v_c], axis=1))
        x = x + g1 * heads_out(att_x, px, hy, w_out[l])

        x = x + g2 * sq_relu_mlp(modulate(rms_norm(x, norm2_g[l]), sh2, sc2), w_mlp1[l], w_mlp2[l])

        if not last:
            qn_c, qr_c = mla_queries(pc, q_norm_g[l], w_uq[l], None)
            att_c = mla_attention(qn_c, qr_c, kn_c, kr_c, v_c)
            xc = xc + cg1 * heads_out(att_c, pc, hy, w_out[l])
            xc = xc + cg2 * sq_relu_mlp(modulate(rms_norm(xc, norm2_g[l]), csh2, csc2),
                                        w_mlp1[l], w_mlp2[l])
    return rms_norm(x, final_norm_g)


N_MIXERS = 2
N_A_LAYERS = (DEPTH + 1) // 2
N_B_LAYERS = DEPTH // 2

HG_EXPAND = 128
HG_HEADS = D_MODEL // HG_EXPAND
HG_KDIM = HG_EXPAND
HG_VDIM = D_MODEL // HG_HEADS
HG_CHUNK = 32

ATT_HEAD_DIM = 128
ATT_HEADS = D_MODEL // ATT_HEAD_DIM
DILATED_GROUPS = ((128, 1), (512, 4), (2048, 16))
N_GROUPS = len(DILATED_GROUPS)
ATT_QKV_COLS = N_GROUPS * 3 * ATT_HEADS * ATT_HEAD_DIM
ROPE_THETA = 500000.0
ROPE_DIM = ATT_HEAD_DIM // 4

D_FF_2 = -(-(8 * D_MODEL) // (3 * 256)) * 256

NORM_EPS = 1e-6


def rms_norm_2(x, g):
    xf = x.astype(jnp.float32)
    y = xf * lax.rsqrt(jnp.mean(xf * xf, axis=-1, keepdims=True) + NORM_EPS)
    return (y * g.astype(jnp.float32)).astype(x.dtype)

def apply_partial_rope(t, cos, sin):
    half = ROPE_DIM // 2
    t1 = t[..., :half]
    t2 = t[..., half:ROPE_DIM]
    return jnp.concatenate([t1 * cos - t2 * sin, t2 * cos + t1 * sin, t[..., ROPE_DIM:]], axis=-1)

def hgrn2_mixer(u, w_in, lb, norm_g, w_out):
    B, S, _ = u.shape
    H, K, C = HG_HEADS, HG_KDIM, HG_CHUNK
    proj = (u @ w_in).astype(jnp.float32).reshape(B, S, 4, H, K)
    q_raw, f_raw, v, g = proj[:, :, 0], proj[:, :, 1], proj[:, :, 2], proj[:, :, 3]
    lb = lb.astype(jnp.float32).reshape(H, K)
    log_f = jnp.log(lb + (1.0 - lb) * jax.nn.sigmoid(f_raw))
    k = (1.0 - lb) * jax.nn.sigmoid(-f_raw)
    q = jax.nn.silu(q_raw)
    NC = S // C
    rs = lambda t: t.reshape(B, NC, C, H, t.shape[-1])
    q, k, v, log_f = rs(q), rs(k), rs(v), rs(log_f)
    b = jnp.cumsum(log_f, axis=2)
    q_dec = q * jnp.exp(b)
    k_inv = k * jnp.exp(-b)
    causal = jnp.tril(jnp.ones((C, C), dtype=bool))
    a = jnp.einsum('bnchk,bnshk->bnhcs', q_dec, k_inv)
    a = jnp.where(causal, a, 0.0)
    o_intra = jnp.einsum('bnhcs,bnshv->bnchv', a, v)
    b_last = b[:, :, -1:]
    k_end = k * jnp.exp(b_last - b)
    chunk_decay = jnp.exp(b_last[:, :, 0])

    def step(state, xs):
        q_c, k_c, v_c, dec = xs
        o_c = jnp.einsum('bchk,bhkv->bchv', q_c, state)
        state = dec[..., None] * state + jnp.einsum('bchk,bchv->bhkv', k_c, v_c)
        return state, o_c

    xs = (jnp.moveaxis(q_dec, 1, 0), jnp.moveaxis(k_end, 1, 0),
          jnp.moveaxis(v, 1, 0), jnp.moveaxis(chunk_decay, 1, 0))
    state0 = jnp.zeros((B, H, K, HG_VDIM), jnp.float32)
    _, o_inter = lax.scan(step, state0, xs)
    o = (o_intra + jnp.moveaxis(o_inter, 0, 1)).reshape(B, S, H, HG_VDIM)
    o = o * lax.rsqrt(jnp.mean(o * o, axis=-1, keepdims=True) + NORM_EPS)
    o = o * norm_g.astype(jnp.float32).reshape(H, HG_VDIM)
    o = o.reshape(B, S, D_MODEL) * jax.nn.silu(g.reshape(B, S, D_MODEL))
    return o.astype(u.dtype) @ w_out

def dilated_group_attention(q, k, v, window, dilation):
    B, S, H, Dh = q.shape
    L = S // dilation
    n_win = window // dilation
    blk = n_win
    nb = -(-L // blk)
    Lp = nb * blk

    def gather(t):
        t = t.reshape(B, L, dilation, H, Dh).transpose(0, 2, 1, 3, 4).reshape(B * dilation, L, H, Dh)
        t = jnp.pad(t, ((0, 0), (0, Lp - L), (0, 0), (0, 0)))
        return t.reshape(B * dilation, nb, blk, H, Dh)

    def with_prev(t):
        prev = jnp.pad(t, ((0, 0), (1, 0), (0, 0), (0, 0), (0, 0)))[:, :-1]
        return jnp.concatenate([prev, t], axis=2)

    qb = gather(q)
    kw = with_prev(gather(k))
    vw = with_prev(gather(v))
    s = jnp.einsum('bnqhd,bnkhd->bnhqk', qb, kw)
    qi = jnp.arange(blk)[:, None]
    ki = jnp.arange(2 * blk)[None, :]
    dist = blk + qi - ki
    band = (dist >= 0) & (dist <= n_win)
    has_prev = (jnp.arange(nb)[:, None, None] > 0) | (ki >= blk)[None]
    valid = band[None] & has_prev
    s = jnp.where(valid[None, :, None], s, -jnp.inf)
    m = jnp.max(s, axis=-1, keepdims=True)
    p = jnp.exp(s - m)
    z = jnp.sum(p, axis=-1, keepdims=True)
    o = jnp.einsum('bnhqk,bnkhd->bnqhd', p, vw) / jnp.swapaxes(z, 2, 3)
    lse = jnp.swapaxes((m + jnp.log(z))[..., 0], 2, 3)

    def scatter_back(t):
        rest = t.shape[3:]
        t = t.reshape(B, dilation, Lp, *rest)[:, :, :L]
        return jnp.moveaxis(t, 1, 2).reshape(B, S, *rest)

    return scatter_back(o), scatter_back(lse)

def dilated_attention_mixer(u, cos, sin, w_in, w_out):
    B, S, _ = u.shape
    proj = (u @ w_in).astype(jnp.float32).reshape(B, S, N_GROUPS, 3, ATT_HEADS, ATT_HEAD_DIM)
    scale = ATT_HEAD_DIM ** -0.5
    outs = []
    lses = []
    for gi, (window, dilation) in enumerate(DILATED_GROUPS):
        q = apply_partial_rope(proj[:, :, gi, 0], cos, sin) * scale
        k = apply_partial_rope(proj[:, :, gi, 1], cos, sin)
        v = proj[:, :, gi, 2]
        o_g, lse_g = dilated_group_attention(q, k, v, window, dilation)
        outs.append(o_g)
        lses.append(lse_g)
    wts = jax.nn.softmax(jnp.stack(lses, axis=0), axis=0)
    o = jnp.einsum('gbsh,gbshd->bshd', wts, jnp.stack(outs, axis=0))
    return o.reshape(B, S, D_MODEL).astype(u.dtype) @ w_out

def swiglu_ffn(u, w_in, w_out):
    gate, up = jnp.split(u @ w_in, 2, axis=-1)
    return (jax.nn.silu(gate) * up) @ w_out

def second_inputs(seed: int = 0) -> dict:
    key = jax.random.key(seed)
    ks = jax.random.split(key, 16)
    D = D_MODEL
    nrm = jax.random.normal
    x = nrm(ks[0], (BATCH, SEQ, D), jnp.float32)
    c = nrm(ks[1], (BATCH, D), jnp.float32)
    offset = jax.random.randint(ks[2], (BATCH, 1), 0, 1024, dtype=jnp.int32)
    positions = offset + jnp.arange(SEQ, dtype=jnp.int32)[None, :]
    ada_w = nrm(ks[3], (DEPTH, D, 6 * D), jnp.float32) * (0.5 * D ** -0.5)
    ada_b = nrm(ks[4], (DEPTH, 6 * D), jnp.float32) * 0.02
    norm_g = 1.0 + 0.05 * nrm(ks[5], (DEPTH, 4, D), jnp.float32)
    hgrn_w_in = nrm(ks[6], (N_A_LAYERS, D, 4 * D), jnp.float32) * D ** -0.5
    hgrn_lower_bounds = 1.0 + 0.5 * nrm(ks[7], (N_A_LAYERS, D), jnp.float32)
    hgrn_norm_g = 1.0 + 0.05 * nrm(ks[8], (N_A_LAYERS, D), jnp.float32)
    hgrn_w_out = nrm(ks[9], (N_A_LAYERS, D, D), jnp.float32) * D ** -0.5
    attn_w_in = nrm(ks[10], (N_B_LAYERS, D, ATT_QKV_COLS), jnp.float32) * D ** -0.5
    attn_w_out = nrm(ks[11], (N_B_LAYERS, D, D), jnp.float32) * D ** -0.5
    ffn_w_in = nrm(ks[12], (DEPTH, D, 2 * D_FF_2), jnp.float32) * D ** -0.5
    ffn_w_out = nrm(ks[13], (DEPTH, D_FF_2, D), jnp.float32) * D_FF_2 ** -0.5
    return {'x': x, 'c': c, 'positions': positions, 'ada_w': ada_w, 'ada_b': ada_b,
            'norm_g': norm_g, 'hgrn_w_in': hgrn_w_in, 'hgrn_lower_bounds': hgrn_lower_bounds,
            'hgrn_norm_g': hgrn_norm_g, 'hgrn_w_out': hgrn_w_out, 'attn_w_in': attn_w_in,
            'attn_w_out': attn_w_out, 'ffn_w_in': ffn_w_in, 'ffn_w_out': ffn_w_out}

def second_block(x, c, positions, ada_w, ada_b, norm_g, hgrn_w_in, hgrn_lower_bounds,
              hgrn_norm_g, hgrn_w_out, attn_w_in, attn_w_out, ffn_w_in, ffn_w_out):
    cond = jax.nn.silu(c)
    inv_freq = ROPE_THETA ** (-jnp.arange(0, ROPE_DIM, 2, dtype=jnp.float32) / ROPE_DIM)
    ang = positions.astype(jnp.float32)[..., None] * inv_freq
    cos = jnp.cos(ang)[:, :, None, :]
    sin = jnp.sin(ang)[:, :, None, :]
    lbs = jnp.cumsum(jax.nn.softmax(hgrn_lower_bounds.astype(jnp.float32), axis=0), axis=0)
    lbs = lbs - lbs[0:1]
    h = x
    for layer in range(DEPTH):
        mod = (cond @ ada_w[layer] + ada_b[layer])[:, None, :]
        sh1, sc1, g1, sh2, sc2, g2 = jnp.split(mod, 6, axis=-1)
        u = rms_norm_2(h, norm_g[layer, 0]) * (1.0 + sc1) + sh1
        idx = layer // N_MIXERS
        if layer % N_MIXERS == 0:
            y = hgrn2_mixer(u, hgrn_w_in[idx], lbs[idx], hgrn_norm_g[idx], hgrn_w_out[idx])
        else:
            y = dilated_attention_mixer(u, cos, sin, attn_w_in[idx], attn_w_out[idx])
        h = h + (1.0 + g1) * rms_norm_2(y, norm_g[layer, 1])
        u = rms_norm_2(h, norm_g[layer, 2]) * (1.0 + sc2) + sh2
        y = swiglu_ffn(u, ffn_w_in[layer], ffn_w_out[layer])
        h = h + (1.0 + g2) * rms_norm_2(y, norm_g[layer, 3])
    return h


def setup_inputs(seed=0):
    out = dict(first_inputs(seed))
    for name, value in second_inputs(seed + 1).items():
        if name != "x":
            out[name + "_2"] = value
    return out


def reference(
    x, c, ctx, c_ctx, norm1_g, norm2_g, w_mod, b_mod, w_in, q_norm_g, kv_norm_g, w_uq, w_ukv,
    hy_conv_w, hy_conv_b, hy_w1, hy_b1, hy_freq, hy_w2, hy_b2, hy_w3, hy_d, w_out, w_mlp1,
    w_mlp2, final_norm_g, c_2, positions_2, ada_w_2, ada_b_2, norm_g_2, hgrn_w_in_2,
    hgrn_lower_bounds_2, hgrn_norm_g_2, hgrn_w_out_2, attn_w_in_2, attn_w_out_2, ffn_w_in_2,
    ffn_w_out_2,
):
    x = first_block(
        x, c, ctx, c_ctx, norm1_g, norm2_g, w_mod, b_mod, w_in, q_norm_g, kv_norm_g, w_uq,
        w_ukv, hy_conv_w, hy_conv_b, hy_w1, hy_b1, hy_freq, hy_w2, hy_b2, hy_w3, hy_d, w_out,
        w_mlp1, w_mlp2, final_norm_g,
    )
    return second_block(
        x, c_2, positions_2, ada_w_2, ada_b_2, norm_g_2, hgrn_w_in_2, hgrn_lower_bounds_2,
        hgrn_norm_g_2, hgrn_w_out_2, attn_w_in_2, attn_w_out_2, ffn_w_in_2, ffn_w_out_2,
    )


_drawn_inputs = setup_inputs


def setup_inputs(seed=0):
    import zlib

    import numpy as np

    out = dict(_drawn_inputs(seed))
    spreads = {}
    factors = {'ctx': 3.389,
     'norm1_g': 2.864,
     'q_norm_g': 8.0,
     'kv_norm_g': 7.142,
     'hy_conv_b': 8.0,
     'hy_b1': 8.0,
     'hy_freq': 8.0,
     'hy_b2': 8.0}
    for name, (base, spread) in spreads.items():
        noise = np.random.default_rng([zlib.crc32(name.encode()), seed]).standard_normal(out[name].shape)
        drawn = base * np.exp(spread * noise) if base else spread * noise
        out[name] = jnp.asarray(drawn.astype(out[name].dtype))
    for name, factor in factors.items():
        out[name] = (out[name] * factor).astype(out[name].dtype)
    return out
```

```python
import math
from contextlib import ExitStack, contextmanager

import numpy as np

import concourse.bass as bass
from concourse import mybir

F32 = mybir.dt.float32
I32 = mybir.dt.int32
ALU = mybir.AluOpType
ACT = mybir.ActivationFunctionType
AX = mybir.AxisListType.X

P = 128
D = 1024
KD = D // P
LX, LC = 512, 256
T = LX + LC
X_COLS, C_COLS = (0, LX), (LX, T)
DEPTH = 2
EPS = 1e-6

HEADS, NOPE, ROPE, VDIM = 8, 64, 32, 64
QK = NOPE + ROPE
Q_LORA, KV_LORA = 384, 256
OFF_KV = Q_LORA
OFF_KR = OFF_KV + KV_LORA
OFF_F = OFF_KR + ROPE
OFF_H = OFF_F + 256
IN_W = OFF_H + 768
HY = 256
D_FF = 4 * D
EMB, ORDER = 33, 64

H2 = 8
CHUNK = 32
D_FF2 = 2816
ROT = 32
GROUPS2 = 3

UNIT = 256
RING = 4
SLOT = 22 * P
BANKS = 8

TWO_PI = 2.0 * math.pi
PI1 = 6.28125
PI2 = float(np.float32(round((TWO_PI - PI1) * 2 ** 19) / 2 ** 19))
PI3 = TWO_PI - PI1 - PI2
ROUND = 1.5 * 2.0 ** 23
SIN_MAX = 3.1415925


class Signal:

    def __init__(self, nc, name, step=1):
        self.sem = nc.alloc_semaphore(name)
        self.step, self.start, self.sent = step, 0, 0
        self.turn = None

    @property
    def one(self):
        self.sent += 1
        return self.sem, self.step

    def at(self, n):
        value = (self.start + n) * self.step
        return value if self.turn is None else value + self.turn[0] * (self.turn[1] * self.step)

    def settle(self):
        self.start += self.sent
        self.sent = 0


class Signals:
    def __init__(self, nc):
        self.named = {}

        def signal(key, name, step=1):
            self.named[key] = Signal(nc, name, step)
            return self.named[key]

        self.weights = [Signal(nc, f"weights_landed_{s}", 16) for s in range(RING)]
        self.acc = signal("acc", "accumulated")
        self.by_act = signal("by_act", "evacuated_by_act")
        self.by_dve = signal("by_dve", "evacuated_by_dve")
        self.landed = signal("landed", "tables_landed", 16)
        self.dve = signal("dve", "dve_step")
        self.act = signal("act", "act_step")
        self.pe = signal("pe", "pe_step")
        self.sq_act = signal("sq_act", "squares_by_act")
        self.sq_dve = signal("sq_dve", "squares_by_dve")
        self.summed = signal("summed", "squares_summed")
        self.rstd = signal("rstd", "rstd_ready")
        self.normed = signal("normed", "normed")
        self.scaled = signal("scaled", "scaled")
        self.scores = signal("scores", "scores_ready")
        self.masked = signal("masked", "scores_masked")
        self.maxed = signal("maxed", "max_ready")
        self.exped = signal("exped", "exp_ready")
        self.recip = signal("recip", "reciprocal_ready")
        self.probs = signal("probs", "probs_ready")
        self.turned = signal("turned", "probs_transposed")
        self.probs_t = signal("probs_t", "transposed_probs_stored")
        self.mixed = signal("mixed", "values_mixed")
        self.stored = signal("stored", "heads_stored")
        self.out = signal("out", "output_stored", 16)

    def all(self):
        return self.weights + list(self.named.values())

    @contextmanager
    def stage(self, nc):
        with nc.Block() as block:
            yield block
        for s in self.all():
            s.settle()

    @contextmanager
    def loop(self, nc, n, **per_turn):
        before = {s: s.start for s in self.all()}
        strides = {}
        for name, k in per_turn.items():
            for j, s in enumerate(self.weights if name == "weights" else [self.named[name]]):
                strides[s] = k[j] if name == "weights" else k
        with nc.Fori(0, n) as i:
            for s, k in strides.items():
                s.turn = (i, k)
            yield i
        made = {s.sem.name: s.start - before[s] for s in before if s.start != before[s]}
        for s in before:
            assert s.start - before[s] == strides.get(s, 0), made
            s.turn = None
            s.start = before[s] + n * strides.get(s, 0)


class Job:

    def __init__(self, lhsT, rhs, kt, m, n, engine, evac, needs=(), after=()):
        self.lhsT, self.rhs, self.kt, self.m, self.n = lhsT, rhs, kt, m, n
        self.engine, self.evac, self.needs, self.after = engine, evac, needs, after


def project(nc, S, M, units):
    jobs = [j for _, _, js in units for j in js]
    ends = np.cumsum([len(js) for _, _, js in units])
    nth = []
    count = {"act": 0, "dve": 0}
    for j in jobs:
        count[j.engine] += 1
        nth.append(count[j.engine])
    done = {"act": S.by_act, "dve": S.by_dve}

    def wait_job(eng, j):
        s = done[jobs[j].engine]
        eng.wait_ge(s.sem, s.at(nth[j]))

    with S.stage(nc) as block:
        @block.sync
        def _(sp):
            for u, (src, place, _) in enumerate(units):
                if u >= RING:
                    sp.wait_ge(S.acc.sem, S.acc.at(int(ends[u - RING])))
                sp.dma_start(place(M.ring[:, u % RING, :]), src).then_inc(*S.weights[u % RING].one)

        @block.tensor
        def _(pe):
            n = 0
            for u, (_, place, js) in enumerate(units):
                w = place(M.ring[:, u % RING, :])
                s = S.weights[u % RING]
                pe.wait_ge(s.sem, s.at(u // RING + 1))
                for j in js:
                    if n >= BANKS:
                        wait_job(pe, n - BANKS)
                    for need in j.needs:
                        wait_job(pe, need)
                    acc = M.ps[0:j.m, n % BANKS, 0:j.n]
                    for k in range(j.kt):
                        mm = pe.matmul(acc, j.lhsT(w, k), j.rhs(w, k), start=k == 0, stop=k == j.kt - 1)
                    mm.then_inc(*S.acc.one)
                    n += 1

        def empty(eng, name):
            for n, j in enumerate(jobs):
                if j.engine == name:
                    eng.wait_ge(S.acc.sem, S.acc.at(n + 1))
                    for other in j.after:
                        wait_job(eng, other)
                    j.evac(eng, M.ps[0:j.m, n % BANKS, 0:j.n]).then_inc(*done[name].one)

        @block.scalar
        def _(act):
            empty(act, "act")

        @block.vector
        def _(dve):
            empty(dve, "dve")


def tiles(w, r0, r1, c0, c1, n=UNIT):
    cols = slice(c0, c1) if isinstance(c0, int) else bass.ds(c0, n)
    return w[r0:r1, cols].rearrange("(k p) n -> p k n", p=P)


def placed(kt, n):
    return lambda slot: slot[:, 0:kt * n].rearrange("p (k n) -> p k n", k=kt)


def feature_jobs(rhs, kt, blocks, groups, engine, evac, m=P):
    return [
        Job(lambda w, k, c=c: w[:, k, c:c + m], lambda w, k, g=g: rhs(k, *g), kt, m, g[1] - g[0],
            engine(b) if callable(engine) else engine, lambda e, acc, b=b, g=g: evac(e, acc, b, g))
        for b, c in blocks for g in groups
    ]


def norm(nc, S, M, src, kt, width, groups, out, scale, bias=None, n_tokens=None):
    lo, hi = groups[0][0], groups[-1][1]
    w = hi - lo
    sq, rs, tmp = M.sq, M.rs, M.tmp
    with S.stage(nc) as block:
        @block.scalar
        def _(act):
            for k in range(0, kt, 2):
                if k >= 2:
                    act.wait_ge(S.summed.sem, S.summed.at(k - 1))
                act.activation(sq[:, 0, 0:w], src(k, lo, hi), ACT.Square).then_inc(*S.sq_act.one)
            act.wait_ge(S.summed.sem, S.summed.at(kt))
            for g, (a, b) in enumerate(groups):
                ln = act.activation(rs[:, a - lo:b - lo], M.ps[:, g, 0:b - a], ACT.Ln, scale=1.0 / width,
                                    bias=M.eps[:, 0:1])
            ln.then_inc(*S.act.one)
            act.wait_ge(S.act.sem, S.act.at(1))
            act.activation(rs[:, 0:w], rs[:, 0:w], ACT.Exp, scale=-0.5).then_inc(*S.rstd.one)
            for k in range(kt):
                act.wait_ge(S.normed.sem, S.normed.at(k + 1))
                for a, b in groups:
                    o = act.activation(out(k, a, b), tmp[:, k % 2, a - lo:b - lo], ACT.Identity,
                                       scale=scale(k, a), bias=0.0 if bias is None else bias(k, a))
                o.then_inc(*S.scaled.one)

        @block.vector
        def _(dve):
            for k in range(1, kt, 2):
                if k >= 2:
                    dve.wait_ge(S.summed.sem, S.summed.at(k - 1))
                dve.tensor_tensor(sq[:, 1, 0:w], src(k, lo, hi), src(k, lo, hi), ALU.mult).then_inc(*S.sq_dve.one)
            dve.wait_ge(S.rstd.sem, S.rstd.at(1))
            for k in range(kt):
                if k >= 2:
                    dve.wait_ge(S.scaled.sem, S.scaled.at(k - 1))
                dve.tensor_tensor(tmp[:, k % 2, 0:w], src(k, lo, hi), rs[:, 0:w], ALU.mult).then_inc(*S.normed.one)

        @block.tensor
        def _(pe):
            for k in range(kt):
                s = S.sq_dve if k % 2 else S.sq_act
                pe.wait_ge(s.sem, s.at(k // 2 + 1))
                for g, (a, b) in enumerate(groups):
                    mm = pe.matmul(M.ps[:, g, 0:b - a], M.ones[:, :], sq[:, k % 2, a - lo:b - lo],
                                   start=k == 0, stop=k == kt - 1)
                mm.then_inc(*S.summed.one)


def chain(eng, sig, ins):
    ins.then_inc(*sig.one)
    eng.wait_ge(sig.sem, sig.at(sig.sent))


def load(nc, S, pairs):
    with S.stage(nc) as block:
        @block.sync
        def _(sp):
            for dst, src in pairs:
                sp.dma_start(dst, src).then_inc(*S.landed.one)
            sp.wait_ge(S.landed.sem, S.landed.at(len(pairs)))
            sp.nop()


def reduce_angle(dve, S, x, k):
    chain(dve, S.dve, dve.tensor_scalar(k, x, 1.0 / TWO_PI, ROUND, ALU.mult, ALU.add))
    chain(dve, S.dve, dve.tensor_scalar(k, k, -ROUND, None, ALU.add))
    for part in (PI1, PI2, PI3):
        chain(dve, S.dve, dve.scalar_tensor_tensor(x, k, -part, x, ALU.mult, ALU.add))
    chain(dve, S.dve, dve.tensor_scalar(x, x, SIN_MAX, -SIN_MAX, ALU.min, ALU.max))


def attention(nc, S, M, heads, nb, kt, score, mask, mix, width, store, p, p_t):
    n_items = heads * nb
    w = kt * P

    def s_ps(n):
        return M.ps[:, 2 * (n % 2):2 * (n % 2) + 2, :].rearrange("p a b -> p (a b)")[:, 0:w]

    t_ps = M.ps[:, 4:6, :].rearrange("p a b -> p (a b)")[:, 0:w]

    with S.stage(nc) as block:
        @block.tensor
        def _(pe):
            def scores(n):
                if n >= 2:
                    pe.wait_ge(S.exped.sem, S.exped.at(n - 1))
                score(pe, n // nb, n % nb, s_ps(n)).then_inc(*S.scores.one)

            def values(h):
                pe.wait_ge(S.probs_t.sem, S.probs_t.at((h + 1) * nb))
                if h >= 2:
                    pe.wait_ge(S.stored.sem, S.stored.at(h - 1))
                mix(pe, h, M.ps[:, 6 + h % 2, :]).then_inc(*S.mixed.one)

            scores(0)
            for n in range(n_items):
                if n + 1 < n_items:
                    scores(n + 1)
                pe.wait_ge(S.probs.sem, S.probs.at(n + 1))
                if n >= 1:
                    pe.wait_ge(S.probs_t.sem, S.probs_t.at(n))
                for j in range(kt):
                    tr = pe.transpose(t_ps[:, j * P:(j + 1) * P], p[:, n % 2, j * P:(j + 1) * P], M.ident[:, :])
                tr.then_inc(*S.turned.one)
                if n % nb == 0 and n:
                    values(n // nb - 1)
            values(heads - 1)

        @block.vector
        def _(dve):
            def maximum(n):
                dve.wait_ge(S.scores.sem, S.scores.at(n + 1))
                src = s_ps(n)
                if mask:
                    if n >= 2:
                        dve.wait_ge(S.turned.sem, S.turned.at(n - 1))
                    for a, b, m in mask(n % nb):
                        added = dve.tensor_tensor(p[:, n % 2, a:b], src[:, a:b], m, ALU.add)
                    added.then_inc(*S.masked.one)
                    dve.wait_ge(S.masked.sem, S.masked.at(n + 1))
                    src = p[:, n % 2, 0:w]
                dve.tensor_reduce(M.nmax[:, n % 4:n % 4 + 1], src, AX, ALU.max, negate=True).then_inc(*S.maxed.one)

            def normalise(n):
                dve.wait_ge(S.exped.sem, S.exped.at(n + 1))
                dve.reciprocal(M.rsum[:, n % 4:n % 4 + 1], M.esum[:, n % 4:n % 4 + 1]).then_inc(*S.recip.one)
                dve.wait_ge(S.recip.sem, S.recip.at(n + 1))
                dve.tensor_scalar(p[:, n % 2, 0:w], p[:, n % 2, 0:w], M.rsum[:, n % 4:n % 4 + 1], None,
                                  ALU.mult).then_inc(*S.probs.one)

            def head(h):
                dve.wait_ge(S.mixed.sem, S.mixed.at(h + 1))
                store(dve, h, M.ps[:, 6 + h % 2, :]).then_inc(*S.stored.one)

            for n in range(n_items):
                maximum(n)
                if n:
                    normalise(n - 1)
                if n > nb and n % nb == 1 % nb:
                    head(n // nb - 1 if nb > 1 else n - 2)
            normalise(n_items - 1)
            if heads > 1 and nb == 1:
                head(heads - 2)
            head(heads - 1)

        @block.scalar
        def _(act):
            def exponent(n):
                act.wait_ge(S.maxed.sem, S.maxed.at(n + 1))
                if not mask and n >= 2:
                    act.wait_ge(S.turned.sem, S.turned.at(n - 1))
                src = p[:, n % 2, 0:w] if mask else s_ps(n)
                act.activation(p[:, n % 2, 0:w], src, ACT.Exp, bias=M.nmax[:, n % 4:n % 4 + 1],
                               accum_out=M.esum[:, n % 4:n % 4 + 1]).then_inc(*S.exped.one)

            def keep(n):
                act.wait_ge(S.turned.sem, S.turned.at(n + 1))
                if n % nb == 0 and n:
                    act.wait_ge(S.mixed.sem, S.mixed.at(n // nb))
                b = n % nb
                act.activation(p_t[:, 0:kt, b * P:(b + 1) * P], t_ps.rearrange("p (k q) -> p k q", k=kt),
                               ACT.Copy).then_inc(*S.probs_t.one)

            for n in range(n_items):
                exponent(n)
                if n:
                    keep(n - 1)
            keep(n_items - 1)



def fourier(nc, S, M, io, ss, lo, length):
    nt = length // P
    with ExitStack() as ctx:
        chan = ctx.enter_context(nc.sbuf_tensor(f"chan{ss}", [P, 2 * P], F32))
        ab = ctx.enter_context(nc.sbuf_tensor(f"ab{ss}", [P, nt, 2, 2, P], F32))
        tok = M.ring[:, :, :].rearrange("p a b -> p (a b)")[:, 0:nt * 2 * length].rearrange(
            "p (t c l) -> p t c l", t=nt, c=2)
        load(nc, S, [(chan[:, :], io["fnet_channels"]), (tok, io[f"fnet_tokens_{length}"])])
        with S.stage(nc) as block:
            @block.tensor
            def _(pe):
                for n in range(2 * nt):
                    t, f = divmod(n, 2)
                    mm = pe.matmul(M.ps[:, n % 8, 0:2 * P], M.p[:, 6 + f, lo + t * P:lo + (t + 1) * P], chan[:, :],
                                   start=True, stop=True)
                    mm.then_inc(*S.pe.one)
                for f in range(2):
                    for t in range(nt):
                        for c in range(2):
                            if f == 0 and c == 0:
                                pe.wait_ge(S.by_dve.sem, S.by_dve.at(2 * nt))
                            mm = pe.matmul(M.ps[:, f, 0:length], ab[:, t, f, c, :], tok[:, t, c, :],
                                           start=t == 0 and c == 0, stop=t == nt - 1 and c == 1)
                    mm.then_inc(*S.acc.one)

            @block.vector
            def _(dve):
                for n in range(2 * nt):
                    t, f = divmod(n, 2)
                    dve.wait_ge(S.pe.sem, S.pe.at(n + 1))
                    dve.tensor_copy(ab[:, t, f, :, :].rearrange("p c n -> p (c n)"),
                                    M.ps[:, n % 8, 0:2 * P]).then_inc(*S.by_dve.one)

            @block.scalar
            def _(act):
                for f in range(2):
                    act.wait_ge(S.acc.sem, S.acc.at(f + 1))
                    act.activation(M.h[:, 4 + f, lo:lo + length], M.ps[:, f, 0:length], ACT.Copy).then_inc(*S.act.one)


def hyena(nc, S, M, io, l, ss, lo, length):
    nt = length // P
    with ExitStack() as ctx:
        def sb(name, shape):
            return ctx.enter_context(nc.sbuf_tensor(f"{name}{ss}", shape, F32))

        flat = M.ring[:, :, :].rearrange("p a b -> p (a b)")
        half = nt * 2 * length
        tk = flat[:, 0:half].rearrange("p (t c f) -> p t c f", t=nt, c=2)
        ta = flat[:, half:2 * half].rearrange("p (t c f) -> p t c f", t=nt, c=2)
        emb = sb("emb", [EMB, length])
        w1 = sb("w1", [EMB, ORDER])
        w2 = sb("w2", [ORDER, ORDER])
        w3 = sb("w3", [ORDER, 2 * HY])
        hid = sb("hid", [ORDER, 2, length])
        kk = sb("kk", [ORDER, length])
        decay = sb("decay", [P, nt, 2 * HY])
        filt = sb("filt", [P, nt, 2 * HY])
        pm = sb("pm", [P, nt, 2, HY])
        inv = sb("inv", [P, HY])
        kf = decay[:, :, :].rearrange("p t (c n) -> p t c n", c=2)
        u = sb("u", [P, 6, length])
        zt = sb("zt", [P, nt, HY])
        yf = sb("yf", [P, nt, 2, HY])
        m4 = filt[:, 0:2, :].rearrange("p a (c n) -> p a c n", c=2)
        pairs = [(emb[:, :], io[f"hy_emb_{length}"]), (w1[:, :], io["hy_w1"][l]), (w2[:, :], io["hy_w2"][l]),
                 (w3[:, :], io["hy_w3"][l]), (decay[:, :, :], io[f"hy_decay_{length}"]),
                 (tk, io[f"hy_tk_{length}"]), (ta, io[f"hy_ta_{length}"])]
        load(nc, S, pairs)
        b1, b2, fr = (M.col(n, l)[0:ORDER] for n in ("hy_b1", "hy_b2", "hy_freq"))
        cw = lambda j, b: M.col("hy_conv_w", l, 6 * j + b)
        p_in = lambda b: M.p[:, 8 + b, lo:lo + length]

        with S.stage(nc) as block:
            @block.tensor
            def _(pe):
                pe.matmul(M.ps[0:ORDER, 0, 0:length], w1[:, :], emb[:, :], start=True, stop=True).then_inc(*S.pe.one)
                pe.wait_ge(S.act.sem, S.act.at(1))
                pe.matmul(M.ps[0:ORDER, 1, 0:length], w2[:, :], hid[:, 0, :], start=True, stop=True).then_inc(*S.pe.one)
                pe.wait_ge(S.act.sem, S.act.at(2))
                for t in range(nt):
                    pe.matmul(M.ps[:, 2 + t, 0:2 * HY], hid[:, 1, t * P:(t + 1) * P], w3[:, :],
                              start=True, stop=True).then_inc(*S.pe.one)
                for t in range(nt):
                    pe.wait_ge(S.by_act.sem, S.by_act.at(t + 1))
                    mm = pe.matmul(M.ps[:, 7, 0:2 * HY], M.ones[:, :], yf[:, t, :, :].rearrange("p c n -> p (c n)"),
                                   start=t == 0, stop=t == nt - 1)
                mm.then_inc(*S.acc.one)

            @block.vector
            def _(dve):
                for s, b in ((0, b1), (1, b2)):
                    dve.wait_ge(S.pe.sem, S.pe.at(s + 1))
                    chain(dve, S.dve, dve.tensor_scalar(hid[:, s, :], M.ps[0:ORDER, s, 0:length], b, fr,
                                                        ALU.add, ALU.mult))
                    reduce_angle(dve, S, hid[:, s, :], kk[:, :])
                    dve.tensor_scalar(kk[:, :], hid[:, s, :], 1.0, None, ALU.mult).then_inc(*S.by_dve.one)
                for t in range(nt):
                    dve.wait_ge(S.pe.sem, S.pe.at(3 + t))
                    chain(dve, S.dve, dve.tensor_tensor(filt[:, t, :], M.ps[:, 2 + t, 0:2 * HY], decay[:, t, :],
                                                        ALU.mult))
                    dve.tensor_tensor(pm[:, t, 0, :], filt[:, t, 0:HY], filt[:, t, HY:2 * HY], ALU.add)
                    dve.tensor_tensor(pm[:, t, 1, :], filt[:, t, HY:2 * HY], filt[:, t, 0:HY],
                                      ALU.subtract).then_inc(*S.by_dve.one)
                for b in range(6):
                    chain(dve, S.dve, dve.tensor_scalar(u[:, b, :], p_in(b), cw(1, b), M.col("hy_conv_b", l, b),
                                                        ALU.mult, ALU.add))
                    chain(dve, S.dve, dve.scalar_tensor_tensor(u[:, b, 1:length], p_in(b)[:, 0:length - 1], cw(0, b),
                                                               u[:, b, 1:length], ALU.mult, ALU.add))
                    chain(dve, S.dve, dve.scalar_tensor_tensor(u[:, b, 0:length - 1], p_in(b)[:, 1:length], cw(2, b),
                                                               u[:, b, 0:length - 1], ALU.mult, ALU.add))
                for b in range(2):
                    dve.tensor_tensor(u[:, 2 + b, :], u[:, 2 + b, :], u[:, 4 + b, :], ALU.mult)
                dve.wait_ge(S.acc.sem, S.acc.at(1))
                chain(dve, S.dve, dve.tensor_copy(zt[:, 0, :], M.ps[:, 7, 0:HY]))
                chain(dve, S.dve, dve.tensor_tensor(inv[:, :], zt[:, 0, :], M.ps[:, 7, HY:2 * HY], ALU.add))
                chain(dve, S.dve, dve.tensor_scalar(inv[:, :], inv[:, :], float(length), None, ALU.mult))
                dve.reciprocal(inv[:, :], inv[:, :])

            @block.scalar
            def _(act):
                for s in range(2):
                    act.wait_ge(S.by_dve.sem, S.by_dve.at(s + 1))
                    act.activation(hid[:, s, :], kk[:, :], ACT.Sin).then_inc(*S.act.one)
                for t in range(nt):
                    act.wait_ge(S.by_dve.sem, S.by_dve.at(3 + t))
                    act.activation(yf[:, t, :, :].rearrange("p c n -> p (c n)"), filt[:, t, :],
                                   ACT.Abs).then_inc(*S.by_act.one)

        with S.stage(nc) as block:
            @block.tensor
            def _(pe):
                for b in range(2):
                    for t in range(nt):
                        pe.transpose(M.ps[:, b, t * P:(t + 1) * P], u[:, 2 + b, t * P:(t + 1) * P],
                                     M.ident[:, :]).then_inc(*S.pe.one)
                for f in range(nt):
                    if f >= 2:
                        pe.wait_ge(S.by_act.sem, S.by_act.at(f - 1))
                    for c in range(2):
                        for t in range(nt):
                            mm = pe.matmul(M.ps[:, 2 + f % 2, c * HY:(c + 1) * HY], tk[:, t, c, f * P:(f + 1) * P],
                                           pm[:, t, c, :], start=t == 0, stop=t == nt - 1)
                    mm.then_inc(*S.acc.one)
                    pe.wait_ge(S.act.sem, S.act.at(2))
                    if f >= 2:
                        pe.wait_ge(S.mixed.sem, S.mixed.at(f - 1))
                    for c in range(2):
                        for t in range(nt):
                            mm = pe.matmul(M.ps[:, 4 + f % 2, c * HY:(c + 1) * HY], ta[:, t, c, f * P:(f + 1) * P],
                                           zt[:, t, :], start=t == 0, stop=t == nt - 1)
                    mm.then_inc(*S.scores.one)
                pe.wait_ge(S.mixed.sem, S.mixed.at(nt))
                for b in range(2):
                    for f in range(nt):
                        for c in range(2):
                            mm = pe.matmul(M.ps[:, 6 + b, 0:length], yf[:, f, c, b * P:(b + 1) * P], ta[:, f, c, :],
                                           start=f == 0 and c == 0, stop=f == nt - 1 and c == 1)
                    mm.then_inc(*S.probs.one)

            @block.scalar
            def _(act):
                for b in range(2):
                    act.wait_ge(S.pe.sem, S.pe.at((b + 1) * nt))
                    act.activation(zt[:, :, b * P:(b + 1) * P],
                                   M.ps[:, b, 0:length].rearrange("p (t c) -> p t c", t=nt), ACT.Copy)\
                        .then_inc(*S.act.one)
                for f in range(nt):
                    act.wait_ge(S.acc.sem, S.acc.at(f + 1))
                    act.activation(kf[:, f, :, :].rearrange("p c n -> p (c n)"), M.ps[:, 2 + f % 2, :],
                                   ACT.Copy).then_inc(*S.by_act.one)

            @block.vector
            def _(dve):
                for f in range(nt):
                    dve.wait_ge(S.by_act.sem, S.by_act.at(f + 1))
                    for c in range(2):
                        k = dve.tensor_tensor(kf[:, f, c, :], kf[:, f, c, :], inv[:, :], ALU.mult)
                    chain(dve, S.dve, k)
                    dve.wait_ge(S.scores.sem, S.scores.at(f + 1))
                    zc, zs = M.ps[:, 4 + f % 2, 0:HY], M.ps[:, 4 + f % 2, HY:2 * HY]
                    dve.tensor_tensor(m4[:, 0, 0, :], zc, kf[:, f, 0, :], ALU.mult)
                    dve.tensor_tensor(m4[:, 0, 1, :], zs, kf[:, f, 1, :], ALU.mult)
                    dve.tensor_tensor(m4[:, 1, 0, :], zs, kf[:, f, 0, :], ALU.mult)
                    chain(dve, S.dve, dve.tensor_tensor(m4[:, 1, 1, :], zc, kf[:, f, 1, :], ALU.mult))
                    dve.tensor_tensor(yf[:, f, 0, :], m4[:, 0, 0, :], m4[:, 0, 1, :], ALU.add)
                    y = dve.tensor_tensor(yf[:, f, 1, :], m4[:, 1, 0, :], m4[:, 1, 1, :], ALU.subtract)
                    y.then_inc(*S.mixed.one)
                    dve.wait_ge(S.mixed.sem, S.mixed.at(f + 1))
                for b in range(2):
                    dve.wait_ge(S.probs.sem, S.probs.at(b + 1))
                    chain(dve, S.dve, dve.scalar_tensor_tensor(u[:, 2 + b, :], u[:, 2 + b, :], M.col("hy_d", l, b),
                                                               M.ps[:, 6 + b, 0:length], ALU.mult, ALU.add))
                    dve.tensor_tensor(M.h[:, 6 + b, lo:lo + length], u[:, 2 + b, :], u[:, b, :],
                                      ALU.mult).then_inc(*S.by_dve.one)


def first_layer(nc, S, M, io, l):
    last = l == DEPTH - 1
    groups = [X_COLS, C_COLS]
    outer = [X_COLS] if last else groups
    side = lambda a: 0 if a < LX else 1
    x = lambda k, a, b: M.x[:, k, a:b]
    h = lambda k, a, b: M.h[:, k, a:b]
    w_in = io["w_in"][l]

    norm(nc, S, M, x, KD, D, groups, h, lambda k, a: M.gain[:, 2 * l, side(a), k:k + 1],
         lambda k, a: M.mod(l, 0, k, side(a)))
    with ExitStack() as ctx:
        M.p = ctx.enter_context(nc.sbuf_tensor(f"p{l}", [P, 14, T], F32))

        def keep(e, acc, b, g):
            m = QK if b == 5 else P
            if e is nc.scalar:
                return e.activation(M.p[0:m, b, g[0]:g[1]], acc, ACT.Copy)
            return e.tensor_copy(M.p[0:m, b, g[0]:g[1]], acc)

        cuts = [(0, [0, 1]), (256, [2, 3]), (512, [4, 5]), (OFF_F, [6, 7]), (OFF_H, [8, 9]),
                (OFF_H + 256, [10, 11]), (OFF_H + 512, [12, 13])]
        units = []
        for c0, blocks in cuts:
            js = []
            for n, b in enumerate(blocks):
                gs = groups if b in (3, 4, 5) else outer
                off, m = (64, QK) if b == 5 else (n * P, P)
                js += feature_jobs(h, KD, [(b, off)], gs, lambda b: "act" if b % 2 else "dve", keep, m)
            units.append((tiles(w_in, 0, D, c0, c0 + UNIT), placed(KD, UNIT), js))
        project(nc, S, M, units)

        norm(nc, S, M, lambda k, a, b: M.p[:, k, a:b], 3, Q_LORA, outer, h,
             lambda k, a: M.col("q_norm_g", l, k))
        norm(nc, S, M, lambda k, a, b: M.p[:, 3 + k, a:b], 2, KV_LORA, groups, lambda k, a, b: M.h[:, 3 + k, a:b],
             lambda k, a: M.col("kv_norm_g", l, k))

        with ExitStack() as att:
            q = att.enter_context(nc.sbuf_tensor(f"q{l}", [P, HEADS, T], F32))
            k_t = att.enter_context(nc.sbuf_tensor(f"k{l}", [P, HEADS, T], F32))
            v = M.p[:, 0:4, :].rearrange("p a b -> p (a b)").rearrange("p (t n) -> p t n", t=T // P)
            scale = 1.0 / math.sqrt(QK)

            def keep_q(e, acc, b, g):
                return e.activation(q[0:QK, b, g[0]:g[1]], acc, ACT.Copy, scale=scale)

            def keep_k(e, acc, b, g):
                return e.tensor_copy(k_t[0:NOPE, b, g[0]:g[1]], acc)

            ukv = lambda w: w[:, 0:2 * D].rearrange("p (k n) -> p k n", k=2)
            vcols = lambda w, k: w[:, k, :].rearrange("p (h n) -> p h n", h=HEADS)[:, :, NOPE:NOPE + VDIM]
            jobs_kv = feature_jobs(lambda k, a, b: M.h[:, 3 + k, a:b], 2, [(b, b * P) for b in range(HEADS)],
                                   groups, "dve", keep_k, NOPE)
            jobs_kv += [Job(lambda w, k, t=t: M.h[:, 3 + k, t * P:(t + 1) * P], vcols, 2, P, HEADS * VDIM, "act",
                            lambda e, acc, t=t: e.activation(v[:, t, :], acc, ACT.Copy)) for t in range(T // P)]
            project(nc, S, M, [
                (tiles(io["w_uq"][l], 0, Q_LORA, 0, HEADS * QK), placed(3, HEADS * QK),
                 feature_jobs(h, 3, [(b, b * QK) for b in range(HEADS)], outer, "act", keep_q, QK)),
                (tiles(io["w_ukv"][l], 0, KV_LORA, 0, D), ukv, jobs_kv),
            ])

            lo, hi = NOPE, QK
            swap = M.ring[:, 0, 0:P]
            rope = M.ring[:, 0, P:P + 2 * LX].rearrange("p (c t) -> p c t", c=2)
            load(nc, S, [(swap, io["rope_swap"]), (rope, io["rope_tables"])])
            srcs = [q[0:QK, b, 0:LX] for b in range(HEADS)] + [M.p[0:QK, 5, 0:LX]]
            with S.stage(nc) as block:
                @block.tensor
                def _(pe):
                    for n, s in enumerate(srcs):
                        if n >= 8:
                            pe.wait_ge(S.by_dve.sem, S.by_dve.at(n - 7))
                        pe.matmul(M.ps[0:QK, n % 8, :], swap[0:QK, 0:QK], s, start=True, stop=True)\
                            .then_inc(*S.pe.one)

                @block.vector
                def _(dve):
                    for n, s in enumerate(srcs):
                        dve.wait_ge(S.pe.sem, S.pe.at(n + 1))
                        t = M.sq[lo:hi, n % 2, 0:LX]
                        dve.tensor_tensor(t, M.ps[lo:hi, n % 8, :], rope[lo:hi, 1, :], ALU.mult)
                        chain(dve, S.dve, dve.tensor_tensor(s[lo:hi, :], s[lo:hi, :], rope[lo:hi, 0, :], ALU.mult))
                        dve.tensor_tensor(s[lo:hi, :], s[lo:hi, :], t, ALU.add).then_inc(*S.by_dve.one)
                        dve.wait_ge(S.by_dve.sem, S.by_dve.at(n + 1))

                @block.scalar
                def _(act):
                    act.wait_ge(S.by_dve.sem, S.by_dve.at(len(srcs)))
                    for b in range(HEADS):
                        act.activation(k_t[lo:hi, b, :], M.p[lo:hi, 5, :], ACT.Copy).then_inc(*S.act.one)

            flat = M.ring[:, :, :].rearrange("p a b -> p (a b)")
            p_t = flat[:, 0:6 * LX].rearrange("p (k q) -> p k q", k=6)
            p = flat[:, 6 * LX:6 * LX + 2 * T].rearrange("p (a b) -> p a b", a=2)
            for lo_q, lo_k, nb, kt in [(0, 0, LX // P, T // P)] + ([] if last else [(LX, LX, LC // P, LC // P)]):
                def score(pe, hd, b, acc):
                    for a in range(0, kt * P, 512):
                        n = min(512, kt * P - a)
                        mm = pe.matmul(acc[:, a:a + n], q[0:QK, hd, lo_q + b * P:lo_q + (b + 1) * P],
                                       k_t[0:QK, hd, lo_k + a:lo_k + a + n], start=True, stop=True)
                    return mm

                def mix(pe, hd, acc):
                    for j in range(kt):
                        mm = pe.matmul(acc[0:VDIM, 0:nb * P], v[:, lo_k // P + j, hd * VDIM:(hd + 1) * VDIM],
                                       p_t[:, j, 0:nb * P], start=j == 0, stop=j == kt - 1)
                    return mm

                def store(dve, hd, acc):
                    r = hd % 2 * VDIM
                    return dve.tensor_copy(M.h[r:r + VDIM, hd // 2, lo_q:lo_q + nb * P], acc[0:VDIM, 0:nb * P])

                attention(nc, S, M, HEADS, nb, kt, score, None, mix, nb * P, store, p, p_t)

        for ss, lo, length in [(f"x{l}", 0, LX)] + ([] if last else [(f"c{l}", LX, LC)]):
            fourier(nc, S, M, io, ss, lo, length)
            hyena(nc, S, M, io, l, ss, lo, length)

    def residual(m):
        def add(e, acc, b, g):
            xs = M.x[:, b, g[0]:g[1]]
            return e.scalar_tensor_tensor(xs, acc, M.mod(l, m, b, side(g[0])), xs, ALU.mult, ALU.add)
        return add

    w_out = io["w_out"][l]
    project(nc, S, M, [(tiles(w_out, 0, D, c * UNIT, (c + 1) * UNIT), placed(KD, UNIT),
                        feature_jobs(h, KD, [(2 * c, 0), (2 * c + 1, P)], outer, "dve", residual(2)))
                       for c in range(4)])

    norm(nc, S, M, x, KD, D, outer, h, lambda k, a: M.gain[:, 2 * l + 1, side(a), k:k + 1],
         lambda k, a: M.mod(l, 3, k, side(a)))
    with nc.sbuf_tensor(f"hidden{l}", [P, 8, T], F32) as hid:
        ng = len(outer)
        jobs = 8 * ng
        with S.loop(nc, D_FF // D, weights=[2] * 4, acc=2 * jobs, by_act=jobs, by_dve=jobs, act=jobs) as i:
            def relu2(e, acc, b, g):
                dst = hid[:, b, g[0]:g[1]]
                chain(e, S.act, e.activation(dst, acc, ACT.Relu))
                return e.activation(dst, dst, ACT.Square)

            units = [(tiles(io["w_mlp1"][l], 0, D, i * D + c * UNIT, i * D + (c + 1) * UNIT), placed(KD, UNIT),
                      feature_jobs(h, KD, [(2 * c, 0), (2 * c + 1, P)], outer, "act", relu2)) for c in range(4)]
            w2 = io["w_mlp2"][l].rearrange("(g k p) n -> g p k n", p=P, k=KD)
            for c in range(4):
                js = feature_jobs(lambda k, a, b: hid[:, k, a:b], KD, [(2 * c, 0), (2 * c + 1, P)], outer, "dve",
                                  residual(5))
                js[0].needs = (8 * ng - 1,)
                units.append((w2[i, :, :, c * UNIT:(c + 1) * UNIT], placed(KD, UNIT), js))
            project(nc, S, M, units)



def recurrence(nc, S, M, io):
    w = io["hgrn_w_in_2"][0]
    nch = LX // CHUNK
    h = lambda k, a, b: M.h[:, k, a:b]
    with ExitStack() as ctx:
        def sb(name, shape):
            return ctx.enter_context(nc.sbuf_tensor("r_" + name, shape, F32))

        qs, sg, kk, gs = (sb(n, [P, 2, LX]) for n in ("q", "sg", "k", "g"))
        b_, eb, nb_, ke = (sb(n, [P, 2, LX]) for n in ("b", "eb", "nb", "ke"))
        v = sb("v", [P, 4, UNIT])
        ket = sb("ket", [P, 2, 4, P])
        at = sb("at", [P, 2, LX])
        st = sb("st", [P, 2, nch, P])
        y = M.y
        with S.loop(nc, H2 // 2, **LOOPS["recurrence"]) as i:
            def unit(sec, jobs):
                return (tiles(w, 0, D, sec * D + i * UNIT, sec * D + (i + 1) * UNIT), placed(KD, UNIT), jobs)

            def forget(e, acc, b, g):
                e.activation(kk[:, b, :], acc, ACT.Sigmoid, scale=-1.0)
                return e.activation(sg[:, b, :], acc, ACT.Sigmoid)

            blocks = [(0, 0), (1, P)]
            token = [Job(lambda w, k, t=t: M.h[:, k, t * P:(t + 1) * P], lambda w, k: w[:, k, :], KD, P, UNIT, "dve",
                         lambda e, acc, t=t: e.tensor_copy(v[:, t, :], acc)) for t in range(4)]
            project(nc, S, M, [
                unit(1, feature_jobs(h, KD, blocks, [X_COLS], "act", forget)),
                unit(0, feature_jobs(h, KD, blocks, [X_COLS], "act",
                                     lambda e, acc, b, g: e.activation(qs[:, b, :], acc, ACT.Silu))),
                unit(3, feature_jobs(h, KD, blocks, [X_COLS], "act",
                                     lambda e, acc, b, g: e.activation(gs[:, b, :], acc, ACT.Silu))),
                unit(2, token),
            ])
            with S.stage(nc) as block:
                @block.vector
                def _(dve):
                    for n in range(2):
                        om, lb = (M.lower[:, j, bass.ds(i * 2 + n, 1)] for j in (1, 0))
                        dve.tensor_scalar(kk[:, n, :], kk[:, n, :], om, None, ALU.mult)
                        f = dve.tensor_scalar(sg[:, n, :], sg[:, n, :], om, lb, ALU.mult, ALU.add)
                    f.then_inc(*S.dve.one)
                    dve.wait_ge(S.act.sem, S.act.at(1))
                    for n in range(2):
                        s = dve.tensor_tensor_scan(b_[:, n, :], M.resets[:, :], sg[:, n, :], 0.0, ALU.mult, ALU.add)
                    chain(dve, S.dve, s)
                    for n in range(2):
                        bn = b_[:, n, :].rearrange("p (c t) -> p c t", t=CHUNK)
                        o = dve.tensor_tensor(ke[:, n, :].rearrange("p (c t) -> p c t", t=CHUNK),
                                              bn[:, :, CHUNK - 1:CHUNK].to_broadcast([P, nch, CHUNK]), bn,
                                              ALU.subtract)
                    o.then_inc(*S.dve.one)
                    dve.wait_ge(S.act.sem, S.act.at(2))
                    dve.tensor_tensor(qs[:, :, :], qs[:, :, :], eb[:, :, :], ALU.mult)
                    dve.wait_ge(S.act.sem, S.act.at(3))
                    dve.tensor_tensor(nb_[:, :, :], nb_[:, :, :], kk[:, :, :], ALU.mult)
                    dve.wait_ge(S.act.sem, S.act.at(4))
                    dve.tensor_tensor(ke[:, :, :], ke[:, :, :], kk[:, :, :], ALU.mult)
                    dve.memset(st[:, :, 0, :], 0.0)

                @block.scalar
                def _(act):
                    act.wait_ge(S.dve.sem, S.dve.at(1))
                    act.activation(sg[:, :, :], sg[:, :, :], ACT.Ln).then_inc(*S.act.one)
                    act.wait_ge(S.dve.sem, S.dve.at(2))
                    act.activation(eb[:, :, :], b_[:, :, :], ACT.Exp).then_inc(*S.act.one)
                    act.activation(nb_[:, :, :], b_[:, :, :], ACT.Exp, scale=-1.0).then_inc(*S.act.one)
                    act.wait_ge(S.dve.sem, S.dve.at(3))
                    act.activation(ke[:, :, :], ke[:, :, :], ACT.Exp).then_inc(*S.act.one)

            def additions(g):
                return 4 if g < 4 else 0

            with S.stage(nc) as block:
                @block.tensor
                def _(pe):
                    for n in range(2):
                        for t in range(4):
                            tr = pe.transpose(M.ps[:, n, t * P:(t + 1) * P], ke[:, n, t * P:(t + 1) * P], M.ident[:, :])
                        tr.then_inc(*S.pe.one)
                        for t in range(4):
                            c = slice(t * P, (t + 1) * P)
                            mm = pe.matmul(M.ps[:, 2 + n, c], nb_[:, n, c], qs[:, n, c], start=True, stop=True)
                        mm.then_inc(*S.scores.one)
                    for g in range(8):
                        t, n = divmod(g, 2)
                        pe.wait_ge(S.by_act.sem, S.by_act.at(n + 1))
                        if g == 4:
                            pe.wait_ge(S.masked.sem, S.masked.at(2))
                        for j in range(4):
                            r = slice(j * CHUNK, (j + 1) * CHUNK)
                            mm = pe.matmul(M.ps[:, additions(g) + j, g % 4 * P:(g % 4 + 1) * P], ket[r, n, t, :],
                                           v[r, t, n * P:(n + 1) * P], start=True, stop=True)
                        mm.then_inc(*S.acc.one)
                    pe.wait_ge(S.mixed.sem, S.mixed.at(2 * (nch - 1)))
                    pe.wait_ge(S.masked.sem, S.masked.at(2))
                    for n in range(2):
                        for t in range(4):
                            c = slice(t * P, (t + 1) * P)
                            pe.matmul(M.ps[:, n, c], v[:, t, n * P:(n + 1) * P], at[:, n, c], start=t == 0, stop=False,
                                      skip_group_check=True)
                        for m in range(1, nch):
                            c = slice(m * CHUNK, (m + 1) * CHUNK)
                            mm = pe.matmul(M.ps[:, n, c], st[:, n, m, :], qs[:, n, c], start=False, stop=m == nch - 1,
                                           skip_group_check=True)
                        mm.then_inc(*S.probs.one)
                    for n in range(2):
                        pe.wait_ge(S.sq_act.sem, S.sq_act.at(n + 1))
                        pe.matmul(M.ps[:, 2 + n, :], M.ones[:, :], nb_[:, n, :], start=True, stop=True)\
                            .then_inc(*S.summed.one)

                @block.scalar
                def _(act):
                    for n in range(2):
                        act.wait_ge(S.pe.sem, S.pe.at(n + 1))
                        act.activation(ket[:, n, :, :].rearrange("p t k -> p (t k)"), M.ps[:, n, :], ACT.Copy)\
                            .then_inc(*S.by_act.one)
                    for n in range(2):
                        act.wait_ge(S.probs.sem, S.probs.at(n + 1))
                        act.activation(nb_[:, n, :], M.ps[:, n, :], ACT.Square).then_inc(*S.sq_act.one)
                    for n in range(2):
                        act.wait_ge(S.summed.sem, S.summed.at(n + 1))
                        act.activation(ke[:, n, :], M.ps[:, 2 + n, :], ACT.Ln, scale=1.0 / P, bias=M.eps[:, 0:1])\
                            .then_inc(*S.act.one)
                        act.wait_ge(S.act.sem, S.act.at(n + 1))
                        act.activation(ke[:, n, :], ke[:, n, :], ACT.Exp, scale=-0.5).then_inc(*S.rstd.one)

                @block.vector
                def _(dve):
                    for n in range(2):
                        dve.wait_ge(S.scores.sem, S.scores.at(n + 1))
                        dve.scalar_tensor_tensor(at[:, n, :].rearrange("p (t c) -> p t c", t=4),
                                                 M.ps[:, 2 + n, :].rearrange("p (t c) -> p t c", t=4), 3.0e38,
                                                 M.causal[:, :].unsqueeze(1).to_broadcast([P, 4, P]),
                                                 ALU.min, ALU.mult).then_inc(*S.masked.one)
                    for m in range(nch - 1):
                        for n in range(2):
                            g = m // 4 * 2 + n
                            if m % 8 == 0 and n == 0:
                                dve.wait_ge(S.acc.sem, S.acc.at(g + 4))
                            if m:
                                dve.wait_ge(S.mixed.sem, S.mixed.at(2 * m - 1 + n))
                            dve.scalar_tensor_tensor(
                                st[:, n, m + 1, :], st[:, n, m, :],
                                eb[:, n, m * CHUNK + CHUNK - 1:m * CHUNK + CHUNK],
                                M.ps[:, additions(g) + m % 4, g % 4 * P:(g % 4 + 1) * P], ALU.mult, ALU.add)\
                                .then_inc(*S.mixed.one)
                    for n in range(2):
                        dve.wait_ge(S.rstd.sem, S.rstd.at(n + 1))
                        chain(dve, S.dve, dve.tensor_tensor(ke[:, n, :], ke[:, n, :], M.ps[:, n, :], ALU.mult))
                        dve.scalar_tensor_tensor(y[:, bass.ds(i * 2 + n, 1), :].rearrange("p a t -> p (a t)"),
                                                 ke[:, n, :], M.hgain[:, bass.ds(i * 2 + n, 1)], gs[:, n, :],
                                                 ALU.mult, ALU.mult).then_inc(*S.by_dve.one)


def dilated(nc, S, M, io):
    w = io["attn_w_in_2"][0]
    h = lambda k, a, b: M.h[:, k, a:b]
    with ExitStack() as ctx:
        def sb(name, shape):
            return ctx.enter_context(nc.sbuf_tensor("d_" + name, shape, F32))

        qk = sb("qk", [P, 12, LX])
        v = sb("v", [P, GROUPS2, 4, UNIT])
        swp = sb("swp", [ROT, 12, LX])
        masks = sb("masks", [P, 4 * LX + 2 * P])
        flat = M.ring[:, :, :].rearrange("p a b -> p (a b)")
        p_t = flat[:, 0:6 * LX].rearrange("p (k q) -> p k q", k=6)
        p = flat[:, 6 * LX:6 * LX + 2 * T].rearrange("p (a b) -> p a b", a=2)
        scale = P ** -0.5
        load(nc, S, [(masks[:, :], io["attn_masks"])])
        with S.loop(nc, H2 // 2, **LOOPS["dilated"]) as i:
            units = []
            for g in range(GROUPS2):
                for s in range(2):
                    def keep(e, acc, b, gr, g=g, s=s):
                        dst = qk[:, 4 * g + 2 * s + b, :]
                        if s == 0:
                            return e.activation(dst, acc, ACT.Copy, scale=scale)
                        return e.tensor_copy(dst, acc)
                    c0 = (3 * g + s) * D
                    units.append((tiles(w, 0, D, c0 + i * UNIT, c0 + (i + 1) * UNIT), placed(KD, UNIT),
                                  feature_jobs(h, KD, [(0, 0), (1, P)], [X_COLS], "dve" if s else "act", keep)))
                js = []
                for t in range(4):
                    def lhs(w_, k, t=t, g=g):
                        if g == 0:
                            return M.h[:, k, t * P:(t + 1) * P]
                        return M.h[:, k, 0:LX].rearrange("p (m r) -> p m r", r=4)[:, :, t]
                    js.append(Job(lhs, lambda w_, k: w_[:, k, :], KD, P, UNIT, "dve",
                                  lambda e, acc, t=t, g=g: e.tensor_copy(v[:, g, t, :], acc)))
                c0 = (3 * g + 2) * D
                units.append((tiles(w, 0, D, c0 + i * UNIT, c0 + (i + 1) * UNIT), placed(KD, UNIT), js))
            project(nc, S, M, units)

            with S.stage(nc) as block:
                @block.sync
                def _(sp):
                    half = ROT // 2
                    sp.dma_start(swp[0:half, :, :], qk[half:ROT, :, :]).then_inc(*S.landed.one)
                    sp.dma_start(swp[half:ROT, :, :], qk[0:half, :, :]).then_inc(*S.landed.one)

                @block.vector
                def _(dve):
                    dve.wait_ge(S.landed.sem, S.landed.at(2))
                    cos = M.rot[:, 0:1, :].to_broadcast([ROT, 12, LX])
                    sin = M.rot[:, 1:2, :].to_broadcast([ROT, 12, LX])
                    dve.tensor_tensor(swp[:, :, :], swp[:, :, :], sin, ALU.mult)
                    chain(dve, S.dve, dve.tensor_tensor(qk[0:ROT, :, :], qk[0:ROT, :, :], cos, ALU.mult))
                    dve.tensor_tensor(qk[0:ROT, :, :], qk[0:ROT, :, :], swp[:, :, :], ALU.add)

            def every4(ap, r):
                return ap.rearrange("p (m r) -> p m r", r=4)[:, :, r]

            def score(pe, hd, r, acc):
                pe.matmul(acc[:, 0:LX], every4(qk[:, hd, :], r), qk[:, 2 + hd, :], start=True, stop=True)
                for g in (1, 2):
                    mm = pe.matmul(acc[:, LX + (g - 1) * P:LX + g * P], every4(qk[:, 4 * g + hd, :], r),
                                   every4(qk[:, 4 * g + 2 + hd, :], r), start=True, stop=True)
                return mm

            def mask(r):
                return [(0, LX, masks[:, r * LX:(r + 1) * LX]), (LX, T, masks[:, 4 * LX:4 * LX + 2 * P])]

            def mix(pe, hd, acc):
                c = slice(hd * P, (hd + 1) * P)
                for j in range(4):
                    pe.matmul(acc, v[:, 0, j, c], p_t[:, j, :], start=j == 0, stop=False, skip_group_check=True)
                for g in (1, 2):
                    for r in range(4):
                        mm = pe.matmul(acc[:, r * P:(r + 1) * P], v[:, g, r, c], p_t[:, 3 + g, r * P:(r + 1) * P],
                                       start=False, stop=g == 2, skip_group_check=True)
                return mm

            def store(dve, hd, acc):
                dst = M.y[:, bass.ds(i * 2 + hd, 1), :].rearrange("p a (m r) -> p r (a m)", r=4)
                return dve.tensor_copy(dst, acc.rearrange("p (r m) -> p r m", r=4))

            attention(nc, S, M, 2, 4, 6, score, mask, mix, LX, store, p, p_t)


LOOPS = {
    "recurrence": dict(weights=[1] * 4, acc=18, by_act=8, by_dve=6, dve=5, act=6, pe=2, sq_act=2, summed=2, rstd=2,
                       scores=2, masked=2, probs=2, mixed=30),
    "dilated": dict(weights=[3, 2, 2, 2], acc=24, by_act=6, by_dve=18, landed=2, dve=1, scores=8, masked=8, maxed=8,
                    exped=8, recip=8, probs=8, turned=8, probs_t=8, mixed=2, stored=2),
}


def second_layer(nc, S, M, io, l):
    x = lambda k, a, b: M.x[:, k, a:b]
    h = lambda k, a, b: M.h[:, k, a:b]
    y_ = lambda k, a, b: M.y[:, k, a:b]
    gx = [X_COLS]

    def keep(e, acc, b, g):
        return e.tensor_copy(M.y[:, b, :], acc)

    def post(n):
        norm(nc, S, M, y_, KD, D, gx, y_, lambda k, a: M.gain2[:, 4 * l + n, k:k + 1])
        with S.stage(nc) as block:
            @block.vector
            def _(dve):
                dve.tensor_tensor(M.x[:, :, 0:LX], M.x[:, :, 0:LX], M.y[:, :, :], ALU.add)

    norm(nc, S, M, x, KD, D, gx, h, lambda k, a: M.gain2[:, 4 * l, k:k + 1], lambda k, a: M.mod(2 + l, 0, k, 0))
    (recurrence if l == 0 else dilated)(nc, S, M, io)
    w_out = io["hgrn_w_out_2" if l == 0 else "attn_w_out_2"][0]
    project(nc, S, M, [(tiles(w_out, 0, D, c * UNIT, (c + 1) * UNIT), placed(KD, UNIT),
                        feature_jobs(y_, KD, [(2 * c, 0), (2 * c + 1, P)], gx, "dve",
                                     lambda e, acc, b, g: e.tensor_copy(M.h[:, b, 0:LX], acc)))
                       for c in range(4)])
    norm(nc, S, M, h, KD, D, gx, y_, lambda k, a: M.gain2[:, 4 * l + 1, k:k + 1])
    with S.stage(nc) as block:
        @block.vector
        def _(dve):
            dve.tensor_tensor(M.x[:, :, 0:LX], M.x[:, :, 0:LX], M.y[:, :, :], ALU.add)

    norm(nc, S, M, x, KD, D, gx, h, lambda k, a: M.gain2[:, 4 * l + 2, k:k + 1], lambda k, a: M.mod(2 + l, 3, k, 0))
    w_up, w_down = io["ffn_w_in_2"][l], io["ffn_w_out_2"][l]
    with ExitStack() as ctx:
        hid = ctx.enter_context(nc.sbuf_tensor(f"ffn_hidden{l}", [P, D_FF2 // P, LX], F32))
        gate = ctx.enter_context(nc.sbuf_tensor(f"ffn_gate{l}", [P, 2, LX], F32))

        def pair(g, base, slot):
            def silu(e, acc, b, _):
                return e.activation(gate[:, b, :], acc, ACT.Silu)

            def mul(e, acc, b, _):
                dst = hid[:, bass.ds(g * 2 + b, 1), :].rearrange("p a t -> p (a t)")
                return e.tensor_tensor(dst, gate[:, b, :], acc, ALU.mult)

            c0 = g * UNIT
            js = feature_jobs(h, KD, [(0, 0), (1, P)], gx, "act", silu)
            ju = feature_jobs(h, KD, [(0, 0), (1, P)], gx, "dve", mul)
            for b in range(2):
                ju[b].after = (base + b,)
                if base:
                    js[b].after = (base - 2 + b,)
            return [(tiles(w_up, 0, D, c0, c0 + UNIT), placed(KD, UNIT), js),
                    (tiles(w_up, 0, D, c0 + D_FF2, c0 + D_FF2 + UNIT), placed(KD, UNIT), ju)]

        with S.loop(nc, 5, weights=[1] * 4, acc=8, by_act=4, by_dve=4) as i:
            project(nc, S, M, pair(i * 2, 0, 0) + pair(i * 2 + 1, 4, 2))
        project(nc, S, M, pair(10, 0, 0))

        kf = D_FF2 // P
        with S.loop(nc, 2, weights=[1] * 4, acc=4, by_dve=4) as i:
            def keep_y(e, acc, b, g):
                return e.tensor_copy(M.y[:, bass.ds(i * 4 + b, 1), :].rearrange("p a t -> p (a t)"), acc)
            project(nc, S, M, [(tiles(w_down, 0, D_FF2, i * 4 * P + c * P, i * 4 * P + (c + 1) * P, P), placed(kf, P),
                                feature_jobs(lambda k, a, b: hid[:, k, :], kf, [(c, 0)], gx, "dve", keep_y))
                               for c in range(4)])
    post(3)



VECTORS = [
    ("c", 8), ("c_ctx", 8), ("c_2", 8), ("b_mod", 96), ("ada_b_2", 96), ("norm1_g", 16), ("norm2_g", 16),
    ("q_norm_g", 6), ("kv_norm_g", 4), ("hy_conv_w", 36), ("hy_conv_b", 12), ("hy_d", 4), ("final_norm_g", 8),
    ("norm_g_2", 64), ("hgrn_lower_bounds_2", 8), ("hgrn_norm_g_2", 8), ("hy_b1", 2), ("hy_freq", 2), ("hy_b2", 2),
]
FIRST_ROW = dict(zip((n for n, _ in VECTORS), np.cumsum([0] + [k for _, k in VECTORS])[:-1].tolist()))
N_ROWS = sum(k for _, k in VECTORS)
ROWS_OF = dict(VECTORS)


class Memory:
    def __init__(self, nc, ctx):
        def sb(name, shape, dt=F32):
            return ctx.enter_context(nc.sbuf_tensor(name, shape, dt))

        self.ps = ctx.enter_context(nc.psum_tensor("ps", [P, BANKS, 512], F32))
        self.ring = sb("ring", [P, RING, SLOT])
        self.x = sb("x_res", [P, KD, T])
        self.h = sb("h", [P, KD, T])
        self.sq = sb("sq", [P, 2, T])
        self.tmp = self.sq
        self.rs = sb("rs", [P, T])
        self.vec = sb("vec", [P, 4, P])
        self.mods = sb("mods", [P, 2 * DEPTH, 48, 2])
        self.gain = sb("gain", [P, 4, 2, KD])
        self.gain2 = sb("gain2", [P, 8, KD])
        self.lower = sb("lower", [P, 2, KD])
        self.hgain = sb("hgain", [P, KD])
        self.ident = sb("ident", [P, P])
        self.ones = sb("ones", [P, P])
        self.eps = sb("eps", [P, 1])
        self.nmax, self.esum, self.rsum = sb("nmax", [P, 4]), sb("esum", [P, 4]), sb("rsum", [P, 4])

    def col(self, name, l=0, k=0, n=1):
        c = FIRST_ROW[name] + l * (ROWS_OF[name] // 2) + k if ROWS_OF[name] and l else FIRST_ROW[name] + k
        return self.vec[:, :, :].rearrange("p a b -> p (a b)")[:, c:c + n]

    def mod(self, s, m, k, side):
        return self.mods[:, s, m * KD + k, side:side + 1]


def vectors(nc, S, M, io):
    with nc.sbuf_tensor("rows", [P, 4, P], F32) as rows:
        with S.stage(nc) as block:
            @block.gpsimd
            def _(pool):
                pool.memset(rows[:, :, :], 0.0)
                pool.memset(M.ones[:, :], 1.0)
                pool.memset(M.eps[:, :], EPS)
                pool.memset(M.nmax[:, :], 0.0)
        pairs = [(M.ident[:, :], io["ident"])]
        for name, n in VECTORS:
            src = io[name]
            if len(src.shape) > 1:
                src = src.rearrange({2: "a b -> (a b)", 3: "a b c -> (a b c)"}[len(src.shape)])
            wd = 64 if name in ("hy_b1", "hy_freq", "hy_b2") else P
            src = src.rearrange("(r w) -> r w", w=wd)
            r = 0
            while r < n:
                row = FIRST_ROW[name] + r
                m = min(n - r, P - row % P)
                pairs.append((rows[row % P:row % P + m, row // P, 0:wd], src[r:r + m, :]))
                r += m
        load(nc, S, pairs)
        with S.stage(nc) as block:
            @block.tensor
            def _(pe):
                for t in range(4):
                    tr = pe.transpose(M.ps[:, 0, t * P:(t + 1) * P], rows[:, t, :], M.ident[:, :])
                tr.then_inc(*S.pe.one)

            @block.scalar
            def _(act):
                act.wait_ge(S.pe.sem, S.pe.at(1))
                act.activation(M.vec[:, :, :].rearrange("p a b -> p (a b)"), M.ps[:, 0, :], ACT.Copy)\
                    .then_inc(*S.act.one)


def modulations(nc, S, M, io):
    with ExitStack() as ctx:
        cond = ctx.enter_context(nc.sbuf_tensor("cond", [P, 3, KD], F32))
        with S.stage(nc) as block:
            @block.scalar
            def _(act):
                act.activation(cond[:, :, :].rearrange("p a b -> p (a b)"), M.col("c", n=24), ACT.Silu)
        for s in range(2 * DEPTH):
            w = io["w_mod" if s < 2 else "ada_w_2"][s % 2]
            first, n = (0, 2) if s < 2 else (2, 1)
            c_b = FIRST_ROW["b_mod" if s < 2 else "ada_b_2"] + 48 * (s % 2)
            with S.loop(nc, 6, weights=[1] * 4, pe=1, by_dve=1) as i:
                with S.stage(nc) as block:
                    @block.sync
                    def _(sp):
                        for u in range(4):
                            c0 = i * (4 * UNIT) + u * UNIT
                            sp.dma_start(placed(KD, UNIT)(M.ring[:, u, :]), tiles(w, 0, D, c0, c0 + UNIT))\
                                .then_inc(*S.weights[u].one)

                    @block.tensor
                    def _(pe):
                        for u in range(4):
                            pe.wait_ge(S.weights[u].sem, S.weights[u].at(1))
                            wt = placed(KD, UNIT)(M.ring[:, u, :])
                            for b in range(2):
                                o = (2 * u + b) * n
                                for k in range(KD):
                                    mm = pe.matmul(M.ps[:, 0, o:o + n], wt[:, k, b * P:(b + 1) * P],
                                                   cond[:, first:first + n, k], start=k == 0, stop=k == KD - 1)
                        mm.then_inc(*S.pe.one)

                    @block.vector
                    def _(dve):
                        dve.wait_ge(S.pe.sem, S.pe.at(1))
                        vec = M.vec[:, :, :].rearrange("p a b -> p (a b)")
                        bias = vec[:, bass.ds(i * 8 + c_b, 8)]
                        dve.tensor_tensor(M.mods[:, s, bass.ds(i * 8, 8), 0:n],
                                          M.ps[:, 0, 0:8 * n].rearrange("p (b n) -> p b n", n=n),
                                          bias.unsqueeze(2).to_broadcast([P, 8, n]), ALU.add).then_inc(*S.by_dve.one)


def gains(nc, S, M):
    vec = M.vec[:, :, :].rearrange("p a b -> p (a b)")
    with nc.sbuf_tensor("lb", [P, 4, KD], F32) as lb, S.stage(nc) as block:
        @block.vector
        def _(dve):
            def gain(dst, s, m, side, g):
                dve.scalar_tensor_tensor(dst, M.mods[:, s, m * KD:(m + 1) * KD, side], 1.0, g, ALU.add, ALU.mult)

            for l in range(DEPTH):
                for j, name in enumerate(("norm1_g", "norm2_g")):
                    for side in range(2):
                        gain(M.gain[:, 2 * l + j, side, :], l, 1 + 3 * j, side, M.col(name, l, n=KD))
                for j, m in enumerate((1, 2, 4, 5)):
                    gain(M.gain2[:, 4 * l + j, :], 2 + l, m, 0, M.col("norm_g_2", l, j * KD, n=KD))
            dve.tensor_copy(M.hgain[:, :], M.col("hgrn_norm_g_2", n=KD))
            b = M.col("hgrn_lower_bounds_2", n=KD)
            chain(dve, S.dve, dve.tensor_tensor(lb[:, 0, :], b, b, ALU.subtract))
            dve.wait_ge(S.act.sem, S.act.at(1))
            chain(dve, S.dve, dve.reciprocal(lb[:, 2, :], lb[:, 1, :]))
            chain(dve, S.dve, dve.tensor_tensor(lb[:, 3, :], lb[:, 1, :], lb[:, 2, :], ALU.mult))
            chain(dve, S.dve, dve.tensor_tensor(M.lower[:, 0, :], lb[:, 3, :], lb[:, 3, :], ALU.subtract))
            dve.tensor_scalar(M.lower[:, 1, :], M.lower[:, 0, :], -1.0, 1.0, ALU.mult, ALU.add)

        @block.scalar
        def _(act):
            act.wait_ge(S.dve.sem, S.dve.at(1))
            act.activation(lb[:, 1, :], lb[:, 0, :], ACT.Exp).then_inc(*S.act.one)


def rotary_tables(nc, S, M, io):
    with ExitStack() as ctx:
        pos = ctx.enter_context(nc.sbuf_tensor("pos", [ROT, LX], I32))
        ang = ctx.enter_context(nc.sbuf_tensor("ang", [ROT, 4, LX], F32))
        par = ctx.enter_context(nc.sbuf_tensor("par", [ROT, 2], F32))
        load(nc, S, [(pos[:, :], io["positions_2"].to_broadcast([ROT, LX])), (par[:, :], io["rot_params"])])
        with S.stage(nc) as block:
            @block.vector
            def _(dve):
                chain(dve, S.dve, dve.tensor_copy(ang[:, 0, :], pos[:, :]))
                chain(dve, S.dve, dve.tensor_scalar(ang[:, 0, :], ang[:, 0, :], par[:, 0:1], None, ALU.mult))
                reduce_angle(dve, S, ang[:, 0, :], ang[:, 1, :])
                chain(dve, S.dve, dve.tensor_scalar(ang[:, 2, :], ang[:, 0, :], math.pi / 2, None, ALU.add))
                chain(dve, S.dve, dve.tensor_scalar(ang[:, 1, :], ang[:, 2, :], math.pi, TWO_PI, ALU.is_gt, ALU.mult))
                chain(dve, S.dve, dve.tensor_tensor(ang[:, 2, :], ang[:, 2, :], ang[:, 1, :], ALU.subtract))
                dve.tensor_scalar(ang[:, 2, :], ang[:, 2, :], SIN_MAX, -SIN_MAX, ALU.min, ALU.max)\
                    .then_inc(*S.by_dve.one)
                dve.wait_ge(S.act.sem, S.act.at(1))
                dve.tensor_scalar(M.rot[:, 1, :], ang[:, 3, :], par[:, 1:2], None, ALU.mult)

            @block.scalar
            def _(act):
                act.wait_ge(S.by_dve.sem, S.by_dve.at(1))
                act.activation(M.rot[:, 0, :], ang[:, 2, :], ACT.Sin)
                act.activation(ang[:, 3, :], ang[:, 0, :], ACT.Sin).then_inc(*S.act.one)


def enter(nc, S, M, io):
    with nc.sbuf_tensor("tok_in", [P, 6, D], F32) as tok:
        load(nc, S, [(tok[:, 0:4, :], io["x"][0].rearrange("(t p) d -> p t d", p=P)),
                     (tok[:, 4:6, :], io["ctx"][0].rearrange("(t p) d -> p t d", p=P))])
        with S.stage(nc) as block:
            @block.tensor
            def _(pe):
                for t in range(T // P):
                    for half in range(2):
                        n = 2 * t + half
                        if n >= BANKS:
                            pe.wait_ge(S.by_act.sem, S.by_act.at(n - BANKS + 1))
                        for k in range(4):
                            c = (4 * half + k) * P
                            tr = pe.transpose(M.ps[:, n % BANKS, k * P:(k + 1) * P], tok[:, t, c:c + P], M.ident[:, :])
                        tr.then_inc(*S.pe.one)

            @block.scalar
            def _(act):
                for n in range(2 * T // P):
                    t, half = divmod(n, 2)
                    act.wait_ge(S.pe.sem, S.pe.at(n + 1))
                    act.activation(M.x[:, 4 * half:4 * half + 4, t * P:(t + 1) * P],
                                   M.ps[:, n % BANKS, :].rearrange("p (k t) -> p k t", k=4), ACT.Copy)\
                        .then_inc(*S.by_act.one)


def leave(nc, S, M, io):
    dst = io["out"][0].rearrange("(t p) d -> t p d", p=P)
    with nc.sbuf_tensor("tok_out", [P, 4, D], F32) as tok, S.stage(nc) as block:
        @block.tensor
        def _(pe):
            for n in range(8):
                t, half = divmod(n, 2)
                for k in range(4):
                    tr = pe.transpose(M.ps[:, n, k * P:(k + 1) * P], M.x[:, 4 * half + k, t * P:(t + 1) * P],
                                      M.ident[:, :])
                tr.then_inc(*S.pe.one)

        @block.scalar
        def _(act):
            for n in range(8):
                t, half = divmod(n, 2)
                act.wait_ge(S.pe.sem, S.pe.at(n + 1))
                act.activation(tok[:, t, half * 512:(half + 1) * 512], M.ps[:, n, :], ACT.Copy)\
                    .then_inc(*S.by_act.one)

        @block.sync
        def _(sp):
            for t in range(4):
                sp.wait_ge(S.by_act.sem, S.by_act.at(2 * t + 2))
                sp.dma_start(dst[t], tok[:, t, :]).then_inc(*S.out.one)
            sp.wait_ge(S.out.sem, S.out.at(4))


def program(nc, io):
    S = Signals(nc)
    with ExitStack() as ctx:
        M = Memory(nc, ctx)
        vectors(nc, S, M, io)
        modulations(nc, S, M, io)
        gains(nc, S, M)
        enter(nc, S, M, io)
        for l in range(DEPTH):
            first_layer(nc, S, M, io, l)
        x = lambda k, a, b: M.x[:, k, a:b]
        norm(nc, S, M, x, KD, D, [X_COLS], x, lambda k, a: M.col("final_norm_g", k=k))
        M.y = ctx.enter_context(nc.sbuf_tensor("y", [P, KD, LX], F32))
        M.rot = ctx.enter_context(nc.sbuf_tensor("rot", [ROT, 2, LX], F32))
        M.resets = ctx.enter_context(nc.sbuf_tensor("resets", [P, LX], F32))
        M.causal = ctx.enter_context(nc.sbuf_tensor("causal", [P, P], F32))
        load(nc, S, [(M.resets[:, :], io["chunk_resets"]), (M.causal[:, :], io["chunk_causal"])])
        rotary_tables(nc, S, M, io)
        for l in range(DEPTH):
            second_layer(nc, S, M, io, l)
        leave(nc, S, M, io)


def tables():
    f = np.float64
    out = {"ident": np.eye(P)}

    def by_tile(a):
        return a.reshape(a.shape[0] // P, P, *a.shape[1:]).swapaxes(0, 1)

    inv = 10000.0 ** (-np.arange(0, 16, 2, dtype=np.float32) / np.float32(16))
    t = np.arange(LX)
    rope = np.zeros((P, 2, LX))
    swap = np.zeros((P, P))
    for axis, pos in enumerate((t // 64, t % 64)):
        ang = (pos.astype(np.float32)[None] * inv.astype(np.float32)[:, None]).astype(np.float32).astype(f)
        for half in range(2):
            r = NOPE + 16 * axis + 8 * half
            rope[r:r + 8, 0] = np.cos(ang)
            rope[r:r + 8, 1] = np.sin(ang) * (1 if half else -1)
            other = NOPE + 16 * axis + 8 * (1 - half)
            for j in range(8):
                swap[other + j, r + j] = 1.0
    out["rope_tables"], out["rope_swap"] = rope, swap

    w = np.arange(64)
    a = 2 * np.pi * np.outer(w, w) / 64
    chan = np.zeros((P, 2, P))
    for g in range(2):
        s = slice(64 * g, 64 * g + 64)
        chan[s, 0, s], chan[s, 1, s] = np.cos(a), np.sin(a)
    out["fnet_channels"] = chan.reshape(P, 2 * P)
    deltas = np.abs(np.linspace(math.log(1e-2) / 1.5, math.log(1e-2) / 0.3, HY))
    for n in (LX, LC):
        i = np.arange(n)
        a = 2 * np.pi * (np.outer(i, i) % n) / n
        out[f"fnet_tokens_{n}"] = by_tile(np.stack([np.cos(a), -np.sin(a)], 1)) / math.sqrt(64 * n)
        a = 2 * np.pi * np.outer(i, i + 0.5) / (2 * n)
        out[f"hy_tk_{n}"] = by_tile(np.stack([np.cos(a), np.sin(a)], 1))
        a = 2 * np.pi * np.outer(i + 0.5, i + 0.5) / (2 * n)
        out[f"hy_ta_{n}"] = by_tile(np.stack([np.cos(a), np.sin(a)], 1))
        tt = np.linspace(0.0, 1.0, n)[:, None]
        bands = (EMB - 1) // 2
        fr = np.linspace(1e-4, bands - 1, bands).astype(np.float32)
        ang = (np.float32(2.0 * math.pi) * np.arange(n, dtype=np.float32)[:, None] / np.float32(n)) * fr
        ang = ang.astype(np.float32).astype(f)
        out[f"hy_emb_{n}"] = np.concatenate([tt, np.cos(ang), -np.sin(ang)], -1).T
        dec = np.exp(-tt * deltas)
        both = np.concatenate([dec, dec], 1)
        both[0, HY:] = 0.0
        out[f"hy_decay_{n}"] = by_tile(both)

    out["chunk_resets"] = np.broadcast_to((t % CHUNK != 0).astype(f), (P, LX))
    s, c = np.arange(P)[:, None], np.arange(P)[None]
    out["chunk_causal"] = ((s // CHUNK == c // CHUNK) & (s <= c)).astype(f)
    inv2 = 500000.0 ** (-np.arange(0, ROT, 2, dtype=np.float32) / np.float32(ROT))
    sign = np.repeat([-1.0, 1.0], ROT // 2)
    out["rot_params"] = np.stack([np.tile(inv2, 2), sign], 1)
    masks = np.zeros((P, 4 * LX + 2 * P))
    m = np.arange(P)
    for r in range(4):
        dist = (r + 4 * m)[:, None] - t[None]
        masks[:, r * LX:(r + 1) * LX] = np.where((dist >= 0) & (dist <= 128), 0.0, -1e30)
    causal = m[:, None] >= m[None]
    masks[:, 4 * LX:4 * LX + P] = np.where(causal, 0.0, -1e30)
    masks[:, 4 * LX + P:] = np.where(causal & (m[:, None] % 4 == m[None] % 4), 0.0, -1e30)
    out["attn_masks"] = masks
    return {k: np.ascontiguousarray(v.astype(np.float32)) for k, v in out.items()}


def kernel(**inputs):
    import concourse.bacc as bacc
    from concourse.bass_utils import run_bass_kernel_spmd

    nc = bacc.Bacc("TRN2", target_bir_lowering=False, num_devices=1)
    arrays, io = {}, {}
    for name, a in {**inputs, **tables()}.items():
        a = np.ascontiguousarray(a)
        arrays[f"in_{name}"] = a
        io[name] = nc.dram_tensor(f"in_{name}", a.shape, mybir.dt.from_np(a.dtype), kind="ExternalInput").ap()
    io["out"] = nc.dram_tensor("out", (1, LX, D), F32, kind="ExternalOutput").ap()
    program(nc, io)
    r = run_bass_kernel_spmd(nc, [arrays], core_ids=[0])
    return r.results[0]["out"]
```

```python
import math
from contextlib import ExitStack, contextmanager

import numpy as np

import concourse.bass as bass
from concourse import mybir

F32 = mybir.dt.float32
F32R = mybir.dt.float32r
I32 = mybir.dt.int32
ALU = mybir.AluOpType
ACT = mybir.ActivationFunctionType
AX = mybir.AxisListType.X

P = 128
D = 1024
KD = D // P
LX, LC = 512, 256
T = LX + LC
X_COLS, C_COLS = (0, LX), (LX, T)
DEPTH = 2
EPS = 1e-6

HEADS, NOPE, ROPE, VDIM = 8, 64, 32, 64
QK = NOPE + ROPE
Q_LORA, KV_LORA = 384, 256
OFF_KV = Q_LORA
OFF_KR = OFF_KV + KV_LORA
OFF_F = OFF_KR + ROPE
OFF_H = OFF_F + 256
IN_W = OFF_H + 768
HY = 256
D_FF = 4 * D
EMB, ORDER = 33, 64

H2 = 8
CHUNK = 32
D_FF2 = 2816
ROT = 32
GROUPS2 = 3

UNIT = 256
RING = 2
SLOT = KD * UNIT
BANKS = 8

TWO_PI = 2.0 * math.pi
PI1 = 6.28125
PI2 = float(np.float32(round((TWO_PI - PI1) * 2 ** 19) / 2 ** 19))
PI3 = TWO_PI - PI1 - PI2
ROUND = 1.5 * 2.0 ** 23
SIN_MAX = 3.1415925


class Signal:

    def __init__(self, nc, name, step=1):
        self.sem = nc.alloc_semaphore(name)
        self.step, self.start, self.sent = step, 0, 0
        self.turn = None

    @property
    def one(self):
        self.sent += 1
        return self.sem, self.step

    def at(self, n):
        value = (self.start + n) * self.step
        return value if self.turn is None else value + self.turn[0] * (self.turn[1] * self.step)

    @property
    def up(self):
        return self.sem, self.step

    def settle(self):
        self.start += self.sent
        self.sent = 0


class Signals:
    def __init__(self, nc):
        self.named = {}

        def signal(key, name, step=1):
            self.named[key] = Signal(nc, name, step)
            return self.named[key]

        self.weights = [Signal(nc, f"weights_landed_{s}", 16) for s in range(RING)]
        self.w_hi = signal("w_hi", "weights_high_parts")
        self.w_lo = signal("w_lo", "weights_low_parts")
        self.value = signal("value", "hidden_value_ready")
        self.hi = signal("hi", "hidden_high_part")
        self.lo = signal("lo", "hidden_low_part")
        self.acc = signal("acc", "accumulated")
        self.by_act = signal("by_act", "evacuated_by_act")
        self.by_dve = signal("by_dve", "evacuated_by_dve")
        self.landed = signal("landed", "tables_landed", 16)
        self.dve = signal("dve", "dve_step")
        self.act = signal("act", "act_step")
        self.pe = signal("pe", "pe_step")
        self.sq_act = signal("sq_act", "squares_by_act")
        self.sq_dve = signal("sq_dve", "squares_by_dve")
        self.summed = signal("summed", "squares_summed")
        self.rstd = signal("rstd", "rstd_ready")
        self.normed = signal("normed", "normed")
        self.scaled = signal("scaled", "scaled")
        self.scores = signal("scores", "scores_ready")
        self.masked = signal("masked", "scores_masked")
        self.maxed = signal("maxed", "max_ready")
        self.exped = signal("exped", "exp_ready")
        self.recip = signal("recip", "reciprocal_ready")
        self.probs = signal("probs", "probs_ready")
        self.turned = signal("turned", "probs_transposed")
        self.probs_t = signal("probs_t", "transposed_probs_stored")
        self.mixed = signal("mixed", "values_mixed")
        self.stored = signal("stored", "heads_stored")
        self.out = signal("out", "output_stored", 16)

    def all(self):
        return self.weights + list(self.named.values())

    @contextmanager
    def stage(self, nc):
        with nc.Block() as block:
            yield block
        for s in self.all():
            s.settle()

    @contextmanager
    def loop(self, nc, n, **per_turn):
        before = {s: s.start for s in self.all()}
        strides = {}
        for name, k in per_turn.items():
            for j, s in enumerate(self.weights if name == "weights" else [self.named[name]]):
                strides[s] = k[j] if name == "weights" else k
        with nc.Fori(0, n) as i:
            for s, k in strides.items():
                s.turn = (i, k)
            yield i
        made = {s.sem.name: s.start - before[s] for s in before if s.start != before[s]}
        for s in before:
            assert s.start - before[s] == strides.get(s, 0), made
            s.turn = None
            s.start = before[s] + n * strides.get(s, 0)


class Split:

    def __init__(self, ctx, nc, name, shape):
        self.hi = ctx.enter_context(nc.sbuf_tensor(name + "_hi", shape, F32R))
        self.lo = ctx.enter_context(nc.sbuf_tensor(name + "_lo", shape, F32R))
        self.parts = (self.hi, self.lo)


class Unit:

    def __init__(self, src, kt, n, jobs):
        self.src, self.kt, self.n, self.jobs = src, kt, n, jobs

    def place(self, slot):
        return slot[:, 0:self.kt * self.n].rearrange("p (k n) -> p k n", k=self.kt)


class Job:

    def __init__(self, w, a, acts, kt, m, n, engine, evac, kind="keep", hidden=None, dst=None, needs=(),
                 after=(), weights_first=True):
        self.w, self.a, self.acts, self.kt, self.m, self.n = w, a, acts, kt, m, n
        self.engine, self.evac, self.kind, self.hidden, self.dst = engine, evac, kind, hidden, dst
        self.needs, self.after, self.weights_first = needs, after, weights_first


def project(nc, S, M, units_of, turns=1, ahead=None):
    units = units_of(0)
    nu = len(units)
    assert turns == 1 or nu % RING == 0
    jobs = [j for u in units for j in u.jobs]
    nj = len(jobs)
    ends = np.cumsum([len(u.jobs) for u in units]).tolist()
    starts = [0] + ends[:-1]
    nth, split_nth, count, n_split = [], [], {"act": 0, "dve": 0}, 0
    for j in jobs:
        count[j.engine] += 1
        nth.append(count[j.engine])
        split_nth.append(n_split)
        n_split += j.kind != "keep"
    done = {"act": S.by_act, "dve": S.by_dve}
    loaded, stale = M.loaded, M.stale
    M.loaded, M.stale = 0, False

    def wait_job(eng, i, j):
        if j < 0 and turns == 1:
            return
        e = jobs[j % nj].engine
        c = nth[j % nj] - (count[e] if j < 0 else 0)
        eng.wait_ge(done[e].sem, done[e].at(i * count[e] + c))

    def run(eng, turn, n=turns):
        if n > 2:
            with eng.Fori(0, n - 1) as i:
                turn(i, False)
        elif n == 2:
            turn(0, False)
        turn(n - 1, True)

    with ExitStack() as ctx:
        wide = max(u.kt * u.n for u in units)
        w = Split(ctx, nc, f"w{M.fresh()}", [P, 2, wide])

        with S.stage(nc) as block:
            @block.sync
            def _(sp):
                def fetch(unit, u):
                    sp.dma_start(unit.place(M.ring[:, u % RING, :]), unit.src).then_inc(*S.weights[u % RING].up)

                if stale:
                    for weights in S.weights:
                        sp.wait_ge(weights.sem, weights.at(0))
                for u in range(loaded, min(RING, nu)):
                    fetch(units_of(0)[u], u)

                def turn(i, last):
                    here, there = units_of(i), None if last else units_of(i + 1)
                    for u in range(nu):
                        v = u + RING
                        if v < nu or not last:
                            sp.wait_ge(S.w_lo.sem, S.w_lo.at(i * nu + u + 1))
                            fetch(here[v] if v < nu else there[v - nu], u)
                run(sp, turn)
                for u, unit in enumerate(ahead or []):
                    sp.wait_ge(S.w_lo.sem, S.w_lo.at(turns * nu))
                    fetch(unit, u)

            @block.tensor
            def _(pe):
                def turn(i, last):
                    n = 0
                    for u, unit in enumerate(units_of(i)):
                        pe.wait_ge(S.w_lo.sem, S.w_lo.at(i * nu + u + 1))
                        parts = [unit.place(t[:, u % 2, :]) for t in w.parts]
                        for j in unit.jobs:
                            wait_job(pe, i, n - BANKS)
                            for need in j.needs:
                                pe.wait_ge(S.lo.sem, S.lo.at(i * n_split + need))
                            acc = M.ps[0:j.m, n % BANKS, 0:j.n]
                            for k in range(j.kt):
                                for wp, ap in ((0, 0), (0, 1), (1, 0)):
                                    ops = [j.w(parts[wp], k), j.a(j.acts.parts[ap], k)]
                                    lhsT, rhs = ops if j.weights_first else ops[::-1]
                                    mm = pe.matmul(acc, lhsT, rhs, start=k == 0 and wp == ap,
                                                   stop=k == j.kt - 1 and wp == 1)
                            mm.then_inc(*S.acc.up)
                            n += 1
                run(pe, turn)

            @block.scalar
            def _(act):
                def high(unit, i, u):
                    s = S.weights[u % RING]
                    act.wait_ge(s.sem, s.at(i * (nu // RING) + u // RING + (0 if u % RING < loaded else 1)))
                    if u >= 2 or not isinstance(i, int) or i > 0:
                        before = ends[u - 2] if u >= 2 else ends[u - 2 + nu] - nj
                        act.wait_ge(S.acc.sem, S.acc.at(i * nj + before))
                    act.activation(unit.place(w.hi[:, u % 2, :]), unit.place(M.ring[:, u % RING, :]), ACT.Copy)\
                        .then_inc(*S.w_hi.up)

                for u in range(min(2, nu)):
                    high(units_of(0)[u], 0, u)

                def turn(i, last):
                    n = 0
                    here = units_of(i)
                    for u, unit in enumerate(here):
                        for j in unit.jobs:
                            m = split_nth[n]
                            if j.engine == "act":
                                act.wait_ge(S.acc.sem, S.acc.at(i * nj + n + 1))
                                for other in j.after:
                                    wait_job(act, i, other)
                                acc = M.ps[0:j.m, n % BANKS, 0:j.n]
                                if j.kind == "relu2":
                                    v = M.v[:, 0, 0:j.n]
                                    if m or turns > 1:
                                        act.wait_ge(S.lo.sem, S.lo.at(i * n_split + m))
                                    act.activation(v, acc, ACT.Relu).then_inc(*S.by_act.up)
                                    act.wait_ge(S.by_act.sem, S.by_act.at(i * count["act"] + nth[n]))
                                    act.activation(j.dst(j.hidden.hi), v, ACT.Square).then_inc(*S.hi.up)
                                else:
                                    j.evac(act, acc).then_inc(*S.by_act.up)
                            elif j.kind == "times":
                                act.wait_ge(S.by_dve.sem, S.by_dve.at(i * count["dve"] + nth[n]))
                                act.activation(j.dst(j.hidden.hi), M.v[:, 0, 0:j.n], ACT.Copy).then_inc(*S.hi.up)
                            n += 1
                        if u + 2 < nu:
                            high(here[u + 2], i, u + 2)
                        elif not last:
                            high(units_of(i + 1)[u + 2 - nu], i + 1, u + 2 - nu)
                run(act, turn)

            @block.vector
            def _(dve):
                def low(unit, i, u):
                    dve.wait_ge(S.w_hi.sem, S.w_hi.at(i * nu + u + 1))
                    dve.tensor_tensor(unit.place(w.lo[:, u % 2, :]), unit.place(M.ring[:, u % RING, :]),
                                      unit.place(w.hi[:, u % 2, :]), ALU.subtract).then_inc(*S.w_lo.up)

                for u in range(min(2, nu)):
                    low(units_of(0)[u], 0, u)

                def turn(i, last):
                    n = 0
                    here = units_of(i)
                    for u, unit in enumerate(here):
                        for j in unit.jobs:
                            m = split_nth[n]
                            acc = M.ps[0:j.m, n % BANKS, 0:j.n]
                            if j.engine == "dve":
                                dve.wait_ge(S.acc.sem, S.acc.at(i * nj + n + 1))
                                for other in j.after:
                                    wait_job(dve, i, other)
                                if j.kind == "times" and (m or turns > 1):
                                    dve.wait_ge(S.lo.sem, S.lo.at(i * n_split + m))
                                j.evac(dve, acc).then_inc(*S.by_dve.up)
                            if j.kind != "keep":
                                v, hi = M.v[:, 0, 0:j.n], j.dst(j.hidden.hi)
                                if j.kind == "relu2":
                                    dve.wait_ge(S.by_act.sem, S.by_act.at(i * count["act"] + nth[n]))
                                    v2 = M.v[:, 1, 0:j.n]
                                    if m or turns > 1:
                                        dve.wait_ge(S.lo.sem, S.lo.at(i * n_split + m))
                                    dve.tensor_tensor(v2, v, v, ALU.mult).then_inc(*S.value.up)
                                    dve.wait_ge(S.value.sem, S.value.at(i * n_split + m + 1))
                                    v = v2
                                dve.wait_ge(S.hi.sem, S.hi.at(i * n_split + m + 1))
                                dve.tensor_tensor(j.dst(j.hidden.lo), v, hi, ALU.subtract).then_inc(*S.lo.up)
                            n += 1
                        if u + 2 < nu:
                            low(here[u + 2], i, u + 2)
                        elif not last:
                            low(units_of(i + 1)[u + 2 - nu], i + 1, u + 2 - nu)
                run(dve, turn)

            n_relu = n_split if any(j.kind == "relu2" for j in jobs) else 0
            S.acc.sent, S.w_hi.sent, S.w_lo.sent = turns * nj, turns * nu, turns * nu
            S.by_act.sent, S.by_dve.sent = turns * count["act"], turns * count["dve"]
            S.hi.sent = S.lo.sent = turns * n_split
            S.value.sent = turns * n_relu
            M.loaded = len(ahead or [])
            for s in range(RING):
                units_in = len(range(s, turns * nu, RING)) if turns > 1 else len(range(s, nu, RING))
                S.weights[s].sent = units_in - (1 if s < loaded else 0) + (1 if s < M.loaded else 0)


def cut(w, r0, r1, c0, n=UNIT, jobs=()):
    src = w[r0:r1, bass.ds(c0, n)].rearrange("(k p) n -> p k n", p=P)
    return Unit(src, (r1 - r0) // P, n, list(jobs))


def feature_jobs(acts, kt, blocks, groups, engine, evac, m=P, k0=0, **more):
    return [
        Job(lambda w, k, c=c: w[:, k, c:c + m], lambda part, k, g=g: part[:, k0 + k, g[0]:g[1]], acts, kt, m,
            g[1] - g[0], engine(b) if callable(engine) else engine,
            evac and (lambda e, acc, b=b, g=g: evac(e, acc, b, g)),
            dst=lambda t, b=b, g=g: t[:, b, g[0]:g[1]], **more)
        for b, c in blocks for g in groups
    ]


def norm(nc, S, M, src, kt, width, groups, out, scale, bias=None, split=None, k0=0, add=None):
    lo, hi = groups[0][0], groups[-1][1]
    w = hi - lo
    sq, rs, tmp = M.sq, M.rs, M.tmp
    with S.stage(nc) as block:
        @block.scalar
        def _(act):
            for k in range(0, kt, 2):
                if k >= 2:
                    act.wait_ge(S.summed.sem, S.summed.at(k - 1))
                act.activation(sq[:, 0, 0:w], src(k, lo, hi), ACT.Square).then_inc(*S.sq_act.one)
            act.wait_ge(S.summed.sem, S.summed.at(kt))
            for g, (a, b) in enumerate(groups):
                ln = act.activation(rs[:, a - lo:b - lo], M.ps[:, g, 0:b - a], ACT.Ln, scale=1.0 / width,
                                    bias=M.eps[:, 0:1])
            ln.then_inc(*S.act.one)
            act.wait_ge(S.act.sem, S.act.at(1))
            act.activation(rs[:, 0:w], rs[:, 0:w], ACT.Exp, scale=-0.5).then_inc(*S.rstd.one)
            for k in range(kt if add is None else 0):
                act.wait_ge(S.normed.sem, S.normed.at(k + 1))
                if split and k >= 2:
                    act.wait_ge(S.lo.sem, S.lo.at(k - 1))
                for a, b in groups:
                    dst = M.f[:, k % 2, a - lo:b - lo] if split else out(k, a, b)
                    o = act.activation(dst, tmp[:, k % 2, a - lo:b - lo], ACT.Identity,
                                       scale=scale(k, a), bias=0.0 if bias is None else bias(k, a))
                o.then_inc(*S.scaled.one)
                if split:
                    act.wait_ge(S.scaled.sem, S.scaled.at(k + 1))
                    act.activation(split.hi[:, k0 + k, lo:hi], M.f[:, k % 2, 0:w], ACT.Copy).then_inc(*S.hi.one)

        @block.vector
        def _(dve):
            def low(k):
                dve.wait_ge(S.hi.sem, S.hi.at(k + 1))
                dve.tensor_tensor(split.lo[:, k0 + k, lo:hi], M.f[:, k % 2, 0:w], split.hi[:, k0 + k, lo:hi],
                                  ALU.subtract).then_inc(*S.lo.one)

            for k in range(1, kt, 2):
                if k >= 2:
                    dve.wait_ge(S.summed.sem, S.summed.at(k - 1))
                dve.tensor_tensor(sq[:, 1, 0:w], src(k, lo, hi), src(k, lo, hi), ALU.mult).then_inc(*S.sq_dve.one)
            dve.wait_ge(S.rstd.sem, S.rstd.at(1))
            for k in range(kt):
                if k >= 2:
                    dve.wait_ge(S.scaled.sem, S.scaled.at(k - 1))
                dve.tensor_tensor(tmp[:, k % 2, 0:w], src(k, lo, hi), rs[:, 0:w], ALU.mult).then_inc(*S.normed.one)
                if split and k:
                    low(k - 1)
                if add is not None:
                    dve.wait_ge(S.normed.sem, S.normed.at(k + 1))
                    dve.scalar_tensor_tensor(add(k, lo, hi), tmp[:, k % 2, 0:w], scale(k, lo), add(k, lo, hi),
                                             ALU.mult, ALU.add).then_inc(*S.scaled.one)
            if split:
                low(kt - 1)

        @block.tensor
        def _(pe):
            for k in range(kt):
                s = S.sq_dve if k % 2 else S.sq_act
                pe.wait_ge(s.sem, s.at(k // 2 + 1))
                for g, (a, b) in enumerate(groups):
                    mm = pe.matmul(M.ps[:, g, 0:b - a], M.ones[:, :], sq[:, k % 2, a - lo:b - lo],
                                   start=k == 0, stop=k == kt - 1)
                mm.then_inc(*S.summed.one)


def chain(eng, sig, ins):
    ins.then_inc(*sig.one)
    eng.wait_ge(sig.sem, sig.at(sig.sent))


def divide(nc, S, M, srcs, split, lo, hi):
    with S.stage(nc) as block:
        @block.scalar
        def _(act):
            for k, src in enumerate(srcs):
                act.activation(split.hi[:, k, lo:hi], src, ACT.Copy).then_inc(*S.hi.one)

        @block.vector
        def _(dve):
            for k, src in enumerate(srcs):
                dve.wait_ge(S.hi.sem, S.hi.at(k + 1))
                dve.tensor_tensor(split.lo[:, k, lo:hi], src, split.hi[:, k, lo:hi], ALU.subtract)


def load(nc, S, pairs):
    with S.stage(nc) as block:
        @block.sync
        def _(sp):
            for dst, src in pairs:
                sp.dma_start(dst, src).then_inc(*S.landed.one)
            sp.wait_ge(S.landed.sem, S.landed.at(len(pairs)))
            sp.nop()


def reduce_angle(dve, S, x, k):
    chain(dve, S.dve, dve.tensor_scalar(k, x, 1.0 / TWO_PI, ROUND, ALU.mult, ALU.add))
    chain(dve, S.dve, dve.tensor_scalar(k, k, -ROUND, None, ALU.add))
    for part in (PI1, PI2, PI3):
        chain(dve, S.dve, dve.scalar_tensor_tensor(x, k, -part, x, ALU.mult, ALU.add))
    chain(dve, S.dve, dve.tensor_scalar(x, x, SIN_MAX, -SIN_MAX, ALU.min, ALU.max))


def attention(nc, S, M, heads, nb, kt, score, mask, mix, store):
    n_items = heads * nb
    w = kt * P

    def s_ps(n):
        return M.ps[:, 2 * (n % 2):2 * (n % 2) + 2, :].rearrange("p a b -> p (a b)")[:, 0:w]

    t_ps = M.ps[:, 4:6, :].rearrange("p a b -> p (a b)")[:, 0:w]
    i = M.fresh()

    with nc.sbuf_tensor(f"p{i}", [P, 2, T], F32) as p, nc.sbuf_tensor(f"pt{i}", [P, kt, nb * P], F32) as p_t, \
            S.stage(nc) as block:
        @block.tensor
        def _(pe):
            def scores(n):
                if n >= 2:
                    pe.wait_ge(S.exped.sem, S.exped.at(n - 1))
                score(pe, n // nb, n % nb, s_ps(n)).then_inc(*S.scores.one)

            def values(h):
                pe.wait_ge(S.probs_t.sem, S.probs_t.at((h + 1) * nb))
                if h >= 2:
                    pe.wait_ge(S.stored.sem, S.stored.at(h - 1))
                mix(pe, h, M.ps[:, 6 + h % 2, :], p_t).then_inc(*S.mixed.one)

            scores(0)
            scores(1)
            for n in range(n_items):
                if n + 2 < n_items:
                    scores(n + 2)
                pe.wait_ge(S.probs.sem, S.probs.at(n + 1))
                if n >= 1:
                    pe.wait_ge(S.probs_t.sem, S.probs_t.at(n))
                for j in range(kt):
                    tr = pe.transpose(t_ps[:, j * P:(j + 1) * P], p[:, n % 2, j * P:(j + 1) * P], M.ident[:, :])
                tr.then_inc(*S.turned.one)
                if n % nb == 0 and n:
                    values(n // nb - 1)
            values(heads - 1)

        @block.vector
        def _(dve):
            def maximum(n):
                dve.wait_ge(S.scores.sem, S.scores.at(n + 1))
                src = s_ps(n)
                if mask:
                    if n >= 2:
                        dve.wait_ge(S.turned.sem, S.turned.at(n - 1))
                    for a, b, m in mask(n % nb):
                        added = dve.tensor_tensor(p[:, n % 2, a:b], src[:, a:b], m, ALU.add)
                    added.then_inc(*S.masked.one)
                    dve.wait_ge(S.masked.sem, S.masked.at(n + 1))
                    src = p[:, n % 2, 0:w]
                dve.tensor_reduce(M.nmax[:, n % 4:n % 4 + 1], src, AX, ALU.max, negate=True).then_inc(*S.maxed.one)

            def normalise(n):
                dve.wait_ge(S.exped.sem, S.exped.at(n + 1))
                dve.reciprocal(M.rsum[:, n % 4:n % 4 + 1], M.esum[:, n % 4:n % 4 + 1]).then_inc(*S.recip.one)
                dve.wait_ge(S.recip.sem, S.recip.at(n + 1))
                dve.tensor_scalar(p[:, n % 2, 0:w], p[:, n % 2, 0:w], M.rsum[:, n % 4:n % 4 + 1], None,
                                  ALU.mult).then_inc(*S.probs.one)

            def head(h):
                dve.wait_ge(S.mixed.sem, S.mixed.at(h + 1))
                store(dve, h, M.ps[:, 6 + h % 2, :]).then_inc(*S.stored.one)

            for n in range(n_items):
                maximum(n)
                if n:
                    normalise(n - 1)
                if n > nb and n % nb == 1 % nb:
                    head(n // nb - 1 if nb > 1 else n - 2)
            normalise(n_items - 1)
            if heads > 1 and nb == 1:
                head(heads - 2)
            head(heads - 1)

        @block.scalar
        def _(act):
            def exponent(n):
                act.wait_ge(S.maxed.sem, S.maxed.at(n + 1))
                if not mask and n >= 2:
                    act.wait_ge(S.turned.sem, S.turned.at(n - 1))
                src = p[:, n % 2, 0:w] if mask else s_ps(n)
                act.activation(p[:, n % 2, 0:w], src, ACT.Exp, bias=M.nmax[:, n % 4:n % 4 + 1],
                               accum_out=M.esum[:, n % 4:n % 4 + 1]).then_inc(*S.exped.one)

            def keep(n):
                act.wait_ge(S.turned.sem, S.turned.at(n + 1))
                if n % nb == 0 and n:
                    act.wait_ge(S.mixed.sem, S.mixed.at(n // nb))
                b = n % nb
                act.activation(p_t[:, 0:kt, b * P:(b + 1) * P], t_ps.rearrange("p (k q) -> p k q", k=kt),
                               ACT.Copy).then_inc(*S.probs_t.one)

            for n in range(n_items):
                exponent(n)
                if n:
                    keep(n - 1)
            keep(n_items - 1)



def fourier(nc, S, M, io, ss, lo, length):
    nt = length // P
    with ExitStack() as ctx:
        chan = ctx.enter_context(nc.sbuf_tensor(f"chan{ss}", [P, 2 * P], F32))
        ab = ctx.enter_context(nc.sbuf_tensor(f"ab{ss}", [P, nt, 2, 2, P], F32))
        tok = ctx.enter_context(nc.sbuf_tensor(f"tok{ss}", [P, nt, 2, length], F32))
        load(nc, S, [(chan[:, :], io["fnet_channels"]), (tok[:, :, :, :], io[f"fnet_tokens_{length}"])])
        with S.stage(nc) as block:
            @block.tensor
            def _(pe):
                for n in range(2 * nt):
                    t, f = divmod(n, 2)
                    mm = pe.matmul(M.ps[:, n % 8, 0:2 * P], M.p[:, 6 + f, lo + t * P:lo + (t + 1) * P], chan[:, :],
                                   start=True, stop=True)
                    mm.then_inc(*S.pe.one)
                for f in range(2):
                    for t in range(nt):
                        for c in range(2):
                            if f == 0 and c == 0:
                                pe.wait_ge(S.by_dve.sem, S.by_dve.at(2 * nt))
                            mm = pe.matmul(M.ps[:, f, 0:length], ab[:, t, f, c, :], tok[:, t, c, :],
                                           start=t == 0 and c == 0, stop=t == nt - 1 and c == 1)
                    mm.then_inc(*S.acc.one)

            @block.vector
            def _(dve):
                for n in range(2 * nt):
                    t, f = divmod(n, 2)
                    dve.wait_ge(S.pe.sem, S.pe.at(n + 1))
                    dve.tensor_copy(ab[:, t, f, :, :].rearrange("p c n -> p (c n)"),
                                    M.ps[:, n % 8, 0:2 * P]).then_inc(*S.by_dve.one)

            @block.scalar
            def _(act):
                for f in range(2):
                    act.wait_ge(S.acc.sem, S.acc.at(f + 1))
                    act.activation(M.p[:, 6 + f, lo:lo + length], M.ps[:, f, 0:length], ACT.Copy).then_inc(*S.act.one)


def hyena(nc, S, M, io, l, ss, lo, length):
    nt = length // P
    with ExitStack() as ctx:
        def sb(name, shape):
            return ctx.enter_context(nc.sbuf_tensor(f"{name}{ss}", shape, F32))

        tk = sb("tk", [P, nt, 2, length])
        ta = sb("ta", [P, nt, 2, length])
        emb = sb("emb", [EMB, length])
        w1 = sb("w1", [EMB, ORDER])
        w2 = sb("w2", [ORDER, ORDER])
        w3 = sb("w3", [ORDER, 2 * HY])
        hid = sb("hid", [ORDER, 2, length])
        kk = sb("kk", [ORDER, length])
        decay = sb("decay", [P, nt, 2 * HY])
        filt = sb("filt", [P, nt, 2 * HY])
        pm = sb("pm", [P, nt, 2, HY])
        inv = sb("inv", [P, HY])
        kf = decay[:, :, :].rearrange("p t (c n) -> p t c n", c=2)
        u = sb("u", [P, 6, length])
        zt = sb("zt", [P, nt, HY])
        yf = sb("yf", [P, nt, 2, HY])
        m4 = filt[:, 0:2, :].rearrange("p a (c n) -> p a c n", c=2)
        pairs = [(emb[:, :], io[f"hy_emb_{length}"]), (w1[:, :], io["hy_w1"][l]), (w2[:, :], io["hy_w2"][l]),
                 (w3[:, :], io["hy_w3"][l]), (decay[:, :, :], io[f"hy_decay_{length}"]),
                 (tk[:, :, :, :], io[f"hy_tk_{length}"]), (ta[:, :, :, :], io[f"hy_ta_{length}"])]
        load(nc, S, pairs)
        b1, b2, fr = (M.col(n, l)[0:ORDER] for n in ("hy_b1", "hy_b2", "hy_freq"))
        cw = lambda j, b: M.col("hy_conv_w", l, 6 * j + b)
        p_in = lambda b: M.p[:, 8 + b, lo:lo + length]

        with S.stage(nc) as block:
            @block.tensor
            def _(pe):
                pe.matmul(M.ps[0:ORDER, 0, 0:length], w1[:, :], emb[:, :], start=True, stop=True).then_inc(*S.pe.one)
                pe.wait_ge(S.act.sem, S.act.at(1))
                pe.matmul(M.ps[0:ORDER, 1, 0:length], w2[:, :], hid[:, 0, :], start=True, stop=True).then_inc(*S.pe.one)
                pe.wait_ge(S.act.sem, S.act.at(2))
                for t in range(nt):
                    pe.matmul(M.ps[:, 2 + t, 0:2 * HY], hid[:, 1, t * P:(t + 1) * P], w3[:, :],
                              start=True, stop=True).then_inc(*S.pe.one)
                for t in range(nt):
                    pe.wait_ge(S.by_act.sem, S.by_act.at(t + 1))
                    mm = pe.matmul(M.ps[:, 7, 0:2 * HY], M.ones[:, :], yf[:, t, :, :].rearrange("p c n -> p (c n)"),
                                   start=t == 0, stop=t == nt - 1)
                mm.then_inc(*S.acc.one)

            @block.vector
            def _(dve):
                for s, b in ((0, b1), (1, b2)):
                    dve.wait_ge(S.pe.sem, S.pe.at(s + 1))
                    chain(dve, S.dve, dve.tensor_scalar(hid[:, s, :], M.ps[0:ORDER, s, 0:length], b, fr,
                                                        ALU.add, ALU.mult))
                    reduce_angle(dve, S, hid[:, s, :], kk[:, :])
                    dve.tensor_scalar(kk[:, :], hid[:, s, :], 1.0, None, ALU.mult).then_inc(*S.by_dve.one)
                for t in range(nt):
                    dve.wait_ge(S.pe.sem, S.pe.at(3 + t))
                    chain(dve, S.dve, dve.tensor_tensor(filt[:, t, :], M.ps[:, 2 + t, 0:2 * HY], decay[:, t, :],
                                                        ALU.mult))
                    dve.tensor_tensor(pm[:, t, 0, :], filt[:, t, 0:HY], filt[:, t, HY:2 * HY], ALU.add)
                    dve.tensor_tensor(pm[:, t, 1, :], filt[:, t, HY:2 * HY], filt[:, t, 0:HY],
                                      ALU.subtract).then_inc(*S.by_dve.one)
                for b in range(6):
                    chain(dve, S.dve, dve.tensor_scalar(u[:, b, :], p_in(b), cw(1, b), M.col("hy_conv_b", l, b),
                                                        ALU.mult, ALU.add))
                    chain(dve, S.dve, dve.scalar_tensor_tensor(u[:, b, 1:length], p_in(b)[:, 0:length - 1], cw(0, b),
                                                               u[:, b, 1:length], ALU.mult, ALU.add))
                    chain(dve, S.dve, dve.scalar_tensor_tensor(u[:, b, 0:length - 1], p_in(b)[:, 1:length], cw(2, b),
                                                               u[:, b, 0:length - 1], ALU.mult, ALU.add))
                for b in range(2):
                    dve.tensor_tensor(u[:, 2 + b, :], u[:, 2 + b, :], u[:, 4 + b, :], ALU.mult)
                dve.wait_ge(S.acc.sem, S.acc.at(1))
                chain(dve, S.dve, dve.tensor_copy(zt[:, 0, :], M.ps[:, 7, 0:HY]))
                chain(dve, S.dve, dve.tensor_tensor(inv[:, :], zt[:, 0, :], M.ps[:, 7, HY:2 * HY], ALU.add))
                chain(dve, S.dve, dve.tensor_scalar(inv[:, :], inv[:, :], float(length), None, ALU.mult))
                dve.reciprocal(inv[:, :], inv[:, :])

            @block.scalar
            def _(act):
                for s in range(2):
                    act.wait_ge(S.by_dve.sem, S.by_dve.at(s + 1))
                    act.activation(hid[:, s, :], kk[:, :], ACT.Sin).then_inc(*S.act.one)
                for t in range(nt):
                    act.wait_ge(S.by_dve.sem, S.by_dve.at(3 + t))
                    act.activation(yf[:, t, :, :].rearrange("p c n -> p (c n)"), filt[:, t, :],
                                   ACT.Abs).then_inc(*S.by_act.one)

        with S.stage(nc) as block:
            @block.tensor
            def _(pe):
                for b in range(2):
                    for t in range(nt):
                        pe.transpose(M.ps[:, b, t * P:(t + 1) * P], u[:, 2 + b, t * P:(t + 1) * P],
                                     M.ident[:, :]).then_inc(*S.pe.one)
                for f in range(nt):
                    if f >= 2:
                        pe.wait_ge(S.by_act.sem, S.by_act.at(f - 1))
                    for c in range(2):
                        for t in range(nt):
                            mm = pe.matmul(M.ps[:, 2 + f % 2, c * HY:(c + 1) * HY], tk[:, t, c, f * P:(f + 1) * P],
                                           pm[:, t, c, :], start=t == 0, stop=t == nt - 1)
                    mm.then_inc(*S.acc.one)
                    pe.wait_ge(S.act.sem, S.act.at(2))
                    if f >= 2:
                        pe.wait_ge(S.mixed.sem, S.mixed.at(f - 1))
                    for c in range(2):
                        for t in range(nt):
                            mm = pe.matmul(M.ps[:, 4 + f % 2, c * HY:(c + 1) * HY], ta[:, t, c, f * P:(f + 1) * P],
                                           zt[:, t, :], start=t == 0, stop=t == nt - 1)
                    mm.then_inc(*S.scores.one)
                pe.wait_ge(S.mixed.sem, S.mixed.at(nt))
                for b in range(2):
                    for f in range(nt):
                        for c in range(2):
                            mm = pe.matmul(M.ps[:, 6 + b, 0:length], yf[:, f, c, b * P:(b + 1) * P], ta[:, f, c, :],
                                           start=f == 0 and c == 0, stop=f == nt - 1 and c == 1)
                    mm.then_inc(*S.probs.one)

            @block.scalar
            def _(act):
                for b in range(2):
                    act.wait_ge(S.pe.sem, S.pe.at((b + 1) * nt))
                    act.activation(zt[:, :, b * P:(b + 1) * P],
                                   M.ps[:, b, 0:length].rearrange("p (t c) -> p t c", t=nt), ACT.Copy)\
                        .then_inc(*S.act.one)
                for f in range(nt):
                    act.wait_ge(S.acc.sem, S.acc.at(f + 1))
                    act.activation(kf[:, f, :, :].rearrange("p c n -> p (c n)"), M.ps[:, 2 + f % 2, :],
                                   ACT.Copy).then_inc(*S.by_act.one)

            @block.vector
            def _(dve):
                for f in range(nt):
                    dve.wait_ge(S.by_act.sem, S.by_act.at(f + 1))
                    for c in range(2):
                        k = dve.tensor_tensor(kf[:, f, c, :], kf[:, f, c, :], inv[:, :], ALU.mult)
                    chain(dve, S.dve, k)
                    dve.wait_ge(S.scores.sem, S.scores.at(f + 1))
                    zc, zs = M.ps[:, 4 + f % 2, 0:HY], M.ps[:, 4 + f % 2, HY:2 * HY]
                    dve.tensor_tensor(m4[:, 0, 0, :], zc, kf[:, f, 0, :], ALU.mult)
                    dve.tensor_tensor(m4[:, 0, 1, :], zs, kf[:, f, 1, :], ALU.mult)
                    dve.tensor_tensor(m4[:, 1, 0, :], zs, kf[:, f, 0, :], ALU.mult)
                    chain(dve, S.dve, dve.tensor_tensor(m4[:, 1, 1, :], zc, kf[:, f, 1, :], ALU.mult))
                    dve.tensor_tensor(yf[:, f, 0, :], m4[:, 0, 0, :], m4[:, 0, 1, :], ALU.add)
                    y = dve.tensor_tensor(yf[:, f, 1, :], m4[:, 1, 0, :], m4[:, 1, 1, :], ALU.subtract)
                    y.then_inc(*S.mixed.one)
                    dve.wait_ge(S.mixed.sem, S.mixed.at(f + 1))
                for b in range(2):
                    dve.wait_ge(S.probs.sem, S.probs.at(b + 1))
                    chain(dve, S.dve, dve.scalar_tensor_tensor(u[:, 2 + b, :], u[:, 2 + b, :], M.col("hy_d", l, b),
                                                               M.ps[:, 6 + b, 0:length], ALU.mult, ALU.add))
                    dve.tensor_tensor(M.p[:, 8 + b, lo:lo + length], u[:, 2 + b, :], u[:, b, :],
                                      ALU.mult).then_inc(*S.by_dve.one)


def px_cut(io, l, c0, jobs=()):
    return cut(io["w_in"][l], 0, D, c0, UNIT, jobs)


def square_cuts(w, jobs_of=lambda c: ()):
    return [cut(w, 0, D, c * UNIT, UNIT, jobs_of(c)) for c in range(D // UNIT)]


def first_layer(nc, S, M, io, l):
    last = l == DEPTH - 1
    groups = [X_COLS, C_COLS]
    outer = [X_COLS] if last else groups
    side = lambda a: 0 if a < LX else 1
    x = lambda k, a, b: M.x[:, k, a:b]

    with ExitStack() as ctx:
        M.p = ctx.enter_context(nc.sbuf_tensor(f"p{l}", [P, 14, T], F32))

        def keep(e, acc, b, g):
            m = QK if b == 5 else P
            if b % 2:
                return e.activation(M.p[0:m, b, g[0]:g[1]], acc, ACT.Copy)
            return e.tensor_copy(M.p[0:m, b, g[0]:g[1]], acc)

        cuts = [(0, [0, 1]), (256, [2, 3]), (512, [4, 5]), (OFF_F, [6, 7]), (OFF_H, [8, 9]),
                (OFF_H + 256, [10, 11]), (OFF_H + 512, [12, 13])]
        w_q = [cut(io["w_uq"][l], 0, Q_LORA, c * 4 * QK, 4 * QK) for c in range(2)]
        with ExitStack() as inner:
            h = Split(inner, nc, f"h{l}", [P, KD, T])
            norm(nc, S, M, x, KD, D, groups, None, lambda k, a: M.gain[:, 2 * l, side(a), k:k + 1],
                 lambda k, a: M.mod(l, 0, k, side(a)), split=h)
            units = []
            for c0, blocks in cuts:
                js = []
                for n, b in enumerate(blocks):
                    gs = groups if b in (3, 4, 5) else outer
                    off, m = (64, QK) if b == 5 else (n * P, P)
                    js += feature_jobs(h, KD, [(b, off)], gs, "act" if b % 2 else "dve", keep, m)
                units.append(px_cut(io, l, c0, js))
            project(nc, S, M, lambda i: units, ahead=w_q)

        for ss, lo, length in [(f"x{l}", 0, LX)] + ([] if last else [(f"c{l}", LX, LC)]):
            fourier(nc, S, M, io, ss, lo, length)
            hyena(nc, S, M, io, l, ss, lo, length)

        with ExitStack() as att:
            q = att.enter_context(nc.sbuf_tensor(f"q{l}", [P, HEADS, T], F32))
            k_t = att.enter_context(nc.sbuf_tensor(f"k{l}", [P, HEADS, T], F32))
            v = M.p[:, 0:4, :].rearrange("p a b -> p (a b)").rearrange("p (t n) -> p t n", t=T // P)
            scale = 1.0 / math.sqrt(QK)

            def keep_q(e, acc, b, g):
                return e.activation(q[0:QK, b, g[0]:g[1]], acc, ACT.Copy, scale=scale)

            def keep_k(e, acc, b, g):
                return e.tensor_copy(k_t[0:NOPE, b, g[0]:g[1]], acc[0:NOPE, :])

            with ExitStack() as inner:
                c = Split(inner, nc, f"c{l}", [P, 5, T])
                norm(nc, S, M, lambda k, a, b: M.p[:, k, a:b], 3, Q_LORA, outer, None,
                     lambda k, a: M.col("q_norm_g", l, k), split=c)
                norm(nc, S, M, lambda k, a, b: M.p[:, 3 + k, a:b], 2, KV_LORA, groups, None,
                     lambda k, a: M.col("kv_norm_g", l, k), split=c, k0=3)
                for u, unit in enumerate(w_q):
                    unit.jobs = [j for b in range(4)
                                 for j in feature_jobs(c, 3, [(4 * u + b, b * QK)], outer, "act", keep_q, QK)]
                vcols = lambda w, k: w[:, k, :].rearrange("p (h n) -> p h n", h=4)[:, :, NOPE:NOPE + VDIM]
                w_kv = []
                for u in range(2):
                    js = feature_jobs(c, 2, [(4 * u + b, b * P) for b in range(4)], groups, "dve", keep_k, k0=3)
                    js += [Job(vcols, lambda part, k, t=t: part[:, 3 + k, t * P:(t + 1) * P], c, 2, P, 4 * VDIM, "act",
                               lambda e, acc, t=t, u=u: e.activation(v[:, t, 4 * VDIM * u:4 * VDIM * (u + 1)], acc,
                                                                     ACT.Copy),
                               weights_first=False) for t in range(T // P)]
                    w_kv.append(cut(io["w_ukv"][l], 0, KV_LORA, u * 4 * P, 4 * P, js))
                project(nc, S, M, lambda i: w_q + w_kv, ahead=square_cuts(io["w_out"][l])[:2])

            lo, hi = NOPE, QK
            srcs = [q[0:QK, b, 0:LX] for b in range(HEADS)] + [M.p[0:QK, 5, 0:LX]]
            with ExitStack() as inner:
                swap = inner.enter_context(nc.sbuf_tensor(f"swap{l}", [P, P], F32))
                rope = inner.enter_context(nc.sbuf_tensor(f"rope{l}", [P, 2, LX], F32))
                load(nc, S, [(swap[:, :], io["rope_swap"]), (rope[:, :, :], io["rope_tables"])])
                with S.stage(nc) as block:
                    @block.tensor
                    def _(pe):
                        for n, s in enumerate(srcs):
                            if n >= 8:
                                pe.wait_ge(S.by_dve.sem, S.by_dve.at(n - 7))
                            pe.matmul(M.ps[0:QK, n % 8, :], swap[0:QK, 0:QK], s, start=True, stop=True)\
                                .then_inc(*S.pe.one)

                    @block.vector
                    def _(dve):
                        for n, s in enumerate(srcs):
                            dve.wait_ge(S.pe.sem, S.pe.at(n + 1))
                            t = M.sq[lo:hi, n % 2, 0:LX]
                            dve.tensor_tensor(t, M.ps[lo:hi, n % 8, :], rope[lo:hi, 1, :], ALU.mult)
                            chain(dve, S.dve, dve.tensor_tensor(s[lo:hi, :], s[lo:hi, :], rope[lo:hi, 0, :], ALU.mult))
                            dve.tensor_tensor(s[lo:hi, :], s[lo:hi, :], t, ALU.add).then_inc(*S.by_dve.one)
                            dve.wait_ge(S.by_dve.sem, S.by_dve.at(n + 1))

                    @block.scalar
                    def _(act):
                        act.wait_ge(S.by_dve.sem, S.by_dve.at(len(srcs)))
                        for b in range(HEADS):
                            act.activation(k_t[lo:hi, b, :], M.p[lo:hi, 5, :], ACT.Copy).then_inc(*S.act.one)

            for lo_q, lo_k, nb, kt in [(0, 0, LX // P, T // P)] + ([] if last else [(LX, LX, LC // P, LC // P)]):
                def score(pe, hd, b, acc):
                    for a in range(0, kt * P, 512):
                        n = min(512, kt * P - a)
                        mm = pe.matmul(acc[:, a:a + n], q[0:QK, hd, lo_q + b * P:lo_q + (b + 1) * P],
                                       k_t[0:QK, hd, lo_k + a:lo_k + a + n], start=True, stop=True)
                    return mm

                def mix(pe, hd, acc, p_t):
                    for j in range(kt):
                        mm = pe.matmul(acc[0:VDIM, 0:nb * P], v[:, lo_k // P + j, hd * VDIM:(hd + 1) * VDIM],
                                       p_t[:, j, 0:nb * P], start=j == 0, stop=j == kt - 1)
                    return mm

                def store(dve, hd, acc):
                    r = hd % 2 * VDIM
                    return dve.tensor_copy(M.p[r:r + VDIM, 10 + hd // 2, lo_q:lo_q + nb * P], acc[0:VDIM, 0:nb * P])

                attention(nc, S, M, HEADS, nb, kt, score, None, mix, store)

        def residual(m):
            def add(e, acc, b, g):
                xs = M.x[:, b, g[0]:g[1]]
                return e.scalar_tensor_tensor(xs, acc, M.mod(l, m, b, side(g[0])), xs, ALU.mult, ALU.add)
            return add

        hi = outer[-1][1]
        up0 = [cut(io["w_mlp1"][l], 0, D, c * UNIT) for c in range(2)]
        with ExitStack() as inner:
            h = Split(inner, nc, f"mix{l}", [P, KD, T])
            divide(nc, S, M, [M.p[:, b, 0:hi] for b in (10, 11, 12, 13, 6, 7, 8, 9)], h, 0, hi)
            units = square_cuts(io["w_out"][l], lambda c: feature_jobs(
                h, KD, [(2 * c, 0), (2 * c + 1, P)], outer, "dve", residual(2)))
            project(nc, S, M, lambda i: units, ahead=up0)

    if last:
        following = []
    else:
        following = [px_cut(io, l + 1, c * UNIT) for c in range(2)]
    with ExitStack() as ctx:
        h = Split(ctx, nc, f"hm{l}", [P, KD, T])
        hid = Split(ctx, nc, f"hid{l}", [P, KD, T])
        norm(nc, S, M, x, KD, D, outer, None, lambda k, a: M.gain[:, 2 * l + 1, side(a), k:k + 1],
             lambda k, a: M.mod(l, 3, k, side(a)), split=h)
        ng = len(outer)
        w2 = io["w_mlp2"][l].rearrange("(g k p) n -> g p k n", p=P, k=KD)

        def mlp_units(i):
            units = [cut(io["w_mlp1"][l], 0, D, i * D + c * UNIT, UNIT, feature_jobs(
                h, KD, [(2 * c, 0), (2 * c + 1, P)], outer, "act", None, kind="relu2", hidden=hid))
                for c in range(4)]
            for c in range(4):
                js = feature_jobs(hid, KD, [(2 * c, 0), (2 * c + 1, P)], outer, "dve", residual(5))
                js[0].needs = (8 * ng,)
                src = w2[i if isinstance(i, int) else bass.ds(i, 1), :, :, c * UNIT:(c + 1) * UNIT]
                if not isinstance(i, int):
                    src = src.rearrange("a p k n -> (a p) k n")
                units.append(Unit(src, KD, UNIT, js))
            return units

        project(nc, S, M, mlp_units, turns=D_FF // D, ahead=following)



def recurrence(nc, S, M, io):
    w = io["hgrn_w_in_2"][0]
    nch = LX // CHUNK
    h = M.split
    with ExitStack() as ctx:
        def sb(name, shape):
            return ctx.enter_context(nc.sbuf_tensor("r_" + name, shape, F32))

        qs, sg, kk, gs = (sb(n, [P, 2, LX]) for n in ("q", "sg", "k", "g"))
        b_, eb, nb_, ke = (sb(n, [P, 2, LX]) for n in ("b", "eb", "nb", "ke"))
        v = sb("v", [P, 4, UNIT])
        ket = sb("ket", [P, 2, 4, P])
        at = sb("at", [P, 2, LX])
        st = sb("st", [P, 2, nch, P])
        y = M.y
        with S.loop(nc, H2 // 2, **LOOPS["recurrence"]) as i:
            def unit(sec, jobs, later=0):
                return cut(w, 0, D, i * UNIT + (later * UNIT + sec * D), UNIT, jobs)

            def forget(e, acc, b, g):
                e.activation(kk[:, b, :], acc, ACT.Sigmoid, scale=-1.0)
                return e.activation(sg[:, b, :], acc, ACT.Sigmoid)

            blocks = [(0, 0), (1, P)]
            token = [Job(lambda w, k: w[:, k, :], lambda part, k, t=t: part[:, k, t * P:(t + 1) * P], h, KD, P, UNIT,
                         "dve", lambda e, acc, t=t: e.tensor_copy(v[:, t, :], acc), weights_first=False)
                     for t in range(4)]
            units = [
                unit(1, feature_jobs(h, KD, blocks, [X_COLS], "act", forget)),
                unit(0, feature_jobs(h, KD, blocks, [X_COLS], "act",
                                     lambda e, acc, b, g: e.activation(qs[:, b, :], acc, ACT.Silu))),
                unit(3, feature_jobs(h, KD, blocks, [X_COLS], "act",
                                     lambda e, acc, b, g: e.activation(gs[:, b, :], acc, ACT.Silu))),
                unit(2, token),
            ]
            project(nc, S, M, lambda _: units, ahead=[unit(1, [], 1), unit(0, [], 1)])
            with S.stage(nc) as block:
                @block.vector
                def _(dve):
                    for n in range(2):
                        om, lb = (M.lower[:, j, bass.ds(i * 2 + n, 1)] for j in (1, 0))
                        dve.tensor_scalar(kk[:, n, :], kk[:, n, :], om, None, ALU.mult)
                        f = dve.tensor_scalar(sg[:, n, :], sg[:, n, :], om, lb, ALU.mult, ALU.add)
                    f.then_inc(*S.dve.one)
                    dve.wait_ge(S.act.sem, S.act.at(1))
                    for n in range(2):
                        s = dve.tensor_tensor_scan(b_[:, n, :], M.resets[:, :], sg[:, n, :], 0.0, ALU.mult, ALU.add)
                    chain(dve, S.dve, s)
                    for n in range(2):
                        bn = b_[:, n, :].rearrange("p (c t) -> p c t", t=CHUNK)
                        o = dve.tensor_tensor(ke[:, n, :].rearrange("p (c t) -> p c t", t=CHUNK),
                                              bn[:, :, CHUNK - 1:CHUNK].to_broadcast([P, nch, CHUNK]), bn,
                                              ALU.subtract)
                    o.then_inc(*S.dve.one)
                    dve.wait_ge(S.act.sem, S.act.at(2))
                    dve.tensor_tensor(qs[:, :, :], qs[:, :, :], eb[:, :, :], ALU.mult)
                    dve.wait_ge(S.act.sem, S.act.at(3))
                    dve.tensor_tensor(nb_[:, :, :], nb_[:, :, :], kk[:, :, :], ALU.mult)
                    dve.wait_ge(S.act.sem, S.act.at(4))
                    dve.tensor_tensor(ke[:, :, :], ke[:, :, :], kk[:, :, :], ALU.mult)
                    dve.memset(st[:, :, 0, :], 0.0)

                @block.scalar
                def _(act):
                    act.wait_ge(S.dve.sem, S.dve.at(1))
                    act.activation(sg[:, :, :], sg[:, :, :], ACT.Ln).then_inc(*S.act.one)
                    act.wait_ge(S.dve.sem, S.dve.at(2))
                    act.activation(eb[:, :, :], b_[:, :, :], ACT.Exp).then_inc(*S.act.one)
                    act.activation(nb_[:, :, :], b_[:, :, :], ACT.Exp, scale=-1.0).then_inc(*S.act.one)
                    act.wait_ge(S.dve.sem, S.dve.at(3))
                    act.activation(ke[:, :, :], ke[:, :, :], ACT.Exp).then_inc(*S.act.one)

            def additions(g):
                return 4 if g < 4 else 0

            with S.stage(nc) as block:
                @block.tensor
                def _(pe):
                    for n in range(2):
                        for t in range(4):
                            tr = pe.transpose(M.ps[:, n, t * P:(t + 1) * P], ke[:, n, t * P:(t + 1) * P], M.ident[:, :])
                        tr.then_inc(*S.pe.one)
                        for t in range(4):
                            c = slice(t * P, (t + 1) * P)
                            mm = pe.matmul(M.ps[:, 2 + n, c], nb_[:, n, c], qs[:, n, c], start=True, stop=True)
                        mm.then_inc(*S.scores.one)
                    for g in range(8):
                        t, n = divmod(g, 2)
                        pe.wait_ge(S.by_act.sem, S.by_act.at(n + 1))
                        if g == 4:
                            pe.wait_ge(S.masked.sem, S.masked.at(2))
                        for j in range(4):
                            r = slice(j * CHUNK, (j + 1) * CHUNK)
                            mm = pe.matmul(M.ps[:, additions(g) + j, g % 4 * P:(g % 4 + 1) * P], ket[r, n, t, :],
                                           v[r, t, n * P:(n + 1) * P], start=True, stop=True)
                        mm.then_inc(*S.acc.one)
                    pe.wait_ge(S.mixed.sem, S.mixed.at(2 * (nch - 1)))
                    pe.wait_ge(S.masked.sem, S.masked.at(2))
                    for n in range(2):
                        for t in range(4):
                            c = slice(t * P, (t + 1) * P)
                            pe.matmul(M.ps[:, n, c], v[:, t, n * P:(n + 1) * P], at[:, n, c], start=t == 0, stop=False,
                                      skip_group_check=True)
                        for m in range(1, nch):
                            c = slice(m * CHUNK, (m + 1) * CHUNK)
                            mm = pe.matmul(M.ps[:, n, c], st[:, n, m, :], qs[:, n, c], start=False, stop=m == nch - 1,
                                           skip_group_check=True)
                        mm.then_inc(*S.probs.one)
                    for n in range(2):
                        pe.wait_ge(S.sq_act.sem, S.sq_act.at(n + 1))
                        pe.matmul(M.ps[:, 2 + n, :], M.ones[:, :], nb_[:, n, :], start=True, stop=True)\
                            .then_inc(*S.summed.one)

                @block.scalar
                def _(act):
                    for n in range(2):
                        act.wait_ge(S.pe.sem, S.pe.at(n + 1))
                        act.activation(ket[:, n, :, :].rearrange("p t k -> p (t k)"), M.ps[:, n, :], ACT.Copy)\
                            .then_inc(*S.by_act.one)
                    for n in range(2):
                        act.wait_ge(S.probs.sem, S.probs.at(n + 1))
                        act.activation(nb_[:, n, :], M.ps[:, n, :], ACT.Square).then_inc(*S.sq_act.one)
                    for n in range(2):
                        act.wait_ge(S.summed.sem, S.summed.at(n + 1))
                        act.activation(ke[:, n, :], M.ps[:, 2 + n, :], ACT.Ln, scale=1.0 / P, bias=M.eps[:, 0:1])\
                            .then_inc(*S.act.one)
                        act.wait_ge(S.act.sem, S.act.at(n + 1))
                        act.activation(ke[:, n, :], ke[:, n, :], ACT.Exp, scale=-0.5).then_inc(*S.rstd.one)

                @block.vector
                def _(dve):
                    for n in range(2):
                        dve.wait_ge(S.scores.sem, S.scores.at(n + 1))
                        dve.scalar_tensor_tensor(at[:, n, :].rearrange("p (t c) -> p t c", t=4),
                                                 M.ps[:, 2 + n, :].rearrange("p (t c) -> p t c", t=4), 3.0e38,
                                                 M.causal[:, :].unsqueeze(1).to_broadcast([P, 4, P]),
                                                 ALU.min, ALU.mult).then_inc(*S.masked.one)
                    for m in range(nch - 1):
                        for n in range(2):
                            g = m // 4 * 2 + n
                            if m % 8 == 0 and n == 0:
                                dve.wait_ge(S.acc.sem, S.acc.at(g + 4))
                            if m:
                                dve.wait_ge(S.mixed.sem, S.mixed.at(2 * m - 1 + n))
                            dve.scalar_tensor_tensor(
                                st[:, n, m + 1, :], st[:, n, m, :],
                                eb[:, n, m * CHUNK + CHUNK - 1:m * CHUNK + CHUNK],
                                M.ps[:, additions(g) + m % 4, g % 4 * P:(g % 4 + 1) * P], ALU.mult, ALU.add)\
                                .then_inc(*S.mixed.one)
                    for n in range(2):
                        dve.wait_ge(S.rstd.sem, S.rstd.at(n + 1))
                        chain(dve, S.dve, dve.tensor_tensor(ke[:, n, :], ke[:, n, :], M.ps[:, n, :], ALU.mult))
                        dve.scalar_tensor_tensor(y[:, bass.ds(i * 2 + n, 1), :].rearrange("p a t -> p (a t)"),
                                                 ke[:, n, :], M.hgain[:, bass.ds(i * 2 + n, 1)], gs[:, n, :],
                                                 ALU.mult, ALU.mult).then_inc(*S.by_dve.one)


def dilated(nc, S, M, io):
    w = io["attn_w_in_2"][0]
    h = M.split
    with ExitStack() as ctx:
        def sb(name, shape):
            return ctx.enter_context(nc.sbuf_tensor("d_" + name, shape, F32))

        qk = sb("qk", [P, 12, LX])
        v = sb("v", [P, GROUPS2, 4, UNIT])
        masks = sb("masks", [P, 4 * LX + 2 * P])
        scale = P ** -0.5
        load(nc, S, [(masks[:, :], io["attn_masks"])])
        with S.loop(nc, H2 // 2, **LOOPS["dilated"]) as i:
            units = []
            for g in range(GROUPS2):
                for s in range(2):
                    def keep(e, acc, b, gr, g=g, s=s):
                        dst = qk[:, 4 * g + 2 * s + b, :]
                        if s == 0:
                            return e.activation(dst, acc, ACT.Copy, scale=scale)
                        return e.tensor_copy(dst, acc)
                    c0 = (3 * g + s) * D
                    units.append(cut(w, 0, D, i * UNIT + c0, UNIT, feature_jobs(
                        h, KD, [(0, 0), (1, P)], [X_COLS], "dve" if s else "act", keep)))
                js = []
                for t in range(4):
                    def tokens(part, k, t=t, g=g):
                        if g == 0:
                            return part[:, k, t * P:(t + 1) * P]
                        return part[:, k, 0:LX].rearrange("p (m r) -> p m r", r=4)[:, :, t]
                    js.append(Job(lambda w_, k: w_[:, k, :], tokens, h, KD, P, UNIT, "dve",
                                  lambda e, acc, t=t, g=g: e.tensor_copy(v[:, g, t, :], acc), weights_first=False))
                units.append(cut(w, 0, D, i * UNIT + (3 * g + 2) * D, UNIT, js))
            project(nc, S, M, lambda _: units, ahead=[cut(w, 0, D, i * UNIT + UNIT), cut(w, 0, D, i * UNIT + UNIT + D)])

            with nc.sbuf_tensor("d_swp", [ROT, 12, LX], F32) as swp, S.stage(nc) as block:
                @block.sync
                def _(sp):
                    half = ROT // 2
                    sp.dma_start(swp[0:half, :, :], qk[half:ROT, :, :]).then_inc(*S.landed.one)
                    sp.dma_start(swp[half:ROT, :, :], qk[0:half, :, :]).then_inc(*S.landed.one)

                @block.vector
                def _(dve):
                    dve.wait_ge(S.landed.sem, S.landed.at(2))
                    cos = M.rot[:, 0:1, :].to_broadcast([ROT, 12, LX])
                    sin = M.rot[:, 1:2, :].to_broadcast([ROT, 12, LX])
                    dve.tensor_tensor(swp[:, :, :], swp[:, :, :], sin, ALU.mult)
                    chain(dve, S.dve, dve.tensor_tensor(qk[0:ROT, :, :], qk[0:ROT, :, :], cos, ALU.mult))
                    dve.tensor_tensor(qk[0:ROT, :, :], qk[0:ROT, :, :], swp[:, :, :], ALU.add)

            def every4(ap, r):
                return ap.rearrange("p (m r) -> p m r", r=4)[:, :, r]

            def score(pe, hd, r, acc):
                pe.matmul(acc[:, 0:LX], every4(qk[:, hd, :], r), qk[:, 2 + hd, :], start=True, stop=True)
                for g in (1, 2):
                    mm = pe.matmul(acc[:, LX + (g - 1) * P:LX + g * P], every4(qk[:, 4 * g + hd, :], r),
                                   every4(qk[:, 4 * g + 2 + hd, :], r), start=True, stop=True)
                return mm

            def mask(r):
                return [(0, LX, masks[:, r * LX:(r + 1) * LX]), (LX, T, masks[:, 4 * LX:4 * LX + 2 * P])]

            def mix(pe, hd, acc, p_t):
                c = slice(hd * P, (hd + 1) * P)
                for j in range(4):
                    pe.matmul(acc, v[:, 0, j, c], p_t[:, j, :], start=j == 0, stop=False, skip_group_check=True)
                for g in (1, 2):
                    for r in range(4):
                        mm = pe.matmul(acc[:, r * P:(r + 1) * P], v[:, g, r, c], p_t[:, 3 + g, r * P:(r + 1) * P],
                                       start=False, stop=g == 2, skip_group_check=True)
                return mm

            def store(dve, hd, acc):
                dst = M.y[:, bass.ds(i * 2 + hd, 1), :].rearrange("p a (m r) -> p r (a m)", r=4)
                return dve.tensor_copy(dst, acc.rearrange("p (r m) -> p r m", r=4))

            attention(nc, S, M, 2, 4, 6, score, mask, mix, store)


LOOPS = {
    "recurrence": dict(weights=[2, 2], w_hi=4, w_lo=4, acc=18, by_act=8, by_dve=6, dve=5, act=6, pe=2, sq_act=2, summed=2, rstd=2,
                       scores=2, masked=2, probs=2, mixed=30),
    "dilated": dict(weights=[5, 4], w_hi=9, w_lo=9, acc=24, by_act=6, by_dve=18, landed=2, dve=1, scores=8, masked=8, maxed=8,
                    exped=8, recip=8, probs=8, turned=8, probs_t=8, mixed=2, stored=2),
}


def second_layer(nc, S, M, io, l):
    x = lambda k, a, b: M.x[:, k, a:b]
    y_ = lambda k, a, b: M.y[:, k, a:b]
    gx = [X_COLS]
    w = io["hgrn_w_in_2" if l == 0 else "attn_w_in_2"][0]
    w_out = io["hgrn_w_out_2" if l == 0 else "attn_w_out_2"][0]
    w_up, w_down = io["ffn_w_in_2"][l], io["ffn_w_out_2"][l]
    n1 = 6
    n_up = D_FF2 // UNIT

    def gate_cut(i, up, jobs=()):
        return cut(w_up, 0, D, i * UNIT + up * D_FF2, UNIT, jobs)

    with ExitStack() as ctx:
        M.split = Split(ctx, nc, f"u{l}", [P, KD, LX])
        norm(nc, S, M, x, KD, D, gx, None, lambda k, a: M.gain2[:, 4 * l, k:k + 1],
             lambda k, a: M.mod(2 + l, 0, k, 0), split=M.split)
        if l == 0:
            first = [cut(w, 0, D, D), cut(w, 0, D, 0)]
        else:
            first = [cut(w, 0, D, 0), cut(w, 0, D, D)]
        fetch(nc, S, M, first)
        (recurrence if l == 0 else dilated)(nc, S, M, io)
        M.loaded, M.stale = 0, True
    with ExitStack() as ctx:
        h = Split(ctx, nc, f"mix2{l}", [P, KD, LX])
        divide(nc, S, M, [M.y[:, b, :] for b in range(KD)], h, 0, LX)
        units = square_cuts(w_out, lambda c: feature_jobs(
            h, KD, [(2 * c, 0), (2 * c + 1, P)], gx, "dve", lambda e, acc, b, g: e.tensor_copy(M.y[:, b, :], acc)))
        project(nc, S, M, lambda i: units, ahead=[gate_cut(0, 0), gate_cut(0, 1)])
    norm(nc, S, M, y_, KD, D, gx, None, lambda k, a: M.gain2[:, 4 * l + 1, k:k + 1], add=x)

    with ExitStack() as ctx:
        h = Split(ctx, nc, f"uf{l}", [P, KD, LX])
        hid = Split(ctx, nc, f"fh{l}", [P, 2 * n1, LX])
        gate = ctx.enter_context(nc.sbuf_tensor(f"gate{l}", [P, 2, LX], F32))
        norm(nc, S, M, x, KD, D, gx, None, lambda k, a: M.gain2[:, 4 * l + 2, k:k + 1],
             lambda k, a: M.mod(2 + l, 3, k, 0), split=h)

        def silu(e, acc, b, _):
            return e.activation(gate[:, b, :], acc, ACT.Silu)

        def times(e, acc, b, _):
            return e.tensor_tensor(M.v[:, 0, :], gate[:, b, :], acc, ALU.mult)

        for part, (u0, nu) in enumerate([(0, n1), (n1, n_up - n1)]):
            def pair(i, u0=u0):
                js = feature_jobs(h, KD, [(0, 0), (1, P)], gx, "act", silu)
                ju = feature_jobs(h, KD, [(0, 0), (1, P)], gx, "dve", times, kind="times", hidden=hid)
                for b in range(2):
                    ju[b].after = (b,)
                    js[b].after = (b - 2,)
                    ju[b].dst = lambda t, b=b: t[:, bass.ds(i * 2 + b, 1), :].rearrange("p a t -> p (a t)")
                return [gate_cut(i + u0, 0, js), gate_cut(i + u0, 1, ju)]

            kt = 2 * nu

            def down(c, jobs=()):
                return cut(w_down, 2 * u0 * P, (2 * u0 + kt) * P, c * P, P, jobs)

            project(nc, S, M, pair, turns=nu, ahead=[down(0), down(1)])

            def keep(e, acc, b, g, part=part):
                if part == 0:
                    return e.tensor_copy(M.y[:, b, :], acc)
                return e.tensor_tensor(M.y[:, b, :], M.y[:, b, :], acc, ALU.add)

            units = [down(c, feature_jobs(hid, kt, [(c, 0)], gx, "dve", keep)) for c in range(KD)]
            project(nc, S, M, lambda i: units, ahead=[gate_cut(n1, 0), gate_cut(n1, 1)] if part == 0 else None)
    norm(nc, S, M, y_, KD, D, gx, None, lambda k, a: M.gain2[:, 4 * l + 3, k:k + 1], add=x)



VECTORS = [
    ("c", 8), ("c_ctx", 8), ("c_2", 8), ("b_mod", 96), ("ada_b_2", 96), ("norm1_g", 16), ("norm2_g", 16),
    ("q_norm_g", 6), ("kv_norm_g", 4), ("hy_conv_w", 36), ("hy_conv_b", 12), ("hy_d", 4), ("final_norm_g", 8),
    ("norm_g_2", 64), ("hgrn_lower_bounds_2", 8), ("hgrn_norm_g_2", 8), ("hy_b1", 2), ("hy_freq", 2), ("hy_b2", 2),
]
FIRST_ROW = dict(zip((n for n, _ in VECTORS), np.cumsum([0] + [k for _, k in VECTORS])[:-1].tolist()))
N_ROWS = sum(k for _, k in VECTORS)
ROWS_OF = dict(VECTORS)


def fetch(nc, S, M, units):
    with S.stage(nc) as block:
        @block.sync
        def _(sp):
            for u, unit in enumerate(units):
                sp.dma_start(unit.place(M.ring[:, u, :]), unit.src).then_inc(*S.weights[u].one)
    M.loaded = len(units)


class Memory:
    def __init__(self, nc, ctx):
        def sb(name, shape, dt=F32):
            return ctx.enter_context(nc.sbuf_tensor(name, shape, dt))

        self.ps = ctx.enter_context(nc.psum_tensor("ps", [P, BANKS, 512], F32))
        self.ring = sb("ring", [P, RING, SLOT])
        self.x = sb("x_res", [P, KD, T])
        self.f = sb("f", [P, 2, T])
        self.v = self.f[:, :, 0:512]
        self.loaded, self.stale = 0, False
        self.count = 0
        self.sq = sb("sq", [P, 2, T])
        self.tmp = self.sq
        self.rs = sb("rs", [P, T])
        self.vec = sb("vec", [P, 4, P])
        self.mods = sb("mods", [P, 2 * DEPTH, 48, 2])
        self.gain = sb("gain", [P, 4, 2, KD])
        self.gain2 = sb("gain2", [P, 8, KD])
        self.lower = sb("lower", [P, 2, KD])
        self.hgain = sb("hgain", [P, KD])
        self.ident = sb("ident", [P, P])
        self.ones = sb("ones", [P, P])
        self.eps = sb("eps", [P, 1])
        self.nmax, self.esum, self.rsum = sb("nmax", [P, 4]), sb("esum", [P, 4]), sb("rsum", [P, 4])

    def fresh(self):
        self.count += 1
        return self.count

    def col(self, name, l=0, k=0, n=1):
        c = FIRST_ROW[name] + l * (ROWS_OF[name] // 2) + k if ROWS_OF[name] and l else FIRST_ROW[name] + k
        return self.vec[:, :, :].rearrange("p a b -> p (a b)")[:, c:c + n]

    def mod(self, s, m, k, side):
        return self.mods[:, s, m * KD + k, side:side + 1]


def vectors(nc, S, M, io):
    with nc.sbuf_tensor("rows", [P, 4, P], F32) as rows:
        with S.stage(nc) as block:
            @block.gpsimd
            def _(pool):
                pool.memset(rows[:, :, :], 0.0)
                pool.memset(M.ones[:, :], 1.0)
                pool.memset(M.eps[:, :], EPS)
                pool.memset(M.nmax[:, :], 0.0)
        pairs = [(M.ident[:, :], io["ident"])]
        for name, n in VECTORS:
            src = io[name]
            if len(src.shape) > 1:
                src = src.rearrange({2: "a b -> (a b)", 3: "a b c -> (a b c)"}[len(src.shape)])
            wd = 64 if name in ("hy_b1", "hy_freq", "hy_b2") else P
            src = src.rearrange("(r w) -> r w", w=wd)
            r = 0
            while r < n:
                row = FIRST_ROW[name] + r
                m = min(n - r, P - row % P)
                pairs.append((rows[row % P:row % P + m, row // P, 0:wd], src[r:r + m, :]))
                r += m
        load(nc, S, pairs)
        with S.stage(nc) as block:
            @block.tensor
            def _(pe):
                for t in range(4):
                    tr = pe.transpose(M.ps[:, 0, t * P:(t + 1) * P], rows[:, t, :], M.ident[:, :])
                tr.then_inc(*S.pe.one)

            @block.scalar
            def _(act):
                act.wait_ge(S.pe.sem, S.pe.at(1))
                act.activation(M.vec[:, :, :].rearrange("p a b -> p (a b)"), M.ps[:, 0, :], ACT.Copy)\
                    .then_inc(*S.act.one)


def modulations(nc, S, M, io):
    slots, turns = 6, 4
    sets = [("w_mod", 0, 0, 2), ("w_mod", 1, 0, 2), ("ada_w_2", 0, 2, 1), ("ada_w_2", 1, 2, 1)]
    with ExitStack() as ctx:
        cond = ctx.enter_context(nc.sbuf_tensor("cond", [P, KD, 3], F32))
        wm = ctx.enter_context(nc.sbuf_tensor("wm", [P, slots, KD, UNIT], F32))
        rows = ctx.enter_context(nc.sbuf_tensor("mod_rows", [2, 2 * DEPTH, 6 * D], F32))
        turned = ctx.enter_context(nc.sbuf_tensor("mod_tiles", [96, 2 * DEPTH, P], F32))
        landed = [Signal(nc, f"modulation_weights_{u}", 16) for u in range(slots)]
        with S.stage(nc) as block:
            @block.scalar
            def _(act):
                act.activation(cond[:, :, :].rearrange("p k s -> p s k"),
                               M.col("c", n=24).rearrange("p (s k) -> p s k", s=3), ACT.Silu)
        with S.stage(nc) as block:
            @block.sync
            def _(sp):
                for s, (name, l, _, _) in enumerate(sets):
                    def turn(i, first):
                        for u in range(slots):
                            if not first:
                                sp.wait_ge(S.acc.sem, S.acc.at((i + (s * turns - 1)) * slots + u + 1))
                            sp.dma_start(wm[:, u, :, :], cut(io[name][l], 0, D, i * (slots * UNIT) + u * UNIT).src)\
                                .then_inc(*landed[u].up)
                    if s == 0:
                        turn(0, True)
                        with sp.Fori(1, turns) as i:
                            turn(i, False)
                    else:
                        with sp.Fori(0, turns) as i:
                            turn(i, False)

            @block.tensor
            def _(pe):
                for s, (_, _, c0, n) in enumerate(sets):
                    def turn(i, first):
                        for u in range(slots):
                            pe.wait_ge(landed[u].sem, landed[u].at(i + (s * turns + 1)))
                            if not first:
                                pe.wait_ge(S.by_act.sem, S.by_act.at((i + (s * turns - 1)) * slots + u + 1))
                            for k in range(KD):
                                mm = pe.matmul(M.ps[0:n, u, 0:UNIT], cond[:, k, c0:c0 + n], wm[:, u, k, :],
                                               start=k == 0, stop=k == KD - 1)
                            mm.then_inc(*S.acc.up)
                    if s == 0:
                        turn(0, True)
                        with pe.Fori(1, turns) as i:
                            turn(i, False)
                    else:
                        with pe.Fori(0, turns) as i:
                            turn(i, False)

            @block.scalar
            def _(act):
                for s, (_, _, _, n) in enumerate(sets):
                    with act.Fori(0, turns) as i:
                        for u in range(slots):
                            act.wait_ge(S.acc.sem, S.acc.at((i + s * turns) * slots + u + 1))
                            act.activation(rows[0:n, s, bass.ds((i * slots + u) * UNIT, UNIT)], M.ps[0:n, u, 0:UNIT],
                                           ACT.Copy).then_inc(*S.by_act.up)

            S.acc.sent = S.by_act.sent = len(sets) * turns * slots
        with S.stage(nc) as block:
            @block.sync
            def _(sp):
                for s, (_, _, _, n) in enumerate(sets):
                    for c in range(n):
                        sp.dma_start(turned[48 * c:48 * c + 48, s, :], rows[c:c + 1, s, :].rearrange(
                            "a (b p) -> a b p", p=P)).then_inc(*S.landed.one)

            @block.tensor
            def _(pe):
                at = 0
                for s, (_, _, _, n) in enumerate(sets):
                    at += n
                    if s == len(sets) - 1:
                        pe.wait_ge(S.landed.sem, S.landed.at(at))
                for s, (_, _, _, n) in enumerate(sets):
                    pe.transpose(M.ps[:, s, 0:48 * n], turned[0:48 * n, s, :], M.ident[0:48 * n, 0:48 * n])\
                        .then_inc(*S.pe.one)

            @block.vector
            def _(dve):
                for s, (_, l, _, n) in enumerate(sets):
                    dve.wait_ge(S.pe.sem, S.pe.at(s + 1))
                    bias = M.col("b_mod" if s < DEPTH else "ada_b_2", l, n=48)
                    dve.tensor_tensor(M.mods[:, s, :, 0:n], M.ps[:, s, 0:48 * n].rearrange("p (n b) -> p b n", n=n),
                                      bias.unsqueeze(2).to_broadcast([P, 48, n]), ALU.add).then_inc(*S.by_dve.one)


def gains(nc, S, M):
    vec = M.vec[:, :, :].rearrange("p a b -> p (a b)")
    with nc.sbuf_tensor("lb", [P, 4, KD], F32) as lb, S.stage(nc) as block:
        @block.vector
        def _(dve):
            def gain(dst, s, m, side, g):
                dve.scalar_tensor_tensor(dst, M.mods[:, s, m * KD:(m + 1) * KD, side], 1.0, g, ALU.add, ALU.mult)

            for l in range(DEPTH):
                for j, name in enumerate(("norm1_g", "norm2_g")):
                    for side in range(2):
                        gain(M.gain[:, 2 * l + j, side, :], l, 1 + 3 * j, side, M.col(name, l, n=KD))
                for j, m in enumerate((1, 2, 4, 5)):
                    gain(M.gain2[:, 4 * l + j, :], 2 + l, m, 0, M.col("norm_g_2", l, j * KD, n=KD))
            dve.tensor_copy(M.hgain[:, :], M.col("hgrn_norm_g_2", n=KD))
            b = M.col("hgrn_lower_bounds_2", n=KD)
            chain(dve, S.dve, dve.tensor_tensor(lb[:, 0, :], b, b, ALU.subtract))
            dve.wait_ge(S.act.sem, S.act.at(1))
            chain(dve, S.dve, dve.reciprocal(lb[:, 2, :], lb[:, 1, :]))
            chain(dve, S.dve, dve.tensor_tensor(lb[:, 3, :], lb[:, 1, :], lb[:, 2, :], ALU.mult))
            chain(dve, S.dve, dve.tensor_tensor(M.lower[:, 0, :], lb[:, 3, :], lb[:, 3, :], ALU.subtract))
            dve.tensor_scalar(M.lower[:, 1, :], M.lower[:, 0, :], -1.0, 1.0, ALU.mult, ALU.add)

        @block.scalar
        def _(act):
            act.wait_ge(S.dve.sem, S.dve.at(1))
            act.activation(lb[:, 1, :], lb[:, 0, :], ACT.Exp).then_inc(*S.act.one)


def rotary_tables(nc, S, M, io):
    with ExitStack() as ctx:
        pos = ctx.enter_context(nc.sbuf_tensor("pos", [ROT, LX], I32))
        ang = ctx.enter_context(nc.sbuf_tensor("ang", [ROT, 4, LX], F32))
        par = ctx.enter_context(nc.sbuf_tensor("par", [ROT, 2], F32))
        load(nc, S, [(pos[:, :], io["positions_2"].to_broadcast([ROT, LX])), (par[:, :], io["rot_params"])])
        with S.stage(nc) as block:
            @block.vector
            def _(dve):
                chain(dve, S.dve, dve.tensor_copy(ang[:, 0, :], pos[:, :]))
                chain(dve, S.dve, dve.tensor_scalar(ang[:, 0, :], ang[:, 0, :], par[:, 0:1], None, ALU.mult))
                reduce_angle(dve, S, ang[:, 0, :], ang[:, 1, :])
                chain(dve, S.dve, dve.tensor_scalar(ang[:, 2, :], ang[:, 0, :], math.pi / 2, None, ALU.add))
                chain(dve, S.dve, dve.tensor_scalar(ang[:, 1, :], ang[:, 2, :], math.pi, TWO_PI, ALU.is_gt, ALU.mult))
                chain(dve, S.dve, dve.tensor_tensor(ang[:, 2, :], ang[:, 2, :], ang[:, 1, :], ALU.subtract))
                dve.tensor_scalar(ang[:, 2, :], ang[:, 2, :], SIN_MAX, -SIN_MAX, ALU.min, ALU.max)\
                    .then_inc(*S.by_dve.one)
                dve.wait_ge(S.act.sem, S.act.at(1))
                dve.tensor_scalar(M.rot[:, 1, :], ang[:, 3, :], par[:, 1:2], None, ALU.mult)

            @block.scalar
            def _(act):
                act.wait_ge(S.by_dve.sem, S.by_dve.at(1))
                act.activation(M.rot[:, 0, :], ang[:, 2, :], ACT.Sin)
                act.activation(ang[:, 3, :], ang[:, 0, :], ACT.Sin).then_inc(*S.act.one)


def enter(nc, S, M, io):
    with nc.sbuf_tensor("tok_in", [P, 6, D], F32) as tok:
        load(nc, S, [(tok[:, 0:4, :], io["x"][0].rearrange("(t p) d -> p t d", p=P)),
                     (tok[:, 4:6, :], io["ctx"][0].rearrange("(t p) d -> p t d", p=P))])
        with S.stage(nc) as block:
            @block.tensor
            def _(pe):
                for t in range(T // P):
                    for half in range(2):
                        n = 2 * t + half
                        if n >= BANKS:
                            pe.wait_ge(S.by_act.sem, S.by_act.at(n - BANKS + 1))
                        for k in range(4):
                            c = (4 * half + k) * P
                            tr = pe.transpose(M.ps[:, n % BANKS, k * P:(k + 1) * P], tok[:, t, c:c + P], M.ident[:, :])
                        tr.then_inc(*S.pe.one)

            @block.scalar
            def _(act):
                for n in range(2 * T // P):
                    t, half = divmod(n, 2)
                    act.wait_ge(S.pe.sem, S.pe.at(n + 1))
                    act.activation(M.x[:, 4 * half:4 * half + 4, t * P:(t + 1) * P],
                                   M.ps[:, n % BANKS, :].rearrange("p (k t) -> p k t", k=4), ACT.Copy)\
                        .then_inc(*S.by_act.one)


def leave(nc, S, M, io):
    dst = io["out"][0].rearrange("(t p) d -> t p d", p=P)
    with nc.sbuf_tensor("tok_out", [P, 4, D], F32) as tok, S.stage(nc) as block:
        @block.tensor
        def _(pe):
            for n in range(8):
                t, half = divmod(n, 2)
                for k in range(4):
                    tr = pe.transpose(M.ps[:, n, k * P:(k + 1) * P], M.x[:, 4 * half + k, t * P:(t + 1) * P],
                                      M.ident[:, :])
                tr.then_inc(*S.pe.one)

        @block.scalar
        def _(act):
            for n in range(8):
                t, half = divmod(n, 2)
                act.wait_ge(S.pe.sem, S.pe.at(n + 1))
                act.activation(tok[:, t, half * 512:(half + 1) * 512], M.ps[:, n, :], ACT.Copy)\
                    .then_inc(*S.by_act.one)

        @block.sync
        def _(sp):
            for t in range(4):
                sp.wait_ge(S.by_act.sem, S.by_act.at(2 * t + 2))
                sp.dma_start(dst[t], tok[:, t, :]).then_inc(*S.out.one)
            sp.wait_ge(S.out.sem, S.out.at(4))


def program(nc, io):
    S = Signals(nc)
    with ExitStack() as ctx:
        M = Memory(nc, ctx)
        vectors(nc, S, M, io)
        modulations(nc, S, M, io)
        gains(nc, S, M)
        enter(nc, S, M, io)
        for l in range(DEPTH):
            first_layer(nc, S, M, io, l)
        x = lambda k, a, b: M.x[:, k, a:b]
        norm(nc, S, M, x, KD, D, [X_COLS], x, lambda k, a: M.col("final_norm_g", k=k))
        M.y = ctx.enter_context(nc.sbuf_tensor("y", [P, KD, LX], F32))
        M.rot = ctx.enter_context(nc.sbuf_tensor("rot", [ROT, 2, LX], F32))
        M.resets = ctx.enter_context(nc.sbuf_tensor("resets", [P, LX], F32))
        M.causal = ctx.enter_context(nc.sbuf_tensor("causal", [P, P], F32))
        load(nc, S, [(M.resets[:, :], io["chunk_resets"]), (M.causal[:, :], io["chunk_causal"])])
        rotary_tables(nc, S, M, io)
        for l in range(DEPTH):
            second_layer(nc, S, M, io, l)
        leave(nc, S, M, io)


def tables():
    f = np.float64
    out = {"ident": np.eye(P)}

    def by_tile(a):
        return a.reshape(a.shape[0] // P, P, *a.shape[1:]).swapaxes(0, 1)

    inv = 10000.0 ** (-np.arange(0, 16, 2, dtype=np.float32) / np.float32(16))
    t = np.arange(LX)
    rope = np.zeros((P, 2, LX))
    swap = np.zeros((P, P))
    for axis, pos in enumerate((t // 64, t % 64)):
        ang = (pos.astype(np.float32)[None] * inv.astype(np.float32)[:, None]).astype(np.float32).astype(f)
        for half in range(2):
            r = NOPE + 16 * axis + 8 * half
            rope[r:r + 8, 0] = np.cos(ang)
            rope[r:r + 8, 1] = np.sin(ang) * (1 if half else -1)
            other = NOPE + 16 * axis + 8 * (1 - half)
            for j in range(8):
                swap[other + j, r + j] = 1.0
    out["rope_tables"], out["rope_swap"] = rope, swap

    w = np.arange(64)
    a = 2 * np.pi * np.outer(w, w) / 64
    chan = np.zeros((P, 2, P))
    for g in range(2):
        s = slice(64 * g, 64 * g + 64)
        chan[s, 0, s], chan[s, 1, s] = np.cos(a), np.sin(a)
    out["fnet_channels"] = chan.reshape(P, 2 * P)
    deltas = np.abs(np.linspace(math.log(1e-2) / 1.5, math.log(1e-2) / 0.3, HY))
    for n in (LX, LC):
        i = np.arange(n)
        a = 2 * np.pi * (np.outer(i, i) % n) / n
        out[f"fnet_tokens_{n}"] = by_tile(np.stack([np.cos(a), -np.sin(a)], 1)) / math.sqrt(64 * n)
        a = 2 * np.pi * np.outer(i, i + 0.5) / (2 * n)
        out[f"hy_tk_{n}"] = by_tile(np.stack([np.cos(a), np.sin(a)], 1))
        a = 2 * np.pi * np.outer(i + 0.5, i + 0.5) / (2 * n)
        out[f"hy_ta_{n}"] = by_tile(np.stack([np.cos(a), np.sin(a)], 1))
        tt = np.linspace(0.0, 1.0, n)[:, None]
        bands = (EMB - 1) // 2
        fr = np.linspace(1e-4, bands - 1, bands).astype(np.float32)
        ang = (np.float32(2.0 * math.pi) * np.arange(n, dtype=np.float32)[:, None] / np.float32(n)) * fr
        ang = ang.astype(np.float32).astype(f)
        out[f"hy_emb_{n}"] = np.concatenate([tt, np.cos(ang), -np.sin(ang)], -1).T
        dec = np.exp(-tt * deltas)
        both = np.concatenate([dec, dec], 1)
        both[0, HY:] = 0.0
        out[f"hy_decay_{n}"] = by_tile(both)

    out["chunk_resets"] = np.broadcast_to((t % CHUNK != 0).astype(f), (P, LX))
    s, c = np.arange(P)[:, None], np.arange(P)[None]
    out["chunk_causal"] = ((s // CHUNK == c // CHUNK) & (s <= c)).astype(f)
    inv2 = 500000.0 ** (-np.arange(0, ROT, 2, dtype=np.float32) / np.float32(ROT))
    sign = np.repeat([-1.0, 1.0], ROT // 2)
    out["rot_params"] = np.stack([np.tile(inv2, 2), sign], 1)
    masks = np.zeros((P, 4 * LX + 2 * P))
    m = np.arange(P)
    for r in range(4):
        dist = (r + 4 * m)[:, None] - t[None]
        masks[:, r * LX:(r + 1) * LX] = np.where((dist >= 0) & (dist <= 128), 0.0, -1e30)
    causal = m[:, None] >= m[None]
    masks[:, 4 * LX:4 * LX + P] = np.where(causal, 0.0, -1e30)
    masks[:, 4 * LX + P:] = np.where(causal & (m[:, None] % 4 == m[None] % 4), 0.0, -1e30)
    out["attn_masks"] = masks
    return {k: np.ascontiguousarray(v.astype(np.float32)) for k, v in out.items()}


def kernel(**inputs):
    import concourse.bacc as bacc
    from concourse.bass_utils import run_bass_kernel_spmd

    nc = bacc.Bacc("TRN2", target_bir_lowering=False, num_devices=1)
    arrays, io = {}, {}
    for name, a in {**inputs, **tables()}.items():
        a = np.ascontiguousarray(a)
        arrays[f"in_{name}"] = a
        io[name] = nc.dram_tensor(f"in_{name}", a.shape, mybir.dt.from_np(a.dtype), kind="ExternalInput").ap()
    io["out"] = nc.dram_tensor("out", (1, LX, D), F32, kind="ExternalOutput").ap()
    program(nc, io)
    r = run_bass_kernel_spmd(nc, [arrays], core_ids=[0])
    return r.results[0]["out"]
```

```python
import math
from contextlib import ExitStack, contextmanager

import numpy as np

import concourse.bass as bass
from concourse import mybir

F32 = mybir.dt.float32
F32R = mybir.dt.float32r
I32 = mybir.dt.int32
ALU = mybir.AluOpType
ACT = mybir.ActivationFunctionType
AX = mybir.AxisListType.X

P = 128
D = 1024
KD = D // P
LX, LC = 512, 256
T = LX + LC
X_COLS, C_COLS = (0, LX), (LX, T)
DEPTH = 2
EPS = 1e-6

HEADS, NOPE, ROPE, VDIM = 8, 64, 32, 64
QK = NOPE + ROPE
Q_LORA, KV_LORA = 384, 256
OFF_KV = Q_LORA
OFF_KR = OFF_KV + KV_LORA
OFF_F = OFF_KR + ROPE
OFF_H = OFF_F + 256
IN_W = OFF_H + 768
HY = 256
D_FF = 4 * D
EMB, ORDER = 33, 64

H2 = 8
CHUNK = 32
D_FF2 = 2816
ROT = 32
GROUPS2 = 3

UNIT = 256
RING = 2
SLOT = KD * UNIT
BANKS = 8

TWO_PI = 2.0 * math.pi
PI1 = 6.28125
PI2 = float(np.float32(round((TWO_PI - PI1) * 2 ** 19) / 2 ** 19))
PI3 = TWO_PI - PI1 - PI2
ROUND = 1.5 * 2.0 ** 23
SIN_MAX = 3.1415925


class Signal:

    def __init__(self, nc, name, step=1):
        self.sem = nc.alloc_semaphore(name)
        self.step, self.start, self.sent = step, 0, 0
        self.turn = None

    @property
    def one(self):
        self.sent += 1
        return self.sem, self.step

    def at(self, n):
        value = (self.start + n) * self.step
        return value if self.turn is None else value + self.turn[0] * (self.turn[1] * self.step)

    @property
    def up(self):
        return self.sem, self.step

    def settle(self):
        self.start += self.sent
        self.sent = 0


class Signals:
    def __init__(self, nc):
        self.named = {}

        def signal(key, name, step=1):
            self.named[key] = Signal(nc, name, step)
            return self.named[key]

        self.weights = [Signal(nc, f"weights_landed_{s}", 16) for s in range(RING)]
        self.w_hi = signal("w_hi", "weights_high_parts")
        self.w_lo = signal("w_lo", "weights_low_parts")
        self.value = signal("value", "hidden_value_ready")
        self.side = [Signal(nc, f"side_weights_landed_{s}", 16) for s in range(2)]
        self.swappable = signal("swappable", "halves_ready_for_change")
        self.swapped = signal("swapped", "halves_changed_places", 16)
        self.roped = signal("roped", "rotary_added")
        self.roped_part = signal("roped_part", "rotary_products")
        self.side_step = signal("side_step", "side_products_by_dve")
        self.side_acc = signal("side_acc", "side_products_added_up")
        self.side_sum = signal("side_sum", "side_columns_summed")
        self.side_done = signal("side_done", "side_columns_stored")
        self.sq_add = signal("sq_add", "squares_added")
        self.hi = signal("hi", "hidden_high_part")
        self.lo = signal("lo", "hidden_low_part")
        self.acc = signal("acc", "accumulated")
        self.by_act = signal("by_act", "evacuated_by_act")
        self.by_dve = signal("by_dve", "evacuated_by_dve")
        self.landed = signal("landed", "tables_landed", 16)
        self.dve = signal("dve", "dve_step")
        self.act = signal("act", "act_step")
        self.pe = signal("pe", "pe_step")
        self.sq_act = signal("sq_act", "squares_by_act")
        self.sq_dve = signal("sq_dve", "squares_by_dve")
        self.summed = signal("summed", "squares_summed")
        self.rstd = signal("rstd", "rstd_ready")
        self.normed = signal("normed", "normed")
        self.scaled = signal("scaled", "scaled")
        self.scores = signal("scores", "scores_ready")
        self.masked = signal("masked", "scores_masked")
        self.maxed = signal("maxed", "max_ready")
        self.exped = signal("exped", "exp_ready")
        self.recip = signal("recip", "reciprocal_ready")
        self.probs = signal("probs", "probs_ready")
        self.turned = signal("turned", "probs_transposed")
        self.probs_t = signal("probs_t", "transposed_probs_stored")
        self.mixed = signal("mixed", "values_mixed")
        self.stored = signal("stored", "heads_stored")
        self.out = signal("out", "output_stored", 16)

    def all(self):
        return self.weights + self.side + list(self.named.values())

    @contextmanager
    def stage(self, nc):
        with nc.Block() as block:
            yield block
        for s in self.all():
            s.settle()

    @contextmanager
    def loop(self, nc, n, **per_turn):
        before = {s: s.start for s in self.all()}
        strides = {}
        for name, k in per_turn.items():
            for j, s in enumerate(self.weights if name == "weights" else [self.named[name]]):
                strides[s] = k[j] if name == "weights" else k
        with nc.Fori(0, n) as i:
            for s, k in strides.items():
                s.turn = (i, k)
            yield i
        made = {s.sem.name: s.start - before[s] for s in before if s.start != before[s]}
        for s in before:
            assert s.start - before[s] == strides.get(s, 0), made
            s.turn = None
            s.start = before[s] + n * strides.get(s, 0)


class Split:

    def __init__(self, ctx, nc, name, shape):
        self.hi = ctx.enter_context(nc.sbuf_tensor(name + "_hi", shape, F32R))
        self.lo = ctx.enter_context(nc.sbuf_tensor(name + "_lo", shape, F32R))
        self.parts = (self.hi, self.lo)


class Side:

    def __init__(self, w, s, c0, n, bias):
        self.w, self.s, self.c0, self.n, self.bias = w, s, c0, n, bias


class Unit:

    def __init__(self, src, kt, n, jobs):
        self.src, self.kt, self.n, self.jobs = src, kt, n, jobs

    def place(self, slot):
        return slot[:, 0:self.kt * self.n].rearrange("p (k n) -> p k n", k=self.kt)

    def pieces(self, slot):
        if not isinstance(self.src, tuple):
            return [(self.place(slot), self.src)]
        to = self.place(slot).rearrange("p k (s n) -> p s k n", s=2)
        return [(to[:, s], src) for s, src in enumerate(self.src)]


class Job:

    def __init__(self, w, a, acts, kt, m, n, engine, evac, kind="keep", hidden=None, dst=None, needs=(),
                 after=(), weights_first=True, square=None, where=None, make=None, taken=None):
        self.where = where
        self.make, self.taken = make, taken
        self.w, self.a, self.acts, self.kt, self.m, self.n = w, a, acts, kt, m, n
        self.engine, self.evac, self.kind, self.hidden, self.dst = engine, evac, kind, hidden, dst
        self.needs, self.after, self.weights_first = needs, after, weights_first
        self.square = square


def project(nc, S, M, units_of, turns=1, ahead=None, sides=(), beside=None):
    units = units_of(0)
    nu = len(units)
    assert turns == 1 or nu % RING == 0
    assert S.lo.start > 0
    parts = len(units[0].src) if isinstance(units[0].src, tuple) else 1
    jobs = [j for u in units for j in u.jobs]
    nj = len(jobs)
    ends = np.cumsum([len(u.jobs) for u in units]).tolist()
    starts = [0] + ends[:-1]
    nth, split_nth, count, n_split = [], [], {"act": 0, "dve": 0}, 0
    for j in jobs:
        count[j.engine] += 1
        nth.append(count[j.engine])
        split_nth.append(n_split)
        n_split += j.kind != "keep"
    done = {"act": S.by_act, "dve": S.by_dve}
    banks = beside.banks if beside else BANKS // 2 if sides else BANKS
    assert turns == 1 or nj % banks == 0 or banks % nj == 0
    n_side = nu - 2
    squares = [n for n, j in enumerate(jobs) if j.square]
    columns = [(t, side, c) for t, side in enumerate(sides) for c in range(side.n)]
    steps = n_side * (KD - 1) * len(columns)
    loaded, stale = M.loaded, M.stale
    M.loaded, M.stale = 0, False

    def wait_job(eng, i, j):
        if j < 0 and turns == 1:
            return
        e = jobs[j % nj].engine
        c = nth[j % nj] - (count[e] if j < 0 else 0)
        eng.wait_ge(done[e].sem, done[e].at(i * count[e] + c))

    def run(eng, turn, n=turns):
        if n > 2 and beside:
            turn(0, False)
            with eng.Fori(1, n - 1) as i:
                turn(i, False)
        elif n > 2:
            with eng.Fori(0, n - 1) as i:
                turn(i, False)
        elif n == 2:
            turn(0, False)
        turn(n - 1, True)

    with ExitStack() as ctx:
        wide = max(u.kt * u.n for u in units)
        w = Split(ctx, nc, f"w{M.fresh()}", [P, 2, wide])
        if sides:
            sw = ctx.enter_context(nc.sbuf_tensor(f"side_w{M.fresh()}", [P, len(sides), KD, UNIT], F32))
            sa = ctx.enter_context(nc.sbuf_tensor(f"side_a{M.fresh()}", [P, 2, len(columns), UNIT], F32))

        with S.stage(nc) as block:
            @block.sync
            def _(sp):
                def fetch(unit, u):
                    for to, src in unit.pieces(M.ring[:, u % RING, :]):
                        sp.dma_start(to, src).then_inc(*S.weights[u % RING].up)

                if stale:
                    for weights in S.weights:
                        sp.wait_ge(weights.sem, weights.at(0))
                for u in range(loaded, min(RING, nu)):
                    fetch(units_of(0)[u], u)

                def fetch_sides(i, u):
                    for half, r in enumerate((slice(0, KD // 2), slice(KD // 2, KD))):
                        if u or not isinstance(i, int) or i:
                            if half:
                                sp.wait_ge(S.side_acc.sem, S.side_acc.at(i * n_side + u))
                            else:
                                step = ((u - 1) * (KD - 1) + KD // 2) * len(columns)
                                sp.wait_ge(S.side_step.sem, S.side_step.at(i * steps + step))
                        for t, side in enumerate(sides):
                            piece = cut(side.w, 0, D, i * (n_side * UNIT) + u * UNIT).src
                            sp.dma_start(sw[:, t, r, :], piece[:, r, :]).then_inc(*S.side[half].up)

                def turn(i, last):
                    here, there = units_of(i), None if last else units_of(i + 1)
                    for u in range(nu):
                        v = u + RING
                        if v < nu or not last:
                            sp.wait_ge(S.w_lo.sem, S.w_lo.at(i * nu + u + 1))
                            fetch(here[v] if v < nu else there[v - nu], u)
                        if beside:
                            beside.sync(sp, i, u)
                        if sides and 2 <= u < nu - 1:
                            fetch_sides(i, u - 1)
                        elif sides and u == nu - 1 and not last:
                            fetch_sides(i + 1, 0)
                if sides:
                    fetch_sides(0, 0)
                run(sp, turn)
                for u, unit in enumerate(ahead or []):
                    sp.wait_ge(S.w_lo.sem, S.w_lo.at(turns * nu))
                    fetch(unit, u)

            @block.tensor
            def _(pe):
                def sum_sides(i, u):
                    if u >= 4 or not isinstance(i, int) or i:
                        pe.wait_ge(S.side_done.sem, S.side_done.at(i * n_side + max(u - 3, 0)))
                    pe.wait_ge(S.side_acc.sem, S.side_acc.at(i * n_side + u - 1))
                    for n in range(len(columns)):
                        for b in range(2):
                            mm = pe.matmul(M.ps[:, banks + u % 2, 2 * n + b:2 * n + b + 1],
                                           sa[:, u % 2, n, b * P:(b + 1) * P], M.ones[:, 0:1], start=True, stop=True)
                    mm.then_inc(*S.side_sum.up)

                def turn(i, last):
                    n = 0
                    for u, unit in enumerate(units_of(i)):
                        pe.wait_ge(S.w_lo.sem, S.w_lo.at(i * nu + u + 1))
                        parts = [unit.place(t[:, u % 2, :]) for t in w.parts]
                        for first, j in enumerate(unit.jobs):
                            if first == 1 and u >= 2 and sides:
                                sum_sides(i, u)
                            wait_job(pe, i, n - banks)
                            for need in j.needs:
                                pe.wait_ge(S.lo.sem, S.lo.at(i * n_split + need))
                            acc = M.ps[0:j.m, n % banks, 0:j.n]
                            if j.make:
                                wait_job(pe, i, j.taken)
                                mm = j.make(pe, acc)
                            for k in range(0 if j.make else j.kt):
                                for wp, ap in ((0, 0), (0, 1), (1, 0)):
                                    ops = [j.w(parts[wp], k), j.a(j.acts.parts[ap], k)]
                                    lhsT, rhs = ops if j.weights_first else ops[::-1]
                                    mm = pe.matmul(acc, lhsT, rhs, start=k == 0 and wp == ap,
                                                   stop=k == j.kt - 1 and wp == 1)
                            mm.then_inc(*S.acc.up)
                            n += 1
                        if beside:
                            beside.tensor(pe, i, u)
                run(pe, turn)

            @block.scalar
            def _(act):
                def high(unit, i, u):
                    s = S.weights[u % RING]
                    act.wait_ge(s.sem, s.at((i * (nu // RING) + u // RING + (0 if u % RING < loaded else 1)) * parts))
                    if u >= 2 or not isinstance(i, int) or i > 0:
                        before = ends[u - 2] if u >= 2 else ends[u - 2 + nu] - nj
                        act.wait_ge(S.acc.sem, S.acc.at(i * nj + before))
                    act.activation(unit.place(w.hi[:, u % 2, :]), unit.place(M.ring[:, u % RING, :]), ACT.Copy)\
                        .then_inc(*S.w_hi.up)

                for u in range(min(2, nu)):
                    high(units_of(0)[u], 0, u)

                def turn(i, last):
                    n = 0
                    here = units_of(i)
                    for u, unit in enumerate(here):
                        for j in unit.jobs:
                            m = split_nth[n]
                            if j.engine == "act":
                                act.wait_ge(S.acc.sem, S.acc.at(i * nj + n + 1))
                                for other in j.after:
                                    wait_job(act, i, other)
                                acc = M.ps[0:j.m, n % banks, 0:j.n]
                                if j.kind == "relu2":
                                    v, v2 = M.sq[:, 1, 0:j.n], M.v[:, m % 2, 0:j.n]
                                    if m >= 2 or turns > 1:
                                        act.wait_ge(S.lo.sem, S.lo.at(i * n_split + m - 1))
                                    act.activation(v, acc, ACT.Relu).then_inc(*S.by_act.up)
                                    act.wait_ge(S.by_act.sem, S.by_act.at(i * count["act"] + nth[n]))
                                    act.activation(v2, v, ACT.Square).then_inc(*S.value.up)
                                    act.wait_ge(S.value.sem, S.value.at(i * n_split + m + 1))
                                    act.activation(j.dst(j.hidden.hi), v2, ACT.Copy).then_inc(*S.hi.up)
                                else:
                                    j.evac(act, acc).then_inc(*S.by_act.up)
                            elif j.kind == "times":
                                act.wait_ge(S.by_dve.sem, S.by_dve.at(i * count["dve"] + nth[n]))
                                act.activation(j.dst(j.hidden.hi), M.v[:, m % 2, 0:j.n], ACT.Copy).then_inc(*S.hi.up)
                            if j.square and last:
                                k = squares.index(n)
                                src, dst, fresh = j.square
                                act.wait_ge(S.by_dve.sem, S.by_dve.at(i * count["dve"] + nth[n]))
                                if not fresh:
                                    if k:
                                        act.wait_ge(S.sq_add.sem, S.sq_add.at(k))
                                    dst = M.sq[:, 0, 0:j.n]
                                act.activation(dst, src, ACT.Square).then_inc(*S.sq_act.up)
                            n += 1
                        if u + 2 < nu:
                            high(here[u + 2], i, u + 2)
                        elif not last:
                            high(units_of(i + 1)[u + 2 - nu], i + 1, u + 2 - nu)
                        if beside:
                            beside.scalar(act, i, u)
                run(act, turn)

            @block.vector
            def _(dve):
                def low(unit, i, u):
                    dve.wait_ge(S.w_hi.sem, S.w_hi.at(i * nu + u + 1))
                    dve.tensor_tensor(unit.place(w.lo[:, u % 2, :]), unit.place(M.ring[:, u % RING, :]),
                                      unit.place(w.hi[:, u % 2, :]), ALU.subtract).then_inc(*S.w_lo.up)

                def multiply_sides(i, u):
                    if u >= 2 or not isinstance(i, int) or i:
                        dve.wait_ge(S.side_sum.sem, S.side_sum.at(i * n_side + max(u - 1, 0)))
                    for k in range(KD):
                        if k % (KD // 2) == 0:
                            landed = S.side[k // (KD // 2)]
                            dve.wait_ge(landed.sem, landed.at((i * n_side + u + 1) * len(sides)))
                        for n, (t, side, c) in enumerate(columns):
                            col = M.cond[:, k, side.c0 + c:side.c0 + c + 1]
                            a = sa[:, u % 2, n, :]
                            if k == 0:
                                p = dve.tensor_scalar(a, sw[:, t, k, :], col, None, ALU.mult)
                            else:
                                step = (u * (KD - 1) + k - 1) * len(columns) + n
                                dve.wait_ge(S.side_step.sem, S.side_step.at(i * steps + step + 1))
                                p = dve.scalar_tensor_tensor(a, sw[:, t, k, :], col, a, ALU.mult, ALU.add)
                            if k < KD - 1:
                                p.then_inc(*S.side_step.up)
                    p.then_inc(*S.side_acc.up)

                def store_sides(i, u):
                    dve.wait_ge(S.side_sum.sem, S.side_sum.at(i * n_side + max(u - 1, 0)))
                    b0 = i * (2 * n_side) + 2 * (u - 2)
                    for n, (_, side, c) in enumerate(columns):
                        o = dve.tensor_tensor(M.mods[:, side.s, bass.ds(b0, 2), c],
                                              M.ps[:, banks + u % 2, 2 * n:2 * n + 2],
                                              M.all_vec[:, bass.ds(b0 + side.bias, 2)], ALU.add)
                    o.then_inc(*S.side_done.up)

                for u in range(min(2, nu)):
                    low(units_of(0)[u], 0, u)

                def turn(i, last):
                    n = 0
                    here = units_of(i)
                    for u, unit in enumerate(here):
                        if beside:
                            beside.vector_first(dve, i, u)
                        for j in unit.jobs:
                            m = split_nth[n]
                            acc = M.ps[0:j.m, n % banks, 0:j.n]
                            if j.engine == "dve":
                                dve.wait_ge(S.acc.sem, S.acc.at(i * nj + n + 1))
                                for other in j.after:
                                    wait_job(dve, i, other)
                                if j.kind == "times" and (m >= 2 or turns > 1):
                                    dve.wait_ge(S.lo.sem, S.lo.at(i * n_split + m - 1))
                                j.evac(dve, acc).then_inc(*S.by_dve.up)
                            if j.kind != "keep":
                                v, hi = M.v[:, m % 2, 0:j.n], j.dst(j.hidden.hi)
                                dve.wait_ge(S.hi.sem, S.hi.at(i * n_split + m + 1))
                                dve.tensor_tensor(j.dst(j.hidden.lo), v, hi, ALU.subtract).then_inc(*S.lo.up)
                            if j.square and last:
                                _, dst, fresh = j.square
                                dve.wait_ge(S.sq_act.sem, S.sq_act.at(squares.index(n) + 1))
                                a = M.sq[:, 0, 0:j.n]
                                if fresh:
                                    dve.engine_nop().then_inc(*S.sq_add.up)
                                else:
                                    dve.tensor_tensor(dst, dst, a, ALU.add).then_inc(*S.sq_add.up)
                            n += 1
                        if u + 2 < nu:
                            low(here[u + 2], i, u + 2)
                        elif not last:
                            low(units_of(i + 1)[u + 2 - nu], i + 1, u + 2 - nu)
                        if beside:
                            beside.vector(dve, i, u, wait_job)
                        if sides and u >= 2:
                            store_sides(i, u)
                        if sides and u < n_side:
                            multiply_sides(i, u)
                run(dve, turn)

            n_relu = n_split if any(j.kind == "relu2" for j in jobs) else 0
            S.acc.sent, S.w_hi.sent, S.w_lo.sent = turns * nj, turns * nu, turns * nu
            S.by_act.sent, S.by_dve.sent = turns * count["act"], turns * count["dve"]
            S.hi.sent = S.lo.sent = turns * n_split
            S.value.sent = turns * n_relu
            S.side_acc.sent = S.side_sum.sent = S.side_done.sent = turns * n_side if sides else 0
            S.side_step.sent = turns * steps
            for landed in S.side:
                landed.sent = turns * n_side * len(sides) if sides else 0
            S.sq_act.sent = S.sq_add.sent = len(squares)
            for name, n in (beside.signals() if beside else {}).items():
                S.named[name].sent = n
            M.loaded = len(ahead or [])
            for s in range(RING):
                units_in = len(range(s, turns * nu, RING)) if turns > 1 else len(range(s, nu, RING))
                S.weights[s].sent = parts * (units_in - (1 if s < loaded else 0)) + (
                    len(ahead[s].pieces(M.ring[:, s, :])) if s < M.loaded else 0)


def cut(w, r0, r1, c0, n=UNIT, jobs=()):
    src = w[r0:r1, bass.ds(c0, n)].rearrange("(k p) n -> p k n", p=P)
    return Unit(src, (r1 - r0) // P, n, list(jobs))


def feature_jobs(acts, kt, blocks, groups, engine, evac, m=P, k0=0, **more):
    jobs = [
        Job(lambda w, k, c=c: w[:, k, c:c + m], lambda part, k, g=g: part[:, k0 + k, g[0]:g[1]], acts, kt, m,
            g[1] - g[0], engine(b) if callable(engine) else engine,
            evac and (lambda e, acc, b=b, g=g: evac(e, acc, b, g)),
            dst=lambda t, b=b, g=g: t[:, b, g[0]:g[1]], where=(b, g), **more)
        for b, c in blocks for g in groups
    ]
    return jobs


def norm(nc, S, M, src, kt, width, groups, out, scale, bias=None, split=None, k0=0, add=None, summed=None):
    lo, hi = groups[0][0], groups[-1][1]
    w = hi - lo
    sq, rs, tmp = M.sq, M.rs, M.tmp
    with S.stage(nc) as block:
        @block.scalar
        def _(act):
            for k in range(0, kt if summed is None else 0, 2):
                if k >= 2:
                    act.wait_ge(S.summed.sem, S.summed.at(k - 1))
                act.activation(sq[:, 0, 0:w], src(k, lo, hi), ACT.Square).then_inc(*S.sq_act.one)
            act.wait_ge(S.summed.sem, S.summed.at(kt if summed is None else 1))
            for g, (a, b) in enumerate(groups):
                ln = act.activation(rs[:, a - lo:b - lo], M.ps[:, g, 0:b - a], ACT.Ln, scale=1.0 / width,
                                    bias=M.eps[:, 0:1])
            ln.then_inc(*S.act.one)
            act.wait_ge(S.act.sem, S.act.at(1))
            act.activation(rs[:, 0:w], rs[:, 0:w], ACT.Exp, scale=-0.5).then_inc(*S.rstd.one)
            for k in range(kt if add is None else 0):
                act.wait_ge(S.normed.sem, S.normed.at(k + 1))
                if split and k >= 2:
                    act.wait_ge(S.lo.sem, S.lo.at(k - 1))
                for a, b in groups:
                    dst = M.f[:, k % 2, a - lo:b - lo] if split else out(k, a, b)
                    o = act.activation(dst, tmp[:, k % 2, a - lo:b - lo], ACT.Identity,
                                       scale=scale(k, a), bias=0.0 if bias is None else bias(k, a))
                o.then_inc(*S.scaled.one)
                if split:
                    act.wait_ge(S.scaled.sem, S.scaled.at(k + 1))
                    act.activation(split.hi[:, k0 + k, lo:hi], M.f[:, k % 2, 0:w], ACT.Copy).then_inc(*S.hi.one)

        @block.vector
        def _(dve):
            def low(k):
                dve.wait_ge(S.hi.sem, S.hi.at(k + 1))
                dve.tensor_tensor(split.lo[:, k0 + k, lo:hi], M.f[:, k % 2, 0:w], split.hi[:, k0 + k, lo:hi],
                                  ALU.subtract).then_inc(*S.lo.one)

            for k in range(1, kt if summed is None else 0, 2):
                if k >= 2:
                    dve.wait_ge(S.summed.sem, S.summed.at(k - 1))
                dve.tensor_tensor(sq[:, 1, 0:w], src(k, lo, hi), src(k, lo, hi), ALU.mult).then_inc(*S.sq_dve.one)
            dve.wait_ge(S.rstd.sem, S.rstd.at(1))
            for k in range(kt):
                if k >= 2:
                    dve.wait_ge(S.scaled.sem, S.scaled.at(k - 1))
                dve.tensor_tensor(tmp[:, k % 2, 0:w], src(k, lo, hi), rs[:, 0:w], ALU.mult).then_inc(*S.normed.one)
                if split and k:
                    low(k - 1)
                if add is not None:
                    dve.wait_ge(S.normed.sem, S.normed.at(k + 1))
                    dve.scalar_tensor_tensor(add(k, lo, hi), tmp[:, k % 2, 0:w], scale(k, lo), add(k, lo, hi),
                                             ALU.mult, ALU.add).then_inc(*S.scaled.one)
            if split:
                low(kt - 1)

        @block.tensor
        def _(pe):
            if summed is not None:
                for g, (a, b) in enumerate(groups):
                    mm = pe.matmul(M.ps[:, g, 0:b - a], M.ones[:, :], summed[:, a:b], start=True, stop=True)
                mm.then_inc(*S.summed.one)
            for k in range(kt if summed is None else 0):
                s = S.sq_dve if k % 2 else S.sq_act
                pe.wait_ge(s.sem, s.at(k // 2 + 1))
                for g, (a, b) in enumerate(groups):
                    mm = pe.matmul(M.ps[:, g, 0:b - a], M.ones[:, :], sq[:, k % 2, a - lo:b - lo],
                                   start=k == 0, stop=k == kt - 1)
                mm.then_inc(*S.summed.one)


def chain(eng, sig, ins):
    ins.then_inc(*sig.one)
    eng.wait_ge(sig.sem, sig.at(sig.sent))


def divide(nc, S, M, srcs, split, lo, hi):
    with S.stage(nc) as block:
        @block.scalar
        def _(act):
            for k, src in enumerate(srcs):
                act.activation(split.hi[:, k, lo:hi], src, ACT.Copy).then_inc(*S.hi.one)

        @block.vector
        def _(dve):
            for k, src in enumerate(srcs):
                dve.wait_ge(S.hi.sem, S.hi.at(k + 1))
                dve.tensor_tensor(split.lo[:, k, lo:hi], src, split.hi[:, k, lo:hi], ALU.subtract)


def load(nc, S, pairs):
    with S.stage(nc) as block:
        @block.sync
        def _(sp):
            for dst, src in pairs:
                sp.dma_start(dst, src).then_inc(*S.landed.one)
            sp.wait_ge(S.landed.sem, S.landed.at(len(pairs)))
            sp.nop()


def reduce_angle(dve, S, x, k):
    chain(dve, S.dve, dve.tensor_scalar(k, x, 1.0 / TWO_PI, ROUND, ALU.mult, ALU.add))
    chain(dve, S.dve, dve.tensor_scalar(k, k, -ROUND, None, ALU.add))
    for part in (PI1, PI2, PI3):
        chain(dve, S.dve, dve.scalar_tensor_tensor(x, k, -part, x, ALU.mult, ALU.add))
    chain(dve, S.dve, dve.tensor_scalar(x, x, SIN_MAX, -SIN_MAX, ALU.min, ALU.max))


def attention(nc, S, M, heads, nb, kt, score, mask, mix, store):
    n_items = heads * nb
    w = kt * P

    def s_ps(n):
        return M.ps[:, 2 * (n % 2):2 * (n % 2) + 2, :].rearrange("p a b -> p (a b)")[:, 0:w]

    t_ps = M.ps[:, 4:6, :].rearrange("p a b -> p (a b)")[:, 0:w]
    i = M.fresh()

    with nc.sbuf_tensor(f"p{i}", [P, 2, T], F32) as p, nc.sbuf_tensor(f"pt{i}", [P, kt, nb * P], F32) as p_t, \
            S.stage(nc) as block:
        @block.tensor
        def _(pe):
            def scores(n):
                if n >= 2:
                    pe.wait_ge(S.exped.sem, S.exped.at(n - 1))
                score(pe, n // nb, n % nb, s_ps(n)).then_inc(*S.scores.one)

            def values(h):
                pe.wait_ge(S.probs_t.sem, S.probs_t.at((h + 1) * nb))
                if h >= 2:
                    pe.wait_ge(S.stored.sem, S.stored.at(h - 1))
                mix(pe, h, M.ps[:, 6 + h % 2, :], p_t).then_inc(*S.mixed.one)

            scores(0)
            scores(1)
            for n in range(n_items):
                if n + 2 < n_items:
                    scores(n + 2)
                pe.wait_ge(S.probs.sem, S.probs.at(n + 1))
                if n >= 1:
                    pe.wait_ge(S.probs_t.sem, S.probs_t.at(n))
                for j in range(kt):
                    tr = pe.transpose(t_ps[:, j * P:(j + 1) * P], p[:, n % 2, j * P:(j + 1) * P], M.ident[:, :])
                tr.then_inc(*S.turned.one)
                if n % nb == 0 and n:
                    values(n // nb - 1)
            values(heads - 1)

        @block.vector
        def _(dve):
            def maximum(n):
                dve.wait_ge(S.scores.sem, S.scores.at(n + 1))
                src = s_ps(n)
                if mask:
                    if n >= 2:
                        dve.wait_ge(S.turned.sem, S.turned.at(n - 1))
                    for a, b, m in mask(n % nb):
                        added = dve.tensor_tensor(p[:, n % 2, a:b], src[:, a:b], m, ALU.add)
                    added.then_inc(*S.masked.one)
                    dve.wait_ge(S.masked.sem, S.masked.at(n + 1))
                    src = p[:, n % 2, 0:w]
                dve.tensor_reduce(M.nmax[:, n % 4:n % 4 + 1], src, AX, ALU.max, negate=True).then_inc(*S.maxed.one)

            def normalise(n):
                dve.wait_ge(S.exped.sem, S.exped.at(n + 1))
                dve.reciprocal(M.rsum[:, n % 4:n % 4 + 1], M.esum[:, n % 4:n % 4 + 1]).then_inc(*S.recip.one)
                dve.wait_ge(S.recip.sem, S.recip.at(n + 1))
                dve.tensor_scalar(p[:, n % 2, 0:w], p[:, n % 2, 0:w], M.rsum[:, n % 4:n % 4 + 1], None,
                                  ALU.mult).then_inc(*S.probs.one)

            def head(h):
                dve.wait_ge(S.mixed.sem, S.mixed.at(h + 1))
                store(dve, h, M.ps[:, 6 + h % 2, :]).then_inc(*S.stored.one)

            for n in range(n_items):
                maximum(n)
                if n:
                    normalise(n - 1)
                if n > nb and n % nb == 1 % nb:
                    head(n // nb - 1 if nb > 1 else n - 2)
            normalise(n_items - 1)
            if heads > 1 and nb == 1:
                head(heads - 2)
            head(heads - 1)

        @block.scalar
        def _(act):
            def exponent(n):
                act.wait_ge(S.maxed.sem, S.maxed.at(n + 1))
                if not mask and n >= 2:
                    act.wait_ge(S.turned.sem, S.turned.at(n - 1))
                src = p[:, n % 2, 0:w] if mask else s_ps(n)
                act.activation(p[:, n % 2, 0:w], src, ACT.Exp, bias=M.nmax[:, n % 4:n % 4 + 1],
                               accum_out=M.esum[:, n % 4:n % 4 + 1]).then_inc(*S.exped.one)

            def keep(n):
                act.wait_ge(S.turned.sem, S.turned.at(n + 1))
                if n % nb == 0 and n:
                    act.wait_ge(S.mixed.sem, S.mixed.at(n // nb))
                b = n % nb
                act.activation(p_t[:, 0:kt, b * P:(b + 1) * P], t_ps.rearrange("p (k q) -> p k q", k=kt),
                               ACT.Copy).then_inc(*S.probs_t.one)

            for n in range(n_items):
                exponent(n)
                if n:
                    keep(n - 1)
            keep(n_items - 1)



def fourier(nc, S, M, io, ss, lo, length):
    nt = length // P
    with ExitStack() as ctx:
        chan = ctx.enter_context(nc.sbuf_tensor(f"chan{ss}", [P, 2 * P], F32))
        ab = ctx.enter_context(nc.sbuf_tensor(f"ab{ss}", [P, nt, 2, 2, P], F32))
        tok = ctx.enter_context(nc.sbuf_tensor(f"tok{ss}", [P, nt, 2, length], F32))
        load(nc, S, [(chan[:, :], io["fnet_channels"])])
        with S.stage(nc) as block:
            @block.sync
            def _(sp):
                sp.dma_start(tok[:, :, :, :], io[f"fnet_tokens_{length}"]).then_inc(*S.landed.one)

            @block.tensor
            def _(pe):
                for n in range(2 * nt):
                    t, f = divmod(n, 2)
                    mm = pe.matmul(M.ps[:, n % 8, 0:2 * P], M.p[:, 6 + f, lo + t * P:lo + (t + 1) * P], chan[:, :],
                                   start=True, stop=True)
                    mm.then_inc(*S.pe.one)
                for f in range(2):
                    for t in range(nt):
                        for c in range(2):
                            if f == 0 and c == 0:
                                pe.wait_ge(S.by_dve.sem, S.by_dve.at(2 * nt))
                            if f == t == c == 0:
                                pe.wait_ge(S.landed.sem, S.landed.at(1))
                            mm = pe.matmul(M.ps[:, f, 0:length], ab[:, t, f, c, :], tok[:, t, c, :],
                                           start=t == 0 and c == 0, stop=t == nt - 1 and c == 1)
                    mm.then_inc(*S.acc.one)

            @block.vector
            def _(dve):
                for n in range(2 * nt):
                    t, f = divmod(n, 2)
                    dve.wait_ge(S.pe.sem, S.pe.at(n + 1))
                    dve.tensor_copy(ab[:, t, f, :, :].rearrange("p c n -> p (c n)"),
                                    M.ps[:, n % 8, 0:2 * P]).then_inc(*S.by_dve.one)

            @block.scalar
            def _(act):
                for f in range(2):
                    act.wait_ge(S.acc.sem, S.acc.at(f + 1))
                    act.activation(M.p[:, 6 + f, lo:lo + length], M.ps[:, f, 0:length], ACT.Copy).then_inc(*S.act.one)


def hyena(nc, S, M, io, l, ss, lo, length):
    nt = length // P
    with ExitStack() as ctx:
        def sb(name, shape):
            return ctx.enter_context(nc.sbuf_tensor(f"{name}{ss}", shape, F32))

        tk = sb("tk", [P, nt, 2, length])
        ta = sb("ta", [P, nt, 2, length])
        emb = sb("emb", [EMB, length])
        w1 = sb("w1", [EMB, ORDER])
        w2 = sb("w2", [ORDER, ORDER])
        w3 = sb("w3", [ORDER, 2 * HY])
        hid = sb("hid", [ORDER, 2, length])
        kk = sb("kk", [ORDER, length])
        decay = sb("decay", [P, nt, 2 * HY])
        filt = sb("filt", [P, nt, 2 * HY])
        pm = sb("pm", [P, nt, 2, HY])
        inv = sb("inv", [P, HY])
        kf = decay[:, :, :].rearrange("p t (c n) -> p t c n", c=2)
        u = sb("u", [P, 6, length])
        zt = sb("zt", [P, nt, HY])
        yf = sb("yf", [P, nt, 2, HY])
        m4 = filt[:, 0:2, :].rearrange("p a (c n) -> p a c n", c=2)
        pairs = [(emb[:, :], io[f"hy_emb_{length}"]), (w1[:, :], io["hy_w1"][l]), (w2[:, :], io["hy_w2"][l]),
                 (w3[:, :], io["hy_w3"][l]), (decay[:, :, :], io[f"hy_decay_{length}"])]
        load(nc, S, pairs)
        b1, b2, fr = (M.col(n, l)[0:ORDER] for n in ("hy_b1", "hy_b2", "hy_freq"))
        cw = lambda j, b: M.col("hy_conv_w", l, 6 * j + b)
        p_in = lambda b: M.p[:, 8 + b, lo:lo + length]

        with S.stage(nc) as block:
            @block.sync
            def _(sp):
                sp.dma_start(tk[:, :, :, :], io[f"hy_tk_{length}"]).then_inc(*S.landed.one)
                sp.dma_start(ta[:, :, :, :], io[f"hy_ta_{length}"]).then_inc(*S.landed.one)
                sp.wait_ge(S.landed.sem, S.landed.at(2))
                sp.nop()

            @block.tensor
            def _(pe):
                pe.matmul(M.ps[0:ORDER, 0, 0:length], w1[:, :], emb[:, :], start=True, stop=True).then_inc(*S.pe.one)
                pe.wait_ge(S.act.sem, S.act.at(1))
                pe.matmul(M.ps[0:ORDER, 1, 0:length], w2[:, :], hid[:, 0, :], start=True, stop=True).then_inc(*S.pe.one)
                pe.wait_ge(S.act.sem, S.act.at(2))
                for t in range(nt):
                    pe.matmul(M.ps[:, 2 + t, 0:2 * HY], hid[:, 1, t * P:(t + 1) * P], w3[:, :],
                              start=True, stop=True).then_inc(*S.pe.one)
                for t in range(nt):
                    pe.wait_ge(S.by_act.sem, S.by_act.at(t + 1))
                    mm = pe.matmul(M.ps[:, 7, 0:2 * HY], M.ones[:, :], yf[:, t, :, :].rearrange("p c n -> p (c n)"),
                                   start=t == 0, stop=t == nt - 1)
                mm.then_inc(*S.acc.one)

            @block.vector
            def _(dve):
                for s, b in ((0, b1), (1, b2)):
                    dve.wait_ge(S.pe.sem, S.pe.at(s + 1))
                    chain(dve, S.dve, dve.tensor_scalar(hid[:, s, :], M.ps[0:ORDER, s, 0:length], b, fr,
                                                        ALU.add, ALU.mult))
                    reduce_angle(dve, S, hid[:, s, :], kk[:, :])
                    dve.tensor_scalar(kk[:, :], hid[:, s, :], 1.0, None, ALU.mult).then_inc(*S.by_dve.one)
                for t in range(nt):
                    dve.wait_ge(S.pe.sem, S.pe.at(3 + t))
                    chain(dve, S.dve, dve.tensor_tensor(filt[:, t, :], M.ps[:, 2 + t, 0:2 * HY], decay[:, t, :],
                                                        ALU.mult))
                    dve.tensor_tensor(pm[:, t, 0, :], filt[:, t, 0:HY], filt[:, t, HY:2 * HY], ALU.add)
                    dve.tensor_tensor(pm[:, t, 1, :], filt[:, t, HY:2 * HY], filt[:, t, 0:HY],
                                      ALU.subtract).then_inc(*S.by_dve.one)
                for b in range(6):
                    chain(dve, S.dve, dve.tensor_scalar(u[:, b, :], p_in(b), cw(1, b), M.col("hy_conv_b", l, b),
                                                        ALU.mult, ALU.add))
                    chain(dve, S.dve, dve.scalar_tensor_tensor(u[:, b, 1:length], p_in(b)[:, 0:length - 1], cw(0, b),
                                                               u[:, b, 1:length], ALU.mult, ALU.add))
                    chain(dve, S.dve, dve.scalar_tensor_tensor(u[:, b, 0:length - 1], p_in(b)[:, 1:length], cw(2, b),
                                                               u[:, b, 0:length - 1], ALU.mult, ALU.add))
                for b in range(2):
                    dve.tensor_tensor(u[:, 2 + b, :], u[:, 2 + b, :], u[:, 4 + b, :], ALU.mult)
                dve.wait_ge(S.acc.sem, S.acc.at(1))
                chain(dve, S.dve, dve.tensor_copy(zt[:, 0, :], M.ps[:, 7, 0:HY]))
                chain(dve, S.dve, dve.tensor_tensor(inv[:, :], zt[:, 0, :], M.ps[:, 7, HY:2 * HY], ALU.add))
                chain(dve, S.dve, dve.tensor_scalar(inv[:, :], inv[:, :], float(length), None, ALU.mult))
                dve.reciprocal(inv[:, :], inv[:, :])

            @block.scalar
            def _(act):
                for s in range(2):
                    act.wait_ge(S.by_dve.sem, S.by_dve.at(s + 1))
                    act.activation(hid[:, s, :], kk[:, :], ACT.Sin).then_inc(*S.act.one)
                for t in range(nt):
                    act.wait_ge(S.by_dve.sem, S.by_dve.at(3 + t))
                    act.activation(yf[:, t, :, :].rearrange("p c n -> p (c n)"), filt[:, t, :],
                                   ACT.Abs).then_inc(*S.by_act.one)

        with S.stage(nc) as block:
            @block.tensor
            def _(pe):
                for b in range(2):
                    for t in range(nt):
                        pe.transpose(M.ps[:, b, t * P:(t + 1) * P], u[:, 2 + b, t * P:(t + 1) * P],
                                     M.ident[:, :]).then_inc(*S.pe.one)
                for f in range(nt):
                    if f >= 2:
                        pe.wait_ge(S.by_act.sem, S.by_act.at(f - 1))
                    for c in range(2):
                        for t in range(nt):
                            mm = pe.matmul(M.ps[:, 2 + f % 2, c * HY:(c + 1) * HY], tk[:, t, c, f * P:(f + 1) * P],
                                           pm[:, t, c, :], start=t == 0, stop=t == nt - 1)
                    mm.then_inc(*S.acc.one)
                    pe.wait_ge(S.act.sem, S.act.at(2))
                    if f >= 2:
                        pe.wait_ge(S.mixed.sem, S.mixed.at(f - 1))
                    for c in range(2):
                        for t in range(nt):
                            mm = pe.matmul(M.ps[:, 4 + f % 2, c * HY:(c + 1) * HY], ta[:, t, c, f * P:(f + 1) * P],
                                           zt[:, t, :], start=t == 0, stop=t == nt - 1)
                    mm.then_inc(*S.scores.one)
                pe.wait_ge(S.mixed.sem, S.mixed.at(nt))
                for b in range(2):
                    for f in range(nt):
                        for c in range(2):
                            mm = pe.matmul(M.ps[:, 6 + b, 0:length], yf[:, f, c, b * P:(b + 1) * P], ta[:, f, c, :],
                                           start=f == 0 and c == 0, stop=f == nt - 1 and c == 1)
                    mm.then_inc(*S.probs.one)

            @block.scalar
            def _(act):
                for b in range(2):
                    act.wait_ge(S.pe.sem, S.pe.at((b + 1) * nt))
                    act.activation(zt[:, :, b * P:(b + 1) * P],
                                   M.ps[:, b, 0:length].rearrange("p (t c) -> p t c", t=nt), ACT.Copy)\
                        .then_inc(*S.act.one)
                for f in range(nt):
                    act.wait_ge(S.acc.sem, S.acc.at(f + 1))
                    act.activation(kf[:, f, :, :].rearrange("p c n -> p (c n)"), M.ps[:, 2 + f % 2, :],
                                   ACT.Copy).then_inc(*S.by_act.one)

            @block.vector
            def _(dve):
                for f in range(nt):
                    dve.wait_ge(S.by_act.sem, S.by_act.at(f + 1))
                    for c in range(2):
                        k = dve.tensor_tensor(kf[:, f, c, :], kf[:, f, c, :], inv[:, :], ALU.mult)
                    chain(dve, S.dve, k)
                    dve.wait_ge(S.scores.sem, S.scores.at(f + 1))
                    zc, zs = M.ps[:, 4 + f % 2, 0:HY], M.ps[:, 4 + f % 2, HY:2 * HY]
                    dve.tensor_tensor(m4[:, 0, 0, :], zc, kf[:, f, 0, :], ALU.mult)
                    dve.tensor_tensor(m4[:, 0, 1, :], zs, kf[:, f, 1, :], ALU.mult)
                    dve.tensor_tensor(m4[:, 1, 0, :], zs, kf[:, f, 0, :], ALU.mult)
                    chain(dve, S.dve, dve.tensor_tensor(m4[:, 1, 1, :], zc, kf[:, f, 1, :], ALU.mult))
                    dve.tensor_tensor(yf[:, f, 0, :], m4[:, 0, 0, :], m4[:, 0, 1, :], ALU.add)
                    y = dve.tensor_tensor(yf[:, f, 1, :], m4[:, 1, 0, :], m4[:, 1, 1, :], ALU.subtract)
                    y.then_inc(*S.mixed.one)
                    dve.wait_ge(S.mixed.sem, S.mixed.at(f + 1))
                for b in range(2):
                    dve.wait_ge(S.probs.sem, S.probs.at(b + 1))
                    chain(dve, S.dve, dve.scalar_tensor_tensor(u[:, 2 + b, :], u[:, 2 + b, :], M.col("hy_d", l, b),
                                                               M.ps[:, 6 + b, 0:length], ALU.mult, ALU.add))
                    dve.tensor_tensor(M.p[:, 8 + b, lo:lo + length], u[:, 2 + b, :], u[:, b, :],
                                      ALU.mult).then_inc(*S.by_dve.one)


def px_cut(io, l, c0, jobs=()):
    return cut(io["w_in"][l], 0, D, c0, UNIT, jobs)


def square_cuts(w, jobs_of=lambda c: ()):
    return [cut(w, 0, D, c * UNIT, UNIT, jobs_of(c)) for c in range(D // UNIT)]


def first_layer(nc, S, M, io, l):
    last = l == DEPTH - 1
    groups = [X_COLS, C_COLS]
    outer = [X_COLS] if last else groups
    side = lambda a: 0 if a < LX else 1
    x = lambda k, a, b: M.x[:, k, a:b]

    with ExitStack() as ctx:
        M.p = ctx.enter_context(nc.sbuf_tensor(f"p{l}", [P, 14, T], F32))

        def keep(e, acc, b, g):
            m = QK if b == 5 else P
            if b % 2:
                return e.activation(M.p[0:m, b, g[0]:g[1]], acc, ACT.Copy)
            return e.tensor_copy(M.p[0:m, b, g[0]:g[1]], acc)

        cuts = [(0, [0, 1]), (256, [2, 3]), (512, [4, 5]), (OFF_F, [6, 7]), (OFF_H, [8, 9]),
                (OFF_H + 256, [10, 11]), (OFF_H + 512, [12, 13])]
        w_q = [cut(io["w_uq"][l], 0, Q_LORA, c * 4 * QK, 4 * QK) for c in range(2)]
        with ExitStack() as inner:
            h = Split(inner, nc, f"h{l}", [P, KD, T])
            norm(nc, S, M, x, KD, D, groups, None, lambda k, a: M.gain[:, 2 * l, side(a), k:k + 1],
                 lambda k, a: M.mod(l, 0, k, side(a)), split=h, summed=M.ssum if l else None)
            units = []
            for c0, blocks in cuts:
                js = []
                for n, b in enumerate(blocks):
                    gs = groups if b in (3, 4, 5) else outer
                    off, m = (64, QK) if b == 5 else (n * P, P)
                    js += feature_jobs(h, KD, [(b, off)], gs, "act" if b % 2 else "dve", keep, m)
                units.append(px_cut(io, l, c0, js))
            project(nc, S, M, lambda i: units, ahead=w_q)

        for ss, lo, length in [(f"x{l}", 0, LX)] + ([] if last else [(f"c{l}", LX, LC)]):
            fourier(nc, S, M, io, ss, lo, length)
            hyena(nc, S, M, io, l, ss, lo, length)

        with ExitStack() as att:
            q = att.enter_context(nc.sbuf_tensor(f"q{l}", [P, HEADS, T], F32))
            k_t = att.enter_context(nc.sbuf_tensor(f"k{l}", [P, HEADS, T], F32))
            v = M.p[:, 0:4, :].rearrange("p a b -> p (a b)").rearrange("p (t n) -> p t n", t=T // P)
            scale = 1.0 / math.sqrt(QK)

            def keep_q(e, acc, b, g):
                return e.activation(q[0:QK, b, g[0]:g[1]], acc, ACT.Copy, scale=scale)

            def keep_k(e, acc, b, g):
                return e.tensor_copy(k_t[0:NOPE, b, g[0]:g[1]], acc[0:NOPE, :])

            with ExitStack() as inner:
                c = Split(inner, nc, f"c{l}", [P, 5, T])
                norm(nc, S, M, lambda k, a, b: M.p[:, k, a:b], 3, Q_LORA, outer, None,
                     lambda k, a: M.col("q_norm_g", l, k), split=c)
                norm(nc, S, M, lambda k, a, b: M.p[:, 3 + k, a:b], 2, KV_LORA, groups, None,
                     lambda k, a: M.col("kv_norm_g", l, k), split=c, k0=3)
                for u, unit in enumerate(w_q):
                    unit.jobs = [j for b in range(4)
                                 for j in feature_jobs(c, 3, [(4 * u + b, b * QK)], outer, "act", keep_q, QK)]
                vcols = lambda w, k: w[:, k, :].rearrange("p (h n) -> p h n", h=4)[:, :, NOPE:NOPE + VDIM]
                w_kv = []
                for u in range(2):
                    js = feature_jobs(c, 2, [(4 * u + b, b * P) for b in range(4)], groups, "dve", keep_k, k0=3)
                    js += [Job(vcols, lambda part, k, t=t: part[:, 3 + k, t * P:(t + 1) * P], c, 2, P, 4 * VDIM, "act",
                               lambda e, acc, t=t, u=u: e.activation(v[:, t, 4 * VDIM * u:4 * VDIM * (u + 1)], acc,
                                                                     ACT.Copy),
                               weights_first=False) for t in range(T // P)]
                    w_kv.append(cut(io["w_ukv"][l], 0, KV_LORA, u * 4 * P, 4 * P, js))
                project(nc, S, M, lambda i: w_q + w_kv, ahead=square_cuts(io["w_out"][l])[:2])

            lo, hi = NOPE, QK
            srcs = [q[0:QK, b, 0:LX] for b in range(HEADS)] + [M.p[0:QK, 5, 0:LX]]
            with ExitStack() as inner:
                swap = inner.enter_context(nc.sbuf_tensor(f"swap{l}", [P, P], F32))
                rope = inner.enter_context(nc.sbuf_tensor(f"rope{l}", [P, 2, LX], F32))
                load(nc, S, [(swap[:, :], io["rope_swap"]), (rope[:, :, :], io["rope_tables"])])
                with S.stage(nc) as block:
                    @block.tensor
                    def _(pe):
                        for n, s in enumerate(srcs):
                            if n >= 8:
                                pe.wait_ge(S.by_dve.sem, S.by_dve.at(n - 7))
                            pe.matmul(M.ps[0:QK, n % 8, :], swap[0:QK, 0:QK], s, start=True, stop=True)\
                                .then_inc(*S.pe.one)

                    @block.vector
                    def _(dve):
                        for n, s in enumerate(srcs):
                            dve.wait_ge(S.pe.sem, S.pe.at(n + 1))
                            t = M.sq[lo:hi, n % 2, 0:LX]
                            dve.tensor_tensor(t, M.ps[lo:hi, n % 8, :], rope[lo:hi, 1, :], ALU.mult)
                            chain(dve, S.dve, dve.tensor_tensor(s[lo:hi, :], s[lo:hi, :], rope[lo:hi, 0, :], ALU.mult))
                            dve.tensor_tensor(s[lo:hi, :], s[lo:hi, :], t, ALU.add).then_inc(*S.by_dve.one)
                            dve.wait_ge(S.by_dve.sem, S.by_dve.at(n + 1))

                    @block.scalar
                    def _(act):
                        act.wait_ge(S.by_dve.sem, S.by_dve.at(len(srcs)))
                        for b in range(HEADS):
                            act.activation(k_t[lo:hi, b, :], M.p[lo:hi, 5, :], ACT.Copy).then_inc(*S.act.one)

            for lo_q, lo_k, nb, kt in [(0, 0, LX // P, T // P)] + ([] if last else [(LX, LX, LC // P, LC // P)]):
                def score(pe, hd, b, acc):
                    for a in range(0, kt * P, 512):
                        n = min(512, kt * P - a)
                        mm = pe.matmul(acc[:, a:a + n], q[0:QK, hd, lo_q + b * P:lo_q + (b + 1) * P],
                                       k_t[0:QK, hd, lo_k + a:lo_k + a + n], start=True, stop=True)
                    return mm

                def mix(pe, hd, acc, p_t):
                    for j in range(kt):
                        mm = pe.matmul(acc[0:VDIM, 0:nb * P], v[:, lo_k // P + j, hd * VDIM:(hd + 1) * VDIM],
                                       p_t[:, j, 0:nb * P], start=j == 0, stop=j == kt - 1)
                    return mm

                def store(dve, hd, acc):
                    r = hd % 2 * VDIM
                    return dve.tensor_copy(M.p[r:r + VDIM, 10 + hd // 2, lo_q:lo_q + nb * P], acc[0:VDIM, 0:nb * P])

                attention(nc, S, M, HEADS, nb, kt, score, None, mix, store)

        def residual(m):
            def add(e, acc, b, g):
                xs = M.x[:, b, g[0]:g[1]]
                return e.scalar_tensor_tensor(xs, acc, M.mod(l, m, b, side(g[0])), xs, ALU.mult, ALU.add)
            return add

        def squared(js):
            for j in js:
                b, (lo, hi) = j.where
                j.square = (M.x[:, b, lo:hi], M.ssum[:, lo:hi], b == 0)
            return js

        hi = outer[-1][1]
        up0 = [cut(io["w_mlp1"][l], 0, D, c * UNIT) for c in range(2)]
        with ExitStack() as inner:
            h = Split(inner, nc, f"mix{l}", [P, KD, T])
            divide(nc, S, M, [M.p[:, b, 0:hi] for b in (10, 11, 12, 13, 6, 7, 8, 9)], h, 0, hi)
            units = square_cuts(io["w_out"][l], lambda c: squared(feature_jobs(
                h, KD, [(2 * c, 0), (2 * c + 1, P)], outer, "dve", residual(2))))
            project(nc, S, M, lambda i: units, ahead=up0)

    if last:
        following = first_units(io, 0)
    else:
        following = [px_cut(io, l + 1, c * UNIT) for c in range(2)]
    with ExitStack() as ctx:
        h = Split(ctx, nc, f"hm{l}", [P, KD, hi])
        hid = Split(ctx, nc, f"hid{l}", [P, KD, hi])
        norm(nc, S, M, x, KD, D, outer, None, lambda k, a: M.gain[:, 2 * l + 1, side(a), k:k + 1],
             lambda k, a: M.mod(l, 3, k, side(a)), split=h, summed=M.ssum)
        ng = len(outer)
        w2 = io["w_mlp2"][l].rearrange("(g k p) n -> g p k n", p=P, k=KD)

        def mlp_units(i):
            units = [cut(io["w_mlp1"][l], 0, D, i * D + c * UNIT, UNIT, feature_jobs(
                h, KD, [(2 * c, 0), (2 * c + 1, P)], outer, "act", None, kind="relu2", hidden=hid))
                for c in range(4)]
            for c in range(4):
                js = squared(feature_jobs(hid, KD, [(2 * c, 0), (2 * c + 1, P)], outer, "dve", residual(5)))
                js[0].needs = (8 * ng,)
                src = w2[i if isinstance(i, int) else bass.ds(i, 1), :, :, c * UNIT:(c + 1) * UNIT]
                if not isinstance(i, int):
                    src = src.rearrange("a p k n -> (a p) k n")
                units.append(Unit(src, KD, UNIT, js))
            return units

        if last:
            sides = [Side(io["ada_w_2"][s], DEPTH + s, 2, 1, FIRST_ROW["ada_b_2"] + 48 * s) for s in range(2)]
        else:
            sides = [Side(io["w_mod"][1], 1, 0, 2, FIRST_ROW["b_mod"] + 48)]
        project(nc, S, M, mlp_units, turns=D_FF // D, ahead=following, sides=sides)



def recurrence(nc, S, M, io):
    w = io["hgrn_w_in_2"][0]
    nch = LX // CHUNK
    h = M.split
    with ExitStack() as ctx:
        def sb(name, shape):
            return ctx.enter_context(nc.sbuf_tensor("r_" + name, shape, F32))

        qs, sg, kk, gs = (sb(n, [P, 2, LX]) for n in ("q", "sg", "k", "g"))
        b_, eb, nb_, ke = (sb(n, [P, 2, LX]) for n in ("b", "eb", "nb", "ke"))
        v = sb("v", [P, 4, UNIT])
        ket = sb("ket", [P, 2, 4, P])
        at = sb("at", [P, 2, LX])
        st = sb("st", [P, 2, nch, P])
        y = M.y
        with S.loop(nc, H2 // 2, **LOOPS["recurrence"]) as i:
            def unit(sec, jobs, later=0):
                return cut(w, 0, D, i * UNIT + (later * UNIT + sec * D), UNIT, jobs)

            def forget(e, acc, b, g):
                e.activation(kk[:, b, :], acc, ACT.Sigmoid, scale=-1.0)
                return e.activation(sg[:, b, :], acc, ACT.Sigmoid)

            blocks = [(0, 0), (1, P)]
            token = [Job(lambda w, k: w[:, k, :], lambda part, k, t=t: part[:, k, t * P:(t + 1) * P], h, KD, P, UNIT,
                         "dve", lambda e, acc, t=t: e.tensor_copy(v[:, t, :], acc), weights_first=False)
                     for t in range(4)]
            units = [
                unit(1, feature_jobs(h, KD, blocks, [X_COLS], "act", forget)),
                unit(0, feature_jobs(h, KD, blocks, [X_COLS], "act",
                                     lambda e, acc, b, g: e.activation(qs[:, b, :], acc, ACT.Silu))),
                unit(3, feature_jobs(h, KD, blocks, [X_COLS], "act",
                                     lambda e, acc, b, g: e.activation(gs[:, b, :], acc, ACT.Silu))),
                unit(2, token),
            ]
            project(nc, S, M, lambda _: units, ahead=[unit(1, [], 1), unit(0, [], 1)])
            with S.stage(nc) as block:
                @block.vector
                def _(dve):
                    for n in range(2):
                        om, lb = (M.lower[:, j, bass.ds(i * 2 + n, 1)] for j in (1, 0))
                        dve.tensor_scalar(kk[:, n, :], kk[:, n, :], om, None, ALU.mult)
                        f = dve.tensor_scalar(sg[:, n, :], sg[:, n, :], om, lb, ALU.mult, ALU.add)
                    f.then_inc(*S.dve.one)
                    dve.wait_ge(S.act.sem, S.act.at(1))
                    for n in range(2):
                        s = dve.tensor_tensor_scan(b_[:, n, :], M.resets[:, :], sg[:, n, :], 0.0, ALU.mult, ALU.add)
                    chain(dve, S.dve, s)
                    for n in range(2):
                        bn = b_[:, n, :].rearrange("p (c t) -> p c t", t=CHUNK)
                        o = dve.tensor_tensor(ke[:, n, :].rearrange("p (c t) -> p c t", t=CHUNK),
                                              bn[:, :, CHUNK - 1:CHUNK].to_broadcast([P, nch, CHUNK]), bn,
                                              ALU.subtract)
                    o.then_inc(*S.dve.one)
                    dve.wait_ge(S.act.sem, S.act.at(2))
                    dve.tensor_tensor(qs[:, :, :], qs[:, :, :], eb[:, :, :], ALU.mult)
                    dve.wait_ge(S.act.sem, S.act.at(3))
                    dve.tensor_tensor(nb_[:, :, :], nb_[:, :, :], kk[:, :, :], ALU.mult)
                    dve.wait_ge(S.act.sem, S.act.at(4))
                    dve.tensor_tensor(ke[:, :, :], ke[:, :, :], kk[:, :, :], ALU.mult)
                    dve.memset(st[:, :, 0, :], 0.0)

                @block.scalar
                def _(act):
                    act.wait_ge(S.dve.sem, S.dve.at(1))
                    act.activation(sg[:, :, :], sg[:, :, :], ACT.Ln).then_inc(*S.act.one)
                    act.wait_ge(S.dve.sem, S.dve.at(2))
                    act.activation(eb[:, :, :], b_[:, :, :], ACT.Exp).then_inc(*S.act.one)
                    act.activation(nb_[:, :, :], b_[:, :, :], ACT.Exp, scale=-1.0).then_inc(*S.act.one)
                    act.wait_ge(S.dve.sem, S.dve.at(3))
                    act.activation(ke[:, :, :], ke[:, :, :], ACT.Exp).then_inc(*S.act.one)

            def additions(g):
                return 4 if g < 4 else 0

            with S.stage(nc) as block:
                @block.tensor
                def _(pe):
                    for n in range(2):
                        for t in range(4):
                            tr = pe.transpose(M.ps[:, n, t * P:(t + 1) * P], ke[:, n, t * P:(t + 1) * P], M.ident[:, :])
                        tr.then_inc(*S.pe.one)
                        for t in range(4):
                            c = slice(t * P, (t + 1) * P)
                            mm = pe.matmul(M.ps[:, 2 + n, c], nb_[:, n, c], qs[:, n, c], start=True, stop=True)
                        mm.then_inc(*S.scores.one)
                    for g in range(8):
                        t, n = divmod(g, 2)
                        pe.wait_ge(S.by_act.sem, S.by_act.at(n + 1))
                        if g == 4:
                            pe.wait_ge(S.masked.sem, S.masked.at(2))
                        for j in range(4):
                            r = slice(j * CHUNK, (j + 1) * CHUNK)
                            mm = pe.matmul(M.ps[:, additions(g) + j, g % 4 * P:(g % 4 + 1) * P], ket[r, n, t, :],
                                           v[r, t, n * P:(n + 1) * P], start=True, stop=True)
                        mm.then_inc(*S.acc.one)
                    pe.wait_ge(S.mixed.sem, S.mixed.at(2 * (nch - 1)))
                    pe.wait_ge(S.masked.sem, S.masked.at(2))
                    for n in range(2):
                        for t in range(4):
                            c = slice(t * P, (t + 1) * P)
                            pe.matmul(M.ps[:, n, c], v[:, t, n * P:(n + 1) * P], at[:, n, c], start=t == 0, stop=False,
                                      skip_group_check=True)
                        for m in range(1, nch):
                            c = slice(m * CHUNK, (m + 1) * CHUNK)
                            mm = pe.matmul(M.ps[:, n, c], st[:, n, m, :], qs[:, n, c], start=False, stop=m == nch - 1,
                                           skip_group_check=True)
                        mm.then_inc(*S.probs.one)
                    for n in range(2):
                        pe.wait_ge(S.sq_act.sem, S.sq_act.at(n + 1))
                        pe.matmul(M.ps[:, 2 + n, :], M.ones[:, :], nb_[:, n, :], start=True, stop=True)\
                            .then_inc(*S.summed.one)

                @block.scalar
                def _(act):
                    for n in range(2):
                        act.wait_ge(S.pe.sem, S.pe.at(n + 1))
                        act.activation(ket[:, n, :, :].rearrange("p t k -> p (t k)"), M.ps[:, n, :], ACT.Copy)\
                            .then_inc(*S.by_act.one)
                    for n in range(2):
                        act.wait_ge(S.probs.sem, S.probs.at(n + 1))
                        act.activation(nb_[:, n, :], M.ps[:, n, :], ACT.Square).then_inc(*S.sq_act.one)
                    for n in range(2):
                        act.wait_ge(S.summed.sem, S.summed.at(n + 1))
                        act.activation(ke[:, n, :], M.ps[:, 2 + n, :], ACT.Ln, scale=1.0 / P, bias=M.eps[:, 0:1])\
                            .then_inc(*S.act.one)
                        act.wait_ge(S.act.sem, S.act.at(n + 1))
                        act.activation(ke[:, n, :], ke[:, n, :], ACT.Exp, scale=-0.5).then_inc(*S.rstd.one)

                @block.vector
                def _(dve):
                    for n in range(2):
                        dve.wait_ge(S.scores.sem, S.scores.at(n + 1))
                        dve.scalar_tensor_tensor(at[:, n, :].rearrange("p (t c) -> p t c", t=4),
                                                 M.ps[:, 2 + n, :].rearrange("p (t c) -> p t c", t=4), 3.0e38,
                                                 M.causal[:, :].unsqueeze(1).to_broadcast([P, 4, P]),
                                                 ALU.min, ALU.mult).then_inc(*S.masked.one)
                    for m in range(nch - 1):
                        for n in range(2):
                            g = m // 4 * 2 + n
                            if m % 8 == 0 and n == 0:
                                dve.wait_ge(S.acc.sem, S.acc.at(g + 4))
                            if m:
                                dve.wait_ge(S.mixed.sem, S.mixed.at(2 * m - 1 + n))
                            dve.scalar_tensor_tensor(
                                st[:, n, m + 1, :], st[:, n, m, :],
                                eb[:, n, m * CHUNK + CHUNK - 1:m * CHUNK + CHUNK],
                                M.ps[:, additions(g) + m % 4, g % 4 * P:(g % 4 + 1) * P], ALU.mult, ALU.add)\
                                .then_inc(*S.mixed.one)
                    for n in range(2):
                        dve.wait_ge(S.rstd.sem, S.rstd.at(n + 1))
                        chain(dve, S.dve, dve.tensor_tensor(ke[:, n, :], ke[:, n, :], M.ps[:, n, :], ALU.mult))
                        dve.scalar_tensor_tensor(y[:, bass.ds(i * 2 + n, 1), :].rearrange("p a t -> p (a t)"),
                                                 ke[:, n, :], M.hgain[:, bass.ds(i * 2 + n, 1)], gs[:, n, :],
                                                 ALU.mult, ALU.mult).then_inc(*S.by_dve.one)


def every4(ap, r):
    return ap.rearrange("p (m r) -> p m r", r=4)[:, :, r]


class Dilated:
    UNITS, ITEMS, JOBS = 6, 4, 12
    banks = 3

    def __init__(self, S, M, qk, v, swp, masks):
        self.S, self.M, self.qk, self.v, self.swp, self.masks = S, M, qk, v, swp, masks
        self.s_ps = M.ps[:, 3:5, :].rearrange("p a b -> p (a b)")[:, 0:T]
        self.t_ps = M.ps[:, 5:7, :].rearrange("p a b -> p (a b)")[:, 0:T]
        self.y_ps = M.ps[:, 7, :]

    def attention_signals(self, heads):
        items = ("scores", "masked", "maxed", "exped", "recip", "probs", "turned", "probs_t")
        return dict({k: heads * self.ITEMS for k in items}, mixed=heads, stored=heads)

    def signals(self):
        n = GROUPS2 * H2
        return dict(self.attention_signals(H2 - 1), swappable=n, swapped=2 * n, roped=n, roped_part=2 * n)

    def wait(self, eng, sig, n):
        if not isinstance(n, int) or n > 0:
            eng.wait_ge(sig.sem, sig.at(n))

    def attended(self, i, u):
        side, step = divmod(u, self.UNITS)
        return None if isinstance(i, int) and 2 * i + side == 0 else (1 - side, i * 2 + (side - 1), step)

    def pe_step(self, pe, b, head, u, after_rope):
        S, qk, v = self.S, self.qk[b], self.v[b]
        base = head * self.ITEMS
        p_t = lambda n: self.M.sq[:, n % 2, :].rearrange("p (k q) -> p k q", q=P)
        if u >= 2:
            n = u - 2
            self.wait(pe, S.probs_t, base + (n + 1))
            if n == 0:
                self.wait(pe, S.stored, head)
            tiles = [(v[:, 0, j, :], j) for j in range(4)] + [(v[:, g, n, :], 3 + g) for g in (1, 2)]
            for m, (values, k) in enumerate(tiles):
                mm = pe.matmul(self.y_ps[:, n * P:(n + 1) * P], values, p_t(n)[:, k, :],
                               start=m == 0, stop=m == len(tiles) - 1)
            if n == self.ITEMS - 1:
                mm.then_inc(*S.mixed.up)
        if 1 <= u <= self.ITEMS:
            n = u - 1
            self.wait(pe, S.probs, base + (n + 1))
            self.wait(pe, S.probs_t, base + n)
            for k in range(T // P):
                tr = pe.transpose(self.t_ps[:, k * P:(k + 1) * P], self.M.f[:, n % 2, k * P:(k + 1) * P],
                                  self.M.ident[:, :])
            tr.then_inc(*S.turned.up)
        if u < self.ITEMS:
            if u == 0 and after_rope:
                self.wait(pe, S.roped, (head + 1) * GROUPS2)
            self.wait(pe, S.masked, base + u)
            pe.matmul(self.s_ps[:, 0:LX], every4(qk[:, 0, :], u), qk[:, 1, :], start=True, stop=True)
            for g in (1, 2):
                mm = pe.matmul(self.s_ps[:, LX + (g - 1) * P:LX + g * P], every4(qk[:, 2 * g, :], u),
                               every4(qk[:, 2 * g + 1, :], u), start=True, stop=True)
            mm.then_inc(*S.scores.up)

    def act_step(self, act, head, u):
        S, M, base = self.S, self.M, head * self.ITEMS
        if 1 <= u <= self.ITEMS:
            n = u - 1
            self.wait(act, S.turned, base + (n + 1))
            act.activation(M.sq[:, n % 2, :], self.t_ps, ACT.Copy).then_inc(*S.probs_t.up)
        if u < self.ITEMS:
            self.wait(act, S.maxed, base + (u + 1))
            p = M.f[:, u % 2, :]
            act.activation(p, p, ACT.Exp, bias=M.nmax[:, u:u + 1], accum_out=M.esum[:, u:u + 1])\
                .then_inc(*S.exped.up)

    def dve_normalise(self, dve, head, u):
        S, M, base = self.S, self.M, head * self.ITEMS
        if 1 <= u <= self.ITEMS:
            n = u - 1
            self.wait(dve, S.exped, base + (n + 1))
            dve.reciprocal(M.rsum[:, n:n + 1], M.esum[:, n:n + 1]).then_inc(*S.recip.up)
            self.wait(dve, S.recip, base + (n + 1))
            dve.tensor_scalar(M.f[:, n % 2, :], M.f[:, n % 2, :], M.rsum[:, n:n + 1], None, ALU.mult)\
                .then_inc(*S.probs.up)

    def dve_step(self, dve, head, u, number=None):
        S, M, base = self.S, self.M, head * self.ITEMS
        if u < self.ITEMS:
            p, masks = M.f[:, u % 2, :], self.masks
            self.wait(dve, S.scores, base + (u + 1))
            dve.tensor_tensor(p[:, 0:LX], self.s_ps[:, 0:LX], masks[:, u * LX:(u + 1) * LX], ALU.add)
            dve.tensor_tensor(p[:, LX:T], self.s_ps[:, LX:T], masks[:, 4 * LX:4 * LX + 2 * P], ALU.add)\
                .then_inc(*S.masked.up)
            self.wait(dve, S.masked, base + (u + 1))
            dve.tensor_reduce(M.nmax[:, u:u + 1], p, AX, ALU.max, negate=True).then_inc(*S.maxed.up)
        if u == self.UNITS - 1:
            self.wait(dve, S.mixed, head + 1)
            dst = M.y[:, bass.ds(head if number is None else number, 1), :].rearrange("p a (m r) -> p r (a m)", r=4)
            dve.tensor_copy(dst, self.y_ps.rearrange("p (r m) -> p r m", r=4)).then_inc(*S.stored.up)

    def sync(self, sp, i, u):
        side, g = divmod(u, self.UNITS)
        g -= 1
        if 0 <= g < GROUPS2:
            self.wait(sp, self.S.swappable, i * (2 * GROUPS2) + (side * GROUPS2 + g + 1))
            qk, half = self.qk[side][:, 2 * g:2 * g + 2, :], ROT // 2
            sp.dma_start(self.swp[0:half, :, :], qk[half:ROT, :, :]).then_inc(*self.S.swapped.up)
            sp.dma_start(self.swp[half:ROT, :, :], qk[0:half, :, :]).then_inc(*self.S.swapped.up)

    def tensor(self, pe, i, u):
        at = self.attended(i, u)
        if at:
            self.pe_step(pe, *at, True)

    def scalar(self, act, i, u):
        at = self.attended(i, u)
        if at:
            self.act_step(act, *at[1:])

    def vector_first(self, dve, i, u):
        at = self.attended(i, u)
        if at:
            self.dve_normalise(dve, *at[1:])

    def vector(self, dve, i, u, wait_job):
        S, M = self.S, self.M
        at = self.attended(i, u)
        if at:
            self.dve_step(dve, *at[1:])
        side, g = divmod(u, self.UNITS)
        g -= 1
        if 0 <= g < GROUPS2:
            n = i * (2 * GROUPS2) + (side * GROUPS2 + g + 1)
            qk = self.qk[side][0:ROT, 2 * g:2 * g + 2, :]
            self.wait(dve, S.swapped, n * 2)
            cos, sin = (M.rot[:, t:t + 1, :].to_broadcast([ROT, 2, LX]) for t in range(2))
            dve.tensor_tensor(self.swp[:, :, :], self.swp[:, :, :], sin, ALU.mult).then_inc(*S.roped_part.up)
            dve.tensor_tensor(qk, qk, cos, ALU.mult).then_inc(*S.roped_part.up)
            self.wait(dve, S.roped_part, n * 2)
            dve.tensor_tensor(qk, qk, self.swp[:, :, :], ALU.add).then_inc(*S.roped.up)
        if g + 1 < GROUPS2:
            if g >= 0:
                self.wait(dve, S.roped, n)
            wait_job(dve, i, side * self.JOBS + 2 * g + 3)
            dve.tensor_copy(M.flag[:, :], M.eps[:, :]).then_inc(*S.swappable.up)


def dilated(nc, S, M, io, ahead):
    w = io["attn_w_in_2"][0].rearrange("(k p) (s n) -> p k s n", p=P, n=D)
    h = M.split
    with ExitStack() as ctx:
        def sb(name, shape):
            return ctx.enter_context(nc.sbuf_tensor("d_" + name, shape, F32))

        qk = [sb(f"qk{b}", [P, 2 * GROUPS2, LX]) for b in range(2)]
        v = [sb(f"v{b}", [P, GROUPS2, 4, P]) for b in range(2)]
        vf = sb("vf", [P, 2, LX])
        swp = sb("swp", [ROT, 2, LX])
        masks = sb("masks", [P, 4 * LX + 2 * P])
        load(nc, S, [(masks[:, :], io["attn_masks"])])
        beside = Dilated(S, M, qk, v, swp, masks)

        def units_of(i):
            units = []
            for b in range(2):
                cols = bass.ds(i * (2 * P) + b * P, P)
                j0 = b * Dilated.JOBS
                for g in range(GROUPS2):
                    def keep(e, acc, s, _, g=g, b=b):
                        return e.activation(qk[b][:, 2 * g + s, :], acc, ACT.Copy, scale=1.0 if s else P ** -0.5)
                    units.append(Unit(tuple(w[:, :, 3 * g + s, cols] for s in range(2)), KD, 2 * P, feature_jobs(
                        h, KD, [(0, 0), (1, P)], [X_COLS], "act", keep)))
                made, turned = (6, 7, 9), (8, 10, 11)
                value, turn = [], []
                for g in range(GROUPS2):
                    j, = feature_jobs(h, KD, [(0, 0)], [X_COLS], "act", lambda e, acc, *_, g=g:
                                      e.activation(vf[:, g % 2, :], acc, ACT.Copy))
                    j.after = (j0 + turned[g - 2],) if g == 2 else (j0 + turned[2 - g] - Dilated.JOBS,)
                    value.append(j)

                    def transposes(pe, acc, g=g):
                        for t in range(4):
                            src = every4(vf[:, g % 2, :], t) if g else vf[:, 0, t * P:(t + 1) * P]
                            tr = pe.transpose(acc[:, t * P:(t + 1) * P], src, M.ident[:, :])
                        return tr

                    turn.append(Job(None, None, None, 0, P, LX, "dve", lambda e, acc, g=g, b=b: e.tensor_copy(
                        v[b][:, g, :, :].rearrange("p t n -> p (t n)"), acc), make=transposes, taken=j0 + made[g]))
                for g, js in enumerate(([value[0]], [value[1], turn[0]], [value[2], turn[1], turn[2]])):
                    c2 = i * (2 * P) + b * P
                    units.append(Unit(tuple(w[:, :, 3 * g + 2, bass.ds(c2 + s * (P // 2), P // 2)] for s in range(2)),
                                      KD, P, js))
            return units

        project(nc, S, M, units_of, turns=H2 // 2, ahead=ahead, beside=beside)
        with S.stage(nc) as block:
            @block.tensor
            def _(pe):
                for u in range(Dilated.UNITS):
                    beside.pe_step(pe, 1, 0, u, False)

            @block.scalar
            def _(act):
                for u in range(Dilated.UNITS):
                    beside.act_step(act, 0, u)

            @block.vector
            def _(dve):
                for u in range(Dilated.UNITS):
                    beside.dve_normalise(dve, 0, u)
                    beside.dve_step(dve, 0, u, H2 - 1)

            for name, n in beside.attention_signals(1).items():
                S.named[name].sent = n


LOOPS = {
    "recurrence": dict(weights=[2, 2], w_hi=4, w_lo=4, acc=18, by_act=8, by_dve=6, dve=5, act=6, pe=2, sq_act=2, summed=2, rstd=2,
                       scores=2, masked=2, probs=2, mixed=30),
}


def first_units(io, l):
    if l == 0:
        return [cut(io["hgrn_w_in_2"][0], 0, D, c) for c in (D, 0)]
    secs = io["attn_w_in_2"][0].rearrange("(k p) (s n) -> p k s n", p=P, n=D)
    return [Unit(tuple(secs[:, :, 3 * g + s, 0:P] for s in range(2)), KD, 2 * P, ()) for g in range(2)]


def second_layer(nc, S, M, io, l):
    x = lambda k, a, b: M.x[:, k, a:b]
    y_ = lambda k, a, b: M.y[:, k, a:b]
    gx = [X_COLS]
    following = first_units(io, 1) if l == 0 else None
    w_out = io["hgrn_w_out_2" if l == 0 else "attn_w_out_2"][0]
    w_up, w_down = io["ffn_w_in_2"][l], io["ffn_w_out_2"][l]
    n1 = 6
    n_up = D_FF2 // UNIT

    def squared(js):
        for j in js:
            j.square = (M.y[:, j.where[0], :], M.ssum[:, 0:LX], j.where[0] == 0)
        return js

    def gate_cut(i, up, jobs=()):
        return cut(w_up, 0, D, i * UNIT + up * D_FF2, UNIT, jobs)

    with ExitStack() as ctx:
        M.split = Split(ctx, nc, f"u{l}", [P, KD, LX])
        norm(nc, S, M, x, KD, D, gx, None, lambda k, a: M.gain2[:, 4 * l, k:k + 1],
             lambda k, a: M.mod(2 + l, 0, k, 0), split=M.split)
        if l == 0:
            recurrence(nc, S, M, io)
            M.loaded, M.stale = 0, True
        else:
            dilated(nc, S, M, io, square_cuts(w_out)[:2])
    with ExitStack() as ctx:
        h = Split(ctx, nc, f"mix2{l}", [P, KD, LX])
        divide(nc, S, M, [M.y[:, b, :] for b in range(KD)], h, 0, LX)
        units = square_cuts(w_out, lambda c: squared(feature_jobs(
            h, KD, [(2 * c, 0), (2 * c + 1, P)], gx, "dve", lambda e, acc, b, g: e.tensor_copy(M.y[:, b, :], acc))))
        project(nc, S, M, lambda i: units, ahead=[gate_cut(0, 0), gate_cut(0, 1)])
    norm(nc, S, M, y_, KD, D, gx, None, lambda k, a: M.gain2[:, 4 * l + 1, k:k + 1], add=x, summed=M.ssum)

    with ExitStack() as ctx:
        h = Split(ctx, nc, f"uf{l}", [P, KD, LX])
        hid = Split(ctx, nc, f"fh{l}", [P, 2 * n1, LX])
        gate = ctx.enter_context(nc.sbuf_tensor(f"gate{l}", [P, 2, LX], F32))
        norm(nc, S, M, x, KD, D, gx, None, lambda k, a: M.gain2[:, 4 * l + 2, k:k + 1],
             lambda k, a: M.mod(2 + l, 3, k, 0), split=h)

        def silu(e, acc, b, _):
            return e.activation(gate[:, b, :], acc, ACT.Silu)

        def times(e, acc, b, _):
            return e.tensor_tensor(M.v[:, b, :], gate[:, b, :], acc, ALU.mult)

        for part, (u0, nu) in enumerate([(0, n1), (n1, n_up - n1)]):
            def pair(i, u0=u0):
                js = feature_jobs(h, KD, [(0, 0), (1, P)], gx, "act", silu)
                ju = feature_jobs(h, KD, [(0, 0), (1, P)], gx, "dve", times, kind="times", hidden=hid)
                for b in range(2):
                    ju[b].after = (b,)
                    js[b].after = (b - 2,)
                    ju[b].dst = lambda t, b=b: t[:, bass.ds(i * 2 + b, 1), :].rearrange("p a t -> p (a t)")
                return [gate_cut(i + u0, 0, js), gate_cut(i + u0, 1, ju)]

            kt = 2 * nu

            def down(c, jobs=()):
                return cut(w_down, 2 * u0 * P, (2 * u0 + kt) * P, c * P, P, jobs)

            project(nc, S, M, pair, turns=nu, ahead=[down(0), down(1)])

            def keep(e, acc, b, g, part=part):
                if part == 0:
                    return e.tensor_copy(M.y[:, b, :], acc)
                return e.tensor_tensor(M.y[:, b, :], M.y[:, b, :], acc, ALU.add)

            units = [down(c, feature_jobs(hid, kt, [(c, 0)], gx, "dve", keep)) for c in range(KD)]
            if part:
                for unit in units:
                    squared(unit.jobs)
            project(nc, S, M, lambda i: units, ahead=[gate_cut(n1, 0), gate_cut(n1, 1)] if part == 0 else following)
    norm(nc, S, M, y_, KD, D, gx, None, lambda k, a: M.gain2[:, 4 * l + 3, k:k + 1], add=x, summed=M.ssum)



VECTORS = [
    ("c", 8), ("c_ctx", 8), ("c_2", 8), ("b_mod", 96), ("ada_b_2", 96), ("norm1_g", 16), ("norm2_g", 16),
    ("q_norm_g", 6), ("kv_norm_g", 4), ("hy_conv_w", 36), ("hy_conv_b", 12), ("hy_d", 4), ("final_norm_g", 8),
    ("norm_g_2", 64), ("hgrn_lower_bounds_2", 8), ("hgrn_norm_g_2", 8), ("hy_b1", 2), ("hy_freq", 2), ("hy_b2", 2),
]
FIRST_ROW = dict(zip((n for n, _ in VECTORS), np.cumsum([0] + [k for _, k in VECTORS])[:-1].tolist()))
N_ROWS = sum(k for _, k in VECTORS)
ROWS_OF = dict(VECTORS)


class Memory:
    def __init__(self, nc, ctx):
        def sb(name, shape, dt=F32):
            return ctx.enter_context(nc.sbuf_tensor(name, shape, dt))

        self.ps = ctx.enter_context(nc.psum_tensor("ps", [P, BANKS, 512], F32))
        self.ring = sb("ring", [P, RING, SLOT])
        self.x = sb("x_res", [P, KD, T])
        self.f = sb("f", [P, 2, T])
        self.v = self.f[:, :, 0:512]
        self.loaded, self.stale = 0, False
        self.cond = sb("cond", [P, KD, 3])
        self.count = 0
        self.sq = sb("sq", [P, 2, T])
        self.tmp = self.sq
        self.rs = sb("rs", [P, T])
        self.ssum = self.rs
        self.vec = sb("vec", [P, 4, P])
        self.mods = sb("mods", [P, 2 * DEPTH, 48, 2])
        self.gain = sb("gain", [P, 4, 2, KD])
        self.gain2 = sb("gain2", [P, 8, KD])
        self.lower = sb("lower", [P, 2, KD])
        self.hgain = sb("hgain", [P, KD])
        self.ident = sb("ident", [P, P])
        self.ones = sb("ones", [P, P])
        self.eps = sb("eps", [P, 1])
        self.flag = sb("flag", [P, 1])
        self.nmax, self.esum, self.rsum = sb("nmax", [P, 4]), sb("esum", [P, 4]), sb("rsum", [P, 4])

    @property
    def all_vec(self):
        return self.vec[:, :, :].rearrange("p a b -> p (a b)")

    def fresh(self):
        self.count += 1
        return self.count

    def col(self, name, l=0, k=0, n=1):
        c = FIRST_ROW[name] + l * (ROWS_OF[name] // 2) + k if ROWS_OF[name] and l else FIRST_ROW[name] + k
        return self.vec[:, :, :].rearrange("p a b -> p (a b)")[:, c:c + n]

    def mod(self, s, m, k, side):
        return self.mods[:, s, m * KD + k, side:side + 1]


def vectors(nc, S, M, io):
    with nc.sbuf_tensor("rows", [P, 4, P], F32) as rows:
        with S.stage(nc) as block:
            @block.gpsimd
            def _(pool):
                pool.memset(rows[:, :, :], 0.0)
                pool.memset(M.ones[:, :], 1.0)
                pool.memset(M.eps[:, :], EPS).then_inc(*S.side_sum.one)
                pool.memset(M.nmax[:, :], 0.0).then_inc(*S.side_done.one)
        pairs = [(M.ident[:, :], io["ident"])]
        for name, n in VECTORS:
            src = io[name]
            if len(src.shape) > 1:
                src = src.rearrange({2: "a b -> (a b)", 3: "a b c -> (a b c)"}[len(src.shape)])
            wd = 64 if name in ("hy_b1", "hy_freq", "hy_b2") else P
            src = src.rearrange("(r w) -> r w", w=wd)
            r = 0
            while r < n:
                row = FIRST_ROW[name] + r
                m = min(n - r, P - row % P)
                pairs.append((rows[row % P:row % P + m, row // P, 0:wd], src[r:r + m, :]))
                r += m
        load(nc, S, pairs)
        with S.stage(nc) as block:
            @block.tensor
            def _(pe):
                for t in range(4):
                    tr = pe.transpose(M.ps[:, 0, t * P:(t + 1) * P], rows[:, t, :], M.ident[:, :])
                tr.then_inc(*S.pe.one)

            @block.scalar
            def _(act):
                act.wait_ge(S.pe.sem, S.pe.at(1))
                act.activation(M.vec[:, :, :].rearrange("p a b -> p (a b)"), M.ps[:, 0, :], ACT.Copy)\
                    .then_inc(*S.act.one)


def modulations(nc, S, M, io):
    slots, turns = 6, 4
    sets = [("w_mod", 0, 0, 2)]
    with ExitStack() as ctx:
        cond = M.cond
        wm = ctx.enter_context(nc.sbuf_tensor("wm", [P, slots, KD, UNIT], F32))
        rows = ctx.enter_context(nc.sbuf_tensor("mod_rows", [2, len(sets), 6 * D], F32))
        turned = ctx.enter_context(nc.sbuf_tensor("mod_tiles", [96, len(sets), P], F32))
        landed = [Signal(nc, f"modulation_weights_{u}", 16) for u in range(slots)]
        with S.stage(nc) as block:
            @block.scalar
            def _(act):
                act.activation(cond[:, :, :].rearrange("p k s -> p s k"),
                               M.col("c", n=24).rearrange("p (s k) -> p s k", s=3), ACT.Silu)
        with S.stage(nc) as block:
            @block.sync
            def _(sp):
                for s, (name, l, _, _) in enumerate(sets):
                    def turn(i, first):
                        for u in range(slots):
                            if not first:
                                sp.wait_ge(S.acc.sem, S.acc.at((i + (s * turns - 1)) * slots + u + 1))
                            sp.dma_start(wm[:, u, :, :], cut(io[name][l], 0, D, i * (slots * UNIT) + u * UNIT).src)\
                                .then_inc(*landed[u].up)
                    if s == 0:
                        turn(0, True)
                        with sp.Fori(1, turns) as i:
                            turn(i, False)
                    else:
                        with sp.Fori(0, turns) as i:
                            turn(i, False)

            @block.tensor
            def _(pe):
                for s, (_, _, c0, n) in enumerate(sets):
                    def turn(i, first):
                        for u in range(slots):
                            pe.wait_ge(landed[u].sem, landed[u].at(i + (s * turns + 1)))
                            if not first:
                                pe.wait_ge(S.by_act.sem, S.by_act.at((i + (s * turns - 1)) * slots + u + 1))
                            for k in range(KD):
                                mm = pe.matmul(M.ps[0:n, u, 0:UNIT], cond[:, k, c0:c0 + n], wm[:, u, k, :],
                                               start=k == 0, stop=k == KD - 1)
                            mm.then_inc(*S.acc.up)
                    if s == 0:
                        turn(0, True)
                        with pe.Fori(1, turns) as i:
                            turn(i, False)
                    else:
                        with pe.Fori(0, turns) as i:
                            turn(i, False)

            @block.scalar
            def _(act):
                for s, (_, _, _, n) in enumerate(sets):
                    with act.Fori(0, turns) as i:
                        for u in range(slots):
                            act.wait_ge(S.acc.sem, S.acc.at((i + s * turns) * slots + u + 1))
                            act.activation(rows[0:n, s, bass.ds((i * slots + u) * UNIT, UNIT)], M.ps[0:n, u, 0:UNIT],
                                           ACT.Copy).then_inc(*S.by_act.up)

            S.acc.sent = S.by_act.sent = len(sets) * turns * slots
        with S.stage(nc) as block:
            @block.sync
            def _(sp):
                for s, (_, _, _, n) in enumerate(sets):
                    for c in range(n):
                        sp.dma_start(turned[48 * c:48 * c + 48, s, :], rows[c:c + 1, s, :].rearrange(
                            "a (b p) -> a b p", p=P)).then_inc(*S.landed.one)

            @block.tensor
            def _(pe):
                at = 0
                for s, (_, _, _, n) in enumerate(sets):
                    at += n
                    if s == len(sets) - 1:
                        pe.wait_ge(S.landed.sem, S.landed.at(at))
                for s, (_, _, _, n) in enumerate(sets):
                    pe.transpose(M.ps[:, s, 0:48 * n], turned[0:48 * n, s, :], M.ident[0:48 * n, 0:48 * n])\
                        .then_inc(*S.pe.one)

            @block.vector
            def _(dve):
                for s, (_, l, _, n) in enumerate(sets):
                    dve.wait_ge(S.pe.sem, S.pe.at(s + 1))
                    bias = M.col("b_mod" if s < DEPTH else "ada_b_2", l, n=48)
                    dve.tensor_tensor(M.mods[:, s, :, 0:n], M.ps[:, s, 0:48 * n].rearrange("p (n b) -> p b n", n=n),
                                      bias.unsqueeze(2).to_broadcast([P, 48, n]), ALU.add).then_inc(*S.by_dve.one)


def gains(nc, S, M, s, bounds=False):
    with S.stage(nc) as block:
        @block.vector
        def _(dve):
            def gain(dst, m, side, g):
                dve.scalar_tensor_tensor(dst, M.mods[:, s, m * KD:(m + 1) * KD, side], 1.0, g, ALU.add, ALU.mult)

            l = s % DEPTH
            if s < DEPTH:
                for j, name in enumerate(("norm1_g", "norm2_g")):
                    for side in range(2):
                        gain(M.gain[:, 2 * l + j, side, :], 1 + 3 * j, side, M.col(name, l, n=KD))
            else:
                for j, m in enumerate((1, 2, 4, 5)):
                    gain(M.gain2[:, 4 * l + j, :], m, 0, M.col("norm_g_2", l, j * KD, n=KD))


def lower_bounds(nc, S, M):
    with nc.sbuf_tensor("lb", [P, 4, KD], F32) as lb, S.stage(nc) as block:
        @block.vector
        def _(dve):
            dve.tensor_copy(M.hgain[:, :], M.col("hgrn_norm_g_2", n=KD))
            b = M.col("hgrn_lower_bounds_2", n=KD)
            chain(dve, S.dve, dve.tensor_tensor(lb[:, 0, :], b, b, ALU.subtract))
            dve.wait_ge(S.act.sem, S.act.at(1))
            chain(dve, S.dve, dve.reciprocal(lb[:, 2, :], lb[:, 1, :]))
            chain(dve, S.dve, dve.tensor_tensor(lb[:, 3, :], lb[:, 1, :], lb[:, 2, :], ALU.mult))
            chain(dve, S.dve, dve.tensor_tensor(M.lower[:, 0, :], lb[:, 3, :], lb[:, 3, :], ALU.subtract))
            dve.tensor_scalar(M.lower[:, 1, :], M.lower[:, 0, :], -1.0, 1.0, ALU.mult, ALU.add)

        @block.scalar
        def _(act):
            act.wait_ge(S.dve.sem, S.dve.at(1))
            act.activation(lb[:, 1, :], lb[:, 0, :], ACT.Exp).then_inc(*S.act.one)


def rotary_tables(nc, S, M, io):
    with ExitStack() as ctx:
        pos = ctx.enter_context(nc.sbuf_tensor("pos", [ROT, LX], I32))
        ang = ctx.enter_context(nc.sbuf_tensor("ang", [ROT, 4, LX], F32))
        par = ctx.enter_context(nc.sbuf_tensor("par", [ROT, 2], F32))
        load(nc, S, [(pos[:, :], io["positions_2"].to_broadcast([ROT, LX])), (par[:, :], io["rot_params"])])
        with S.stage(nc) as block:
            @block.vector
            def _(dve):
                chain(dve, S.dve, dve.tensor_copy(ang[:, 0, :], pos[:, :]))
                chain(dve, S.dve, dve.tensor_scalar(ang[:, 0, :], ang[:, 0, :], par[:, 0:1], None, ALU.mult))
                reduce_angle(dve, S, ang[:, 0, :], ang[:, 1, :])
                chain(dve, S.dve, dve.tensor_scalar(ang[:, 2, :], ang[:, 0, :], math.pi / 2, None, ALU.add))
                chain(dve, S.dve, dve.tensor_scalar(ang[:, 1, :], ang[:, 2, :], math.pi, TWO_PI, ALU.is_gt, ALU.mult))
                chain(dve, S.dve, dve.tensor_tensor(ang[:, 2, :], ang[:, 2, :], ang[:, 1, :], ALU.subtract))
                dve.tensor_scalar(ang[:, 2, :], ang[:, 2, :], SIN_MAX, -SIN_MAX, ALU.min, ALU.max)\
                    .then_inc(*S.by_dve.one)
                dve.wait_ge(S.act.sem, S.act.at(1))
                dve.tensor_scalar(M.rot[:, 1, :], ang[:, 3, :], par[:, 1:2], None, ALU.mult)

            @block.scalar
            def _(act):
                act.wait_ge(S.by_dve.sem, S.by_dve.at(1))
                act.activation(M.rot[:, 0, :], ang[:, 2, :], ACT.Sin)
                act.activation(ang[:, 3, :], ang[:, 0, :], ACT.Sin).then_inc(*S.act.one)


def enter(nc, S, M, io):
    with nc.sbuf_tensor("tok_in", [P, 6, D], F32) as tok:
        load(nc, S, [(tok[:, 0:4, :], io["x"][0].rearrange("(t p) d -> p t d", p=P)),
                     (tok[:, 4:6, :], io["ctx"][0].rearrange("(t p) d -> p t d", p=P))])
        with S.stage(nc) as block:
            @block.tensor
            def _(pe):
                for t in range(T // P):
                    for half in range(2):
                        n = 2 * t + half
                        if n >= BANKS:
                            pe.wait_ge(S.by_act.sem, S.by_act.at(n - BANKS + 1))
                        for k in range(4):
                            c = (4 * half + k) * P
                            tr = pe.transpose(M.ps[:, n % BANKS, k * P:(k + 1) * P], tok[:, t, c:c + P], M.ident[:, :])
                        tr.then_inc(*S.pe.one)

            @block.scalar
            def _(act):
                for n in range(2 * T // P):
                    t, half = divmod(n, 2)
                    act.wait_ge(S.pe.sem, S.pe.at(n + 1))
                    act.activation(M.x[:, 4 * half:4 * half + 4, t * P:(t + 1) * P],
                                   M.ps[:, n % BANKS, :].rearrange("p (k t) -> p k t", k=4), ACT.Copy)\
                        .then_inc(*S.by_act.one)


def leave(nc, S, M, io):
    dst = io["out"][0].rearrange("(t p) d -> t p d", p=P)
    with nc.sbuf_tensor("tok_out", [P, 4, D], F32) as tok, S.stage(nc) as block:
        @block.tensor
        def _(pe):
            for n in range(8):
                t, half = divmod(n, 2)
                for k in range(4):
                    tr = pe.transpose(M.ps[:, n, k * P:(k + 1) * P], M.x[:, 4 * half + k, t * P:(t + 1) * P],
                                      M.ident[:, :])
                tr.then_inc(*S.pe.one)

        @block.scalar
        def _(act):
            for n in range(8):
                t, half = divmod(n, 2)
                act.wait_ge(S.pe.sem, S.pe.at(n + 1))
                act.activation(tok[:, t, half * 512:(half + 1) * 512], M.ps[:, n, :], ACT.Copy)\
                    .then_inc(*S.by_act.one)

        @block.sync
        def _(sp):
            for t in range(4):
                sp.wait_ge(S.by_act.sem, S.by_act.at(2 * t + 2))
                sp.dma_start(dst[t], tok[:, t, :]).then_inc(*S.out.one)
            sp.wait_ge(S.out.sem, S.out.at(4))


def program(nc, io):
    S = Signals(nc)
    with ExitStack() as ctx:
        M = Memory(nc, ctx)
        vectors(nc, S, M, io)
        modulations(nc, S, M, io)
        gains(nc, S, M, 0)
        lower_bounds(nc, S, M)
        enter(nc, S, M, io)
        first_layer(nc, S, M, io, 0)
        gains(nc, S, M, 1)
        first_layer(nc, S, M, io, 1)
        gains(nc, S, M, 2)
        gains(nc, S, M, 3)
        x = lambda k, a, b: M.x[:, k, a:b]
        norm(nc, S, M, x, KD, D, [X_COLS], x, lambda k, a: M.col("final_norm_g", k=k), summed=M.ssum)
        M.y = ctx.enter_context(nc.sbuf_tensor("y", [P, KD, LX], F32))
        M.rot = ctx.enter_context(nc.sbuf_tensor("rot", [ROT, 2, LX], F32))
        M.resets = ctx.enter_context(nc.sbuf_tensor("resets", [P, LX], F32))
        M.causal = ctx.enter_context(nc.sbuf_tensor("causal", [P, P], F32))
        load(nc, S, [(M.resets[:, :], io["chunk_resets"]), (M.causal[:, :], io["chunk_causal"])])
        rotary_tables(nc, S, M, io)
        for l in range(DEPTH):
            second_layer(nc, S, M, io, l)
        leave(nc, S, M, io)


def tables():
    f = np.float64
    out = {"ident": np.eye(P)}

    def by_tile(a):
        return a.reshape(a.shape[0] // P, P, *a.shape[1:]).swapaxes(0, 1)

    inv = 10000.0 ** (-np.arange(0, 16, 2, dtype=np.float32) / np.float32(16))
    t = np.arange(LX)
    rope = np.zeros((P, 2, LX))
    swap = np.zeros((P, P))
    for axis, pos in enumerate((t // 64, t % 64)):
        ang = (pos.astype(np.float32)[None] * inv.astype(np.float32)[:, None]).astype(np.float32).astype(f)
        for half in range(2):
            r = NOPE + 16 * axis + 8 * half
            rope[r:r + 8, 0] = np.cos(ang)
            rope[r:r + 8, 1] = np.sin(ang) * (1 if half else -1)
            other = NOPE + 16 * axis + 8 * (1 - half)
            for j in range(8):
                swap[other + j, r + j] = 1.0
    out["rope_tables"], out["rope_swap"] = rope, swap

    w = np.arange(64)
    a = 2 * np.pi * np.outer(w, w) / 64
    chan = np.zeros((P, 2, P))
    for g in range(2):
        s = slice(64 * g, 64 * g + 64)
        chan[s, 0, s], chan[s, 1, s] = np.cos(a), np.sin(a)
    out["fnet_channels"] = chan.reshape(P, 2 * P)
    deltas = np.abs(np.linspace(math.log(1e-2) / 1.5, math.log(1e-2) / 0.3, HY))
    for n in (LX, LC):
        i = np.arange(n)
        a = 2 * np.pi * (np.outer(i, i) % n) / n
        out[f"fnet_tokens_{n}"] = by_tile(np.stack([np.cos(a), -np.sin(a)], 1)) / math.sqrt(64 * n)
        a = 2 * np.pi * np.outer(i, i + 0.5) / (2 * n)
        out[f"hy_tk_{n}"] = by_tile(np.stack([np.cos(a), np.sin(a)], 1))
        a = 2 * np.pi * np.outer(i + 0.5, i + 0.5) / (2 * n)
        out[f"hy_ta_{n}"] = by_tile(np.stack([np.cos(a), np.sin(a)], 1))
        tt = np.linspace(0.0, 1.0, n)[:, None]
        bands = (EMB - 1) // 2
        fr = np.linspace(1e-4, bands - 1, bands).astype(np.float32)
        ang = (np.float32(2.0 * math.pi) * np.arange(n, dtype=np.float32)[:, None] / np.float32(n)) * fr
        ang = ang.astype(np.float32).astype(f)
        out[f"hy_emb_{n}"] = np.concatenate([tt, np.cos(ang), -np.sin(ang)], -1).T
        dec = np.exp(-tt * deltas)
        both = np.concatenate([dec, dec], 1)
        both[0, HY:] = 0.0
        out[f"hy_decay_{n}"] = by_tile(both)

    out["chunk_resets"] = np.broadcast_to((t % CHUNK != 0).astype(f), (P, LX))
    s, c = np.arange(P)[:, None], np.arange(P)[None]
    out["chunk_causal"] = ((s // CHUNK == c // CHUNK) & (s <= c)).astype(f)
    inv2 = 500000.0 ** (-np.arange(0, ROT, 2, dtype=np.float32) / np.float32(ROT))
    sign = np.repeat([-1.0, 1.0], ROT // 2)
    out["rot_params"] = np.stack([np.tile(inv2, 2), sign], 1)
    masks = np.zeros((P, 4 * LX + 2 * P))
    m = np.arange(P)
    for r in range(4):
        dist = (r + 4 * m)[:, None] - t[None]
        masks[:, r * LX:(r + 1) * LX] = np.where((dist >= 0) & (dist <= 128), 0.0, -1e30)
    causal = m[:, None] >= m[None]
    masks[:, 4 * LX:4 * LX + P] = np.where(causal, 0.0, -1e30)
    masks[:, 4 * LX + P:] = np.where(causal & (m[:, None] % 4 == m[None] % 4), 0.0, -1e30)
    out["attn_masks"] = masks
    return {k: np.ascontiguousarray(v.astype(np.float32)) for k, v in out.items()}


def kernel(**inputs):
    import concourse.bacc as bacc
    from concourse.bass_utils import run_bass_kernel_spmd

    nc = bacc.Bacc("TRN2", target_bir_lowering=False, num_devices=1)
    arrays, io = {}, {}
    for name, a in {**inputs, **tables()}.items():
        a = np.ascontiguousarray(a)
        arrays[f"in_{name}"] = a
        io[name] = nc.dram_tensor(f"in_{name}", a.shape, mybir.dt.from_np(a.dtype), kind="ExternalInput").ap()
    io["out"] = nc.dram_tensor("out", (1, LX, D), F32, kind="ExternalOutput").ap()
    program(nc, io)
    r = run_bass_kernel_spmd(nc, [arrays], core_ids=[0])
    return r.results[0]["out"]
```
